# Optimizing a Trainium2 kernel written in Bass

```python
import math
import jax, jax.numpy as jnp
from jax import lax
import numpy as np
import jax
import jax.numpy as jnp

D_MODEL = 1024
BATCH = 1
SEQ = 512
DEPTH = 4

N_MIXERS = 3
EPS = 1e-6
N_GLA = (DEPTH + 2) // 3
N_SGU = (DEPTH + 1) // 3
N_FOX = DEPTH // 3

GLA_HEADS = 4
GLA_DK = D_MODEL // (2 * GLA_HEADS)
GLA_DV = D_MODEL // GLA_HEADS
GLA_KD = GLA_HEADS * GLA_DK
GLA_VD = GLA_HEADS * GLA_DV
GLA_RANK = 16
GLA_NORMALIZER = 16.0
GLA_CHUNK = 64
GLA_IN = 2 * GLA_KD + 2 * GLA_VD + GLA_RANK

SGU_WIDTH = D_MODEL
SGU_GROUPS = 4
SGU_GDIM = SGU_WIDTH // SGU_GROUPS
SGU_CHUNK = 128
SGU_IN = 3 * SGU_WIDTH

FOX_HEADS = 16
FOX_DH = 64
FOX_AD = FOX_HEADS * FOX_DH
FOX_BLOCK = 128
FOX_IN = 4 * FOX_AD + FOX_HEADS
FORGET_BIAS_INIT = 2.0


def rms_norm(x, g):
    xf = x.astype(jnp.float32)
    xf = xf * lax.rsqrt(jnp.mean(xf * xf, axis=-1, keepdims=True) + EPS)
    return xf.astype(x.dtype) * g

def layer_norm(x, g, b):
    xf = x.astype(jnp.float32)
    mu = jnp.mean(xf, axis=-1, keepdims=True)
    var = jnp.mean(jnp.square(xf - mu), axis=-1, keepdims=True)
    return ((xf - mu) * lax.rsqrt(var + EPS)).astype(x.dtype) * g + b

def gla_mixer(h, w_in, w_a2, b_a, g_head, w_out):
    B, S, _ = h.shape
    H, DK, DV, C = GLA_HEADS, GLA_DK, GLA_DV, GLA_CHUNK
    N = S // C
    q, k, v, z, a_low = jnp.split(h @ w_in, [GLA_KD, 2 * GLA_KD, 2 * GLA_KD + GLA_VD,
                                             2 * GLA_KD + 2 * GLA_VD], axis=-1)
    log_a = jax.nn.log_sigmoid((a_low @ w_a2 + b_a).astype(jnp.float32)) / GLA_NORMALIZER
    q = q.astype(jnp.float32) * (DK ** -0.5)

    def to_chunks(t, d):
        return t.astype(jnp.float32).reshape(B, N, C, H, d).transpose(1, 0, 3, 2, 4)

    qc, kc, vc, gc = to_chunks(q, DK), to_chunks(k, DK), to_chunks(v, DV), to_chunks(log_a, DK)
    causal = jnp.tril(jnp.ones((C, C), dtype=bool))

    def step(state, xs):
        qb, kb, vb, gb = xs
        b = jnp.cumsum(gb, axis=2)
        o_inter = jnp.einsum('bhik,bhkv->bhiv', qb * jnp.exp(b), state)
        diff = b[:, :, :, None, :] - b[:, :, None, :, :]
        decay = jnp.exp(jnp.where(causal[:, :, None], diff, -jnp.inf))
        attn = jnp.einsum('bhik,bhjk,bhijk->bhij', qb, kb, decay)
        o = o_inter + jnp.einsum('bhij,bhjv->bhiv', attn, vb)
        b_last = b[:, :, -1:, :]
        state = (jnp.exp(b_last[:, :, 0, :])[..., None] * state
                 + jnp.einsum('bhjk,bhjv->bhkv', kb * jnp.exp(b_last - b), vb))
        return state, o

    state0 = jnp.zeros((B, H, DK, DV), jnp.float32)
    _, o = lax.scan(step, state0, (qc, kc, vc, gc))
    o = o.transpose(1, 0, 3, 2, 4).reshape(B, S, H, DV)
    o = rms_norm(o, g_head).reshape(B, S, GLA_VD).astype(h.dtype)
    return (o * jax.nn.silu(z)) @ w_out

def sgu_mixer(h, w_in, ln_g, ln_b, w_s, b_s, w_out):
    B, S, _ = h.shape
    C, G, Dg = SGU_CHUNK, SGU_GROUPS, SGU_GDIM
    N = S // C
    u, v, z = jnp.split(h @ w_in, 3, axis=-1)
    u = jax.nn.gelu(u)
    v = layer_norm(jax.nn.gelu(v), ln_g, ln_b)
    w_causal = jnp.where(jnp.tril(jnp.ones((C, C), dtype=bool))[None], w_s, 0.0)
    vc = v.reshape(B, N, C, G, Dg)
    mixed = jnp.einsum('gts,bnsgd->bntgd', w_causal, vc) + b_s.T[None, None, :, :, None]
    sg = u * mixed.reshape(B, S, SGU_WIDTH)
    return (sg * jax.nn.silu(z)) @ w_out

def fox_mixer(h, w_in, b_f, g_q, g_k, w_out):
    B, S, _ = h.shape
    H, Dh, BLK = FOX_HEADS, FOX_DH, FOX_BLOCK
    q, k, v, z, f_logit = jnp.split(h @ w_in, [FOX_AD, 2 * FOX_AD, 3 * FOX_AD, 4 * FOX_AD], axis=-1)
    q = rms_norm(q.reshape(B, S, H, Dh), g_q).transpose(0, 2, 1, 3)
    k = rms_norm(k.reshape(B, S, H, Dh), g_k).transpose(0, 2, 1, 3)
    v = v.reshape(B, S, H, Dh).transpose(0, 2, 1, 3)
    log_f = jax.nn.log_sigmoid((f_logit + b_f).astype(jnp.float32))
    F = jnp.cumsum(log_f, axis=1).transpose(0, 2, 1)
    scale = Dh ** -0.5
    outs = []
    for i in range(S // BLK):
        lo, hi = i * BLK, (i + 1) * BLK
        s = jnp.einsum('bhqd,bhkd->bhqk', q[:, :, lo:hi], k[:, :, :hi]).astype(jnp.float32) * scale
        s = s + F[:, :, lo:hi, None] - F[:, :, None, :hi]
        causal = (lo + jnp.arange(BLK))[:, None] >= jnp.arange(hi)[None, :]
        p = jax.nn.softmax(jnp.where(causal, s, -jnp.inf), axis=-1).astype(v.dtype)
        outs.append(jnp.einsum('bhqk,bhkd->bhqd', p, v[:, :, :hi]))
    o = jnp.concatenate(outs, axis=2).transpose(0, 2, 1, 3).reshape(B, S, FOX_AD)
    return (o * jax.nn.silu(z)) @ w_out

def first_inputs(seed: int = 0) -> dict:
    key = jax.random.key(seed)
    ks = jax.random.split(key, 32)
    D = D_MODEL
    nrm = lambda k, shape, s: jax.random.normal(k, shape, jnp.float32) * s
    return {
        "x": nrm(ks[0], (BATCH, SEQ, D), 1.0),
        "c": nrm(ks[1], (BATCH, D), 1.0),
        "norm_pre_g": 1.0 + nrm(ks[2], (DEPTH, D), 0.1),
        "norm_post_g": 1.0 + nrm(ks[3], (DEPTH, D), 0.1),
        "w_mod": nrm(ks[4], (DEPTH, D, 3 * D), D ** -0.5),
        "b_mod": nrm(ks[5], (DEPTH, 3 * D), 0.01),
        "gla_w_in": nrm(ks[6], (N_GLA, D, GLA_IN), D ** -0.5),
        "gla_w_a2": nrm(ks[7], (N_GLA, GLA_RANK, GLA_KD), GLA_RANK ** -0.5),
        "gla_b_a": nrm(ks[8], (N_GLA, GLA_KD), 0.1),
        "gla_g_head": 1.0 + nrm(ks[9], (N_GLA, GLA_HEADS, GLA_DV), 0.1),
        "gla_w_out": nrm(ks[10], (N_GLA, GLA_VD, D), GLA_VD ** -0.5),
        "sgu_w_in": nrm(ks[11], (N_SGU, D, SGU_IN), D ** -0.5),
        "sgu_ln_g": 1.0 + nrm(ks[12], (N_SGU, SGU_WIDTH), 0.1),
        "sgu_ln_b": nrm(ks[13], (N_SGU, SGU_WIDTH), 0.1),
        "sgu_w_s": nrm(ks[14], (N_SGU, SGU_GROUPS, SGU_CHUNK, SGU_CHUNK), SGU_CHUNK ** -0.5),
        "sgu_b_s": 1.0 + nrm(ks[15], (N_SGU, SGU_GROUPS, SGU_CHUNK), 0.1),
        "sgu_w_out": nrm(ks[16], (N_SGU, SGU_WIDTH, D), SGU_WIDTH ** -0.5),
        "fox_w_in": nrm(ks[17], (N_FOX, D, FOX_IN), D ** -0.5),
        "fox_b_f": FORGET_BIAS_INIT + nrm(ks[18], (N_FOX, FOX_HEADS), 0.1),
        "fox_g_q": 1.0 + nrm(ks[19], (N_FOX, FOX_DH), 0.1),
        "fox_g_k": 1.0 + nrm(ks[20], (N_FOX, FOX_DH), 0.1),
        "fox_w_out": nrm(ks[21], (N_FOX, FOX_AD, D), FOX_AD ** -0.5),
    }

def first_block(x, c, norm_pre_g, norm_post_g, w_mod, b_mod,
              gla_w_in, gla_w_a2, gla_b_a, gla_g_head, gla_w_out,
              sgu_w_in, sgu_ln_g, sgu_ln_b, sgu_w_s, sgu_b_s, sgu_w_out,
              fox_w_in, fox_b_f, fox_g_q, fox_g_k, fox_w_out):
    cond = jax.nn.silu(c)
    for i in range(DEPTH):
        mod = (cond @ w_mod[i] + b_mod[i])[:, None, :]
        shift, scale, gate = jnp.split(mod, 3, axis=-1)
        h = rms_norm(x, norm_pre_g[i]) * (1.0 + scale) + shift
        kind, j = i % N_MIXERS, i // N_MIXERS
        if kind == 0:
            o = gla_mixer(h, gla_w_in[j], gla_w_a2[j], gla_b_a[j], gla_g_head[j], gla_w_out[j])
        elif kind == 1:
            o = sgu_mixer(h, sgu_w_in[j], sgu_ln_g[j], sgu_ln_b[j], sgu_w_s[j], sgu_b_s[j], sgu_w_out[j])
        else:
            o = fox_mixer(h, fox_w_in[j], fox_b_f[j], fox_g_q[j], fox_g_k[j], fox_w_out[j])
        x = x + gate * rms_norm(o, norm_post_g[i])
    return x


DEPTH_2 = 2

GRID_W = 64
CTX_LEN = 256
NORM_EPS = 1e-6
ROPE_THETA = 10000.0
Q_BLOCK = 128

GDN_HEADS = 8
GDN_DK = 64
GDN_DV = 64
GDN_CONV = 5
GDN_CHUNK = 64
GDN_QK_W = GDN_HEADS * GDN_DK
GDN_V_W = GDN_HEADS * GDN_DV

MLA_HEADS = 8
MLA_NOPE = 64
MLA_ROPE = 32
MLA_V = 64
MLA_Q_LORA = 256
MLA_KV_LORA = 128

NA_HEADS = 8
NA_DIM = 64
NA_WIN_H = 8
NA_WIN_W = 16
NA_W = NA_HEADS * NA_DIM

GQA_HEADS = 8
GQA_KV_HEADS = 2
GQA_DIM = 64

D_FF = -(-(8 * D_MODEL) // (3 * 256)) * 256

EVEN_SPLITS = (2 * GDN_QK_W + GDN_V_W, GDN_V_W, 2 * GDN_HEADS, 2 * GDN_HEADS, MLA_Q_LORA, MLA_KV_LORA, MLA_ROPE)
ODD_SPLITS = (NA_W, NA_W, NA_W, GQA_HEADS * GQA_DIM, GQA_KV_HEADS * GQA_DIM, GQA_KV_HEADS * GQA_DIM)
IN_EVEN = sum(EVEN_SPLITS)
IN_ODD = sum(ODD_SPLITS)
MIX_EVEN = GDN_V_W + MLA_HEADS * MLA_V
MIX_ODD = NA_W + GQA_HEADS * GQA_DIM
N_EVEN = (DEPTH_2 + 1) // 2
N_ODD = DEPTH_2 // 2


def split_cols(z, sizes):
    offs = [int(o) for o in np.cumsum(sizes)[:-1]]
    return jnp.split(z, offs, axis=-1)

def to_heads(t, n):
    return t.reshape(t.shape[0], t.shape[1], n, -1)

def rms_norm_2(x, g):
    xf = x.astype(jnp.float32)
    y = xf * lax.rsqrt(jnp.mean(xf * xf, -1, keepdims=True) + NORM_EPS)
    return (y * g.astype(jnp.float32)).astype(x.dtype)

def l2_normalize(x):
    xf = x.astype(jnp.float32)
    return (xf * lax.rsqrt(jnp.sum(xf * xf, -1, keepdims=True) + NORM_EPS)).astype(x.dtype)

def modulate(h, shift, scale):
    return h * (1.0 + scale) + shift

def swiglu(u, w_gate, w_up, w_down):
    return (jax.nn.silu(u @ w_gate) * (u @ w_up)) @ w_down

def axial_rope(n_tokens, rot_dim):
    t = jnp.arange(n_tokens, dtype=jnp.int32)
    row = (t // GRID_W).astype(jnp.float32)
    col = (t % GRID_W).astype(jnp.float32)
    n_freq = rot_dim // 4
    inv_freq = ROPE_THETA ** (-jnp.arange(n_freq, dtype=jnp.float32) / n_freq)
    ang = jnp.concatenate([row[:, None] * inv_freq, col[:, None] * inv_freq], -1)
    return jnp.cos(ang), jnp.sin(ang)

def apply_rope(x, cos, sin):
    half = x.shape[-1] // 2
    x1, x2 = x[..., :half], x[..., half:]
    cs, sn = cos[None, :, None, :], sin[None, :, None, :]
    return jnp.concatenate([x1 * cs - x2 * sn, x2 * cs + x1 * sn], -1).astype(x.dtype)

def short_conv(x, w):
    n_tap = w.shape[0]
    pad = n_tap // 2
    t_len = x.shape[1]
    xp = jnp.pad(x, ((0, 0), (pad, pad), (0, 0)))
    out = xp[:, 0:t_len] * w[0]
    for j in range(1, n_tap):
        out = out + xp[:, j:j + t_len] * w[j]
    return out

def blocked_attention(q, k, v, scale):
    b, tq, h, d = q.shape
    hk = k.shape[2]
    grp = h // hk
    nb = tq // Q_BLOCK
    qb = q.reshape(b, nb, Q_BLOCK, hk, grp, d).transpose(1, 0, 2, 3, 4, 5)

    def one_block(q_i):
        s = jnp.einsum('bqkgd,bskd->bkgqs', q_i, k).astype(jnp.float32) * scale
        p = jax.nn.softmax(s, axis=-1).astype(v.dtype)
        return jnp.einsum('bkgqs,bskd->bqkgd', p, v)

    o = lax.map(one_block, qb)
    return o.transpose(1, 0, 2, 3, 4, 5).reshape(b, tq, h, v.shape[-1])

def delta_rule_chunked(q, k, v, g, beta, s0):
    f32 = jnp.float32
    b, t_len, h, dk = q.shape
    dv = v.shape[-1]
    n = t_len // GDN_CHUNK
    cl = GDN_CHUNK

    def chunks(t):
        return jnp.moveaxis(t.astype(f32).reshape(b, n, cl, h, *t.shape[3:]), 3, 1)

    qc, kc, vc, gch, bc = chunks(q), chunks(k), chunks(v), chunks(g), chunks(beta)
    gc = jnp.cumsum(gch, -1)
    tril = jnp.tril(jnp.ones((cl, cl), bool))
    strict = jnp.tril(jnp.ones((cl, cl), bool), -1)
    decay = jnp.exp(jnp.where(tril, gc[..., :, None] - gc[..., None, :], -jnp.inf))
    kb = kc * bc[..., None]
    vb = vc * bc[..., None]
    m = jnp.where(strict, jnp.einsum('bhncd,bhnsd->bhncs', kb, kc) * decay, 0.0)
    eye = jnp.eye(cl, dtype=f32)
    tmat = lax.linalg.triangular_solve(m + eye, jnp.broadcast_to(eye, m.shape), left_side=True,
                                       lower=True, unit_diagonal=True)
    u = jnp.einsum('bhncs,bhnsv->bhncv', tmat, vb)
    w = jnp.einsum('bhncs,bhnsk->bhnck', tmat, kb * jnp.exp(gc)[..., None])
    qk = jnp.einsum('bhncd,bhnsd->bhncs', qc, kc) * decay
    q_dec = qc * jnp.exp(gc)[..., None]
    k_dec = kc * jnp.exp(gc[..., -1:] - gc)[..., None]
    g_last = jnp.exp(gc[..., -1])
    xs = tuple(jnp.moveaxis(t, 2, 0) for t in (u, w, qk, q_dec, k_dec, g_last))

    def step(s, inp):
        u_i, w_i, qk_i, qd_i, kd_i, gl_i = inp
        v_new = u_i - jnp.einsum('bhck,bhkv->bhcv', w_i, s)
        o_i = jnp.einsum('bhck,bhkv->bhcv', qd_i, s) + jnp.einsum('bhcs,bhsv->bhcv', qk_i, v_new)
        s = s * gl_i[..., None, None] + jnp.einsum('bhck,bhcv->bhkv', kd_i, v_new)
        return s, o_i

    s_fin, o = lax.scan(step, s0.astype(f32), xs)
    return s_fin, o.transpose(1, 0, 3, 2, 4).reshape(b, t_len, h, dv)

def gdn_prepare(qkv, a, bt, conv_w, a_log, dt_bias):
    b, t_len, _ = qkv.shape
    qkv = jax.nn.silu(short_conv(qkv, conv_w))
    q, k, v = jnp.split(qkv, [GDN_QK_W, 2 * GDN_QK_W], axis=-1)
    q = l2_normalize(q.reshape(b, t_len, GDN_HEADS, GDN_DK)) * (GDN_DK ** -0.5)
    k = l2_normalize(k.reshape(b, t_len, GDN_HEADS, GDN_DK))
    v = v.reshape(b, t_len, GDN_HEADS, GDN_DV)
    a = a.reshape(b, t_len, 2, GDN_HEADS).astype(jnp.float32)
    bt = bt.reshape(b, t_len, 2, GDN_HEADS).astype(jnp.float32)
    g = -jnp.exp(a_log.astype(jnp.float32)) * jax.nn.softplus(a + dt_bias.astype(jnp.float32))
    return q, k, v, g, jax.nn.sigmoid(bt)

def gdn_bidirectional(lat, ctx):
    q_l, k_l, v_l, g_l, b_l = lat
    q_c, k_c, v_c, g_c, b_c = ctx
    s0 = jnp.zeros((q_l.shape[0], GDN_HEADS, GDN_DK, GDN_DV), jnp.float32)
    s_cf, oc_f = delta_rule_chunked(q_c, k_c, v_c, g_c[:, :, 0], b_c[:, :, 0], s0)
    _, ol_f = delta_rule_chunked(q_l, k_l, v_l, g_l[:, :, 0], b_l[:, :, 0], s_cf)
    fl = lambda t: jnp.flip(t, 1)
    s_cb, oc_b = delta_rule_chunked(fl(q_c), fl(k_c), fl(v_c), fl(g_c[:, :, 1]), fl(b_c[:, :, 1]), s0)
    _, ol_b = delta_rule_chunked(fl(q_l), fl(k_l), fl(v_l), fl(g_l[:, :, 1]), fl(b_l[:, :, 1]), s_cb)
    return ol_f + fl(ol_b), oc_f + fl(oc_b)

def gdn_output(o, gate, out_norm):
    b, t_len, h, dv = o.shape
    o = rms_norm_2(o.astype(gate.dtype), out_norm)
    return (o * jax.nn.silu(gate.reshape(b, t_len, h, dv))).reshape(b, t_len, h * dv)

def mla_q(q_down, q_norm, w_q_up, rope):
    b, t_len, _ = q_down.shape
    q = (rms_norm_2(q_down, q_norm) @ w_q_up).reshape(b, t_len, MLA_HEADS, MLA_NOPE + MLA_ROPE)
    if rope is None:
        return q
    return jnp.concatenate([q[..., :MLA_NOPE], apply_rope(q[..., MLA_NOPE:], *rope)], -1)

def mla_kv(kv_down, k_pe, kv_norm, w_kv_up, rope):
    b, t_len, _ = kv_down.shape
    kv = (rms_norm_2(kv_down, kv_norm) @ w_kv_up).reshape(b, t_len, MLA_HEADS, MLA_NOPE + MLA_V)
    k_pe = k_pe[:, :, None, :]
    if rope is not None:
        k_pe = apply_rope(k_pe, *rope)
    k = jnp.concatenate([kv[..., :MLA_NOPE], jnp.broadcast_to(k_pe, (b, t_len, MLA_HEADS, MLA_ROPE))], -1)
    return k, kv[..., MLA_NOPE:]

def neighbourhood_attention(q, k, v, k_ctx, v_ctx, rpb):
    b, s_len, h, d = q.shape
    rows = s_len // GRID_W
    kh = min(NA_WIN_H, rows)
    kw = NA_WIN_W
    nk = kh * kw
    r = jnp.arange(rows)
    col = jnp.arange(GRID_W)
    rs = jnp.clip(r - kh // 2, 0, rows - kh)
    cs = jnp.clip(col - kw // 2, 0, GRID_W - kw)
    kr = rs[:, None] + jnp.arange(kh)
    kc = cs[:, None] + jnp.arange(kw)
    idx = (kr[:, None, :, None] * GRID_W + kc[None, :, None, :]).reshape(rows, GRID_W * nk)
    dr = kr - r[:, None] + (NA_WIN_H - 1)
    dc = kc - col[:, None] + (NA_WIN_W - 1)
    bias = rpb[:, dr[:, None, :, None], dc[None, :, None, :]]
    bias = bias.reshape(h, rows, GRID_W, nk).transpose(1, 0, 2, 3).astype(jnp.float32)
    qr = q.reshape(b, rows, GRID_W, h, d).transpose(1, 0, 2, 3, 4)
    scale = d ** -0.5

    def row_block(inp):
        q_i, idx_i, b_i = inp
        kg = jnp.take(k, idx_i, axis=1).reshape(b, GRID_W, nk, h, d)
        vg = jnp.take(v, idx_i, axis=1).reshape(b, GRID_W, nk, h, d)
        s_loc = jnp.einsum('bqhd,bqnhd->bhqn', q_i, kg).astype(jnp.float32) * scale + b_i[None]
        s_ctx = jnp.einsum('bqhd,bshd->bhqs', q_i, k_ctx).astype(jnp.float32) * scale
        p = jax.nn.softmax(jnp.concatenate([s_loc, s_ctx], -1), axis=-1).astype(v.dtype)
        return (jnp.einsum('bhqn,bqnhd->bqhd', p[..., :nk], vg)
                + jnp.einsum('bhqs,bshd->bqhd', p[..., nk:], v_ctx))

    o = lax.map(row_block, (qr, idx, bias))
    return o.transpose(1, 0, 2, 3, 4).reshape(b, s_len, h, d)

def even_mixer(u_lat, u_ctx, need_ctx, w_in, w_out, conv_w, a_log, dt_bias, out_norm,
               q_norm, w_q_up, kv_norm, w_kv_up, rope):
    b, s_len, _ = u_lat.shape
    lat = split_cols(u_lat @ w_in, EVEN_SPLITS)
    ctx = split_cols(u_ctx @ w_in, EVEN_SPLITS)
    o_lat, o_ctx = gdn_bidirectional(gdn_prepare(lat[0], lat[2], lat[3], conv_w, a_log, dt_bias),
                                     gdn_prepare(ctx[0], ctx[2], ctx[3], conv_w, a_log, dt_bias))
    a_lat = gdn_output(o_lat, lat[1], out_norm)
    k_c, v_c = mla_kv(ctx[5], ctx[6], kv_norm, w_kv_up, None)
    k_l, v_l = mla_kv(lat[5], lat[6], kv_norm, w_kv_up, rope)
    q_l = mla_q(lat[4], q_norm, w_q_up, rope)
    scale = (MLA_NOPE + MLA_ROPE) ** -0.5
    b_lat = blocked_attention(q_l, jnp.concatenate([k_c, k_l], 1), jnp.concatenate([v_c, v_l], 1), scale)
    y_lat = jnp.concatenate([a_lat, b_lat.reshape(b, s_len, -1)], -1) @ w_out
    if not need_ctx:
        return y_lat, None
    l_len = u_ctx.shape[1]
    a_ctx = gdn_output(o_ctx, ctx[1], out_norm)
    b_ctx = blocked_attention(mla_q(ctx[4], q_norm, w_q_up, None), k_c, v_c, scale)
    y_ctx = jnp.concatenate([a_ctx, b_ctx.reshape(b, l_len, -1)], -1) @ w_out
    return y_lat, y_ctx

def odd_mixer(u_lat, u_ctx, need_ctx, w_in, w_out, rpb, q_norm, k_norm, rope):
    b, s_len, _ = u_lat.shape
    lat = split_cols(u_lat @ w_in, ODD_SPLITS)
    ctx = split_cols(u_ctx @ w_in, ODD_SPLITS)
    kn_c, vn_c = to_heads(ctx[1], NA_HEADS), to_heads(ctx[2], NA_HEADS)
    c_lat = neighbourhood_attention(to_heads(lat[0], NA_HEADS), to_heads(lat[1], NA_HEADS),
                                    to_heads(lat[2], NA_HEADS), kn_c, vn_c, rpb)
    kd_c = rms_norm_2(to_heads(ctx[4], GQA_KV_HEADS), k_norm)
    vd_c = to_heads(ctx[5], GQA_KV_HEADS)
    qd_l = apply_rope(rms_norm_2(to_heads(lat[3], GQA_HEADS), q_norm), *rope)
    kd_l = apply_rope(rms_norm_2(to_heads(lat[4], GQA_KV_HEADS), k_norm), *rope)
    scale = GQA_DIM ** -0.5
    d_lat = blocked_attention(qd_l, jnp.concatenate([kd_c, kd_l], 1),
                              jnp.concatenate([vd_c, to_heads(lat[5], GQA_KV_HEADS)], 1), scale)
    y_lat = jnp.concatenate([c_lat.reshape(b, s_len, -1), d_lat.reshape(b, s_len, -1)], -1) @ w_out
    if not need_ctx:
        return y_lat, None
    l_len = u_ctx.shape[1]
    c_ctx_o = blocked_attention(to_heads(ctx[0], NA_HEADS), kn_c, vn_c, NA_DIM ** -0.5)
    d_ctx = blocked_attention(rms_norm_2(to_heads(ctx[3], GQA_HEADS), q_norm), kd_c, vd_c, scale)
    y_ctx = jnp.concatenate([c_ctx_o.reshape(b, l_len, -1), d_ctx.reshape(b, l_len, -1)], -1) @ w_out
    return y_lat, y_ctx

def second_inputs(seed: int = 0) -> dict:
    key = jax.random.key(seed)
    ks = iter(jax.random.split(key, 40))
    f32 = jnp.float32

    def nrm(shape, scale):
        return jax.random.normal(next(ks), shape, f32) * scale

    def gain(shape):
        return 1.0 + 0.05 * jax.random.normal(next(ks), shape, f32)

    d = D_MODEL
    x = nrm((BATCH, SEQ, d), 1.0)
    c = nrm((BATCH, d), 1.0)
    ctx = nrm((BATCH, CTX_LEN, d), 1.0)
    c_ctx = nrm((d,), 1.0)
    w_mod = nrm((DEPTH_2, d, 6 * d), 0.5 * d ** -0.5)
    b_mod = nrm((DEPTH_2, 6 * d), 0.01)
    g_pre_mix = gain((DEPTH_2, d))
    g_post_mix = gain((DEPTH_2, d))
    g_pre_ffn = gain((DEPTH_2, d))
    g_post_ffn = gain((DEPTH_2, d))
    w_ffn_gate = nrm((DEPTH_2, d, D_FF), d ** -0.5)
    w_ffn_up = nrm((DEPTH_2, d, D_FF), d ** -0.5)
    w_ffn_down = nrm((DEPTH_2, D_FF, d), D_FF ** -0.5)
    w_in_even = nrm((N_EVEN, d, IN_EVEN), d ** -0.5)
    w_out_even = nrm((N_EVEN, MIX_EVEN, d), MIX_EVEN ** -0.5)
    gdn_conv = nrm((N_EVEN, GDN_CONV, 2 * GDN_QK_W + GDN_V_W), GDN_CONV ** -0.5)
    gdn_a_log = jnp.log(jax.random.uniform(next(ks), (N_EVEN, 2, GDN_HEADS), f32, 1.0, 16.0))
    dt = jnp.exp(jax.random.uniform(next(ks), (N_EVEN, 2, GDN_HEADS), f32,
                                    float(np.log(1e-3)), float(np.log(1e-1))))
    gdn_dt_bias = dt + jnp.log(-jnp.expm1(-dt))
    gdn_out_norm = gain((N_EVEN, GDN_DV))
    mla_q_norm = gain((N_EVEN, MLA_Q_LORA))
    mla_w_q_up = nrm((N_EVEN, MLA_Q_LORA, MLA_HEADS * (MLA_NOPE + MLA_ROPE)), MLA_Q_LORA ** -0.5)
    mla_kv_norm = gain((N_EVEN, MLA_KV_LORA))
    mla_w_kv_up = nrm((N_EVEN, MLA_KV_LORA, MLA_HEADS * (MLA_NOPE + MLA_V)), MLA_KV_LORA ** -0.5)
    w_in_odd = nrm((N_ODD, d, IN_ODD), d ** -0.5)
    w_out_odd = nrm((N_ODD, MIX_ODD, d), MIX_ODD ** -0.5)
    na_rpb = nrm((N_ODD, NA_HEADS, 2 * NA_WIN_H - 1, 2 * NA_WIN_W - 1), 0.1)
    gqa_q_norm = gain((N_ODD, GQA_DIM))
    gqa_k_norm = gain((N_ODD, GQA_DIM))
    return {'x': x, 'c': c, 'ctx': ctx, 'c_ctx': c_ctx, 'w_mod': w_mod, 'b_mod': b_mod,
            'g_pre_mix': g_pre_mix, 'g_post_mix': g_post_mix, 'g_pre_ffn': g_pre_ffn,
            'g_post_ffn': g_post_ffn, 'w_ffn_gate': w_ffn_gate, 'w_ffn_up': w_ffn_up,
            'w_ffn_down': w_ffn_down, 'w_in_even': w_in_even, 'w_out_even': w_out_even,
            'gdn_conv': gdn_conv, 'gdn_a_log': gdn_a_log, 'gdn_dt_bias': gdn_dt_bias,
            'gdn_out_norm': gdn_out_norm, 'mla_q_norm': mla_q_norm, 'mla_w_q_up': mla_w_q_up,
            'mla_kv_norm': mla_kv_norm, 'mla_w_kv_up': mla_w_kv_up, 'w_in_odd': w_in_odd,
            'w_out_odd': w_out_odd, 'na_rpb': na_rpb, 'gqa_q_norm': gqa_q_norm, 'gqa_k_norm': gqa_k_norm}

def second_block(x, c, ctx, c_ctx, w_mod, b_mod, g_pre_mix, g_post_mix, g_pre_ffn, g_post_ffn,
              w_ffn_gate, w_ffn_up, w_ffn_down, w_in_even, w_out_even, gdn_conv, gdn_a_log,
              gdn_dt_bias, gdn_out_norm, mla_q_norm, mla_w_q_up, mla_kv_norm, mla_w_kv_up,
              w_in_odd, w_out_odd, na_rpb, gqa_q_norm, gqa_k_norm):
    s_len = x.shape[1]
    rope_mla = axial_rope(s_len, MLA_ROPE)
    rope_gqa = axial_rope(s_len, GQA_DIM)
    h, hc = x, ctx
    for i in range(DEPTH_2):
        last = i == DEPTH_2 - 1
        mod = (jax.nn.silu(c) @ w_mod[i] + b_mod[i])[:, None, :]
        mod_c = (jax.nn.silu(c_ctx) @ w_mod[i] + b_mod[i])[None, None, :]
        sh_m, sc_m, gt_m, sh_f, sc_f, gt_f = jnp.split(mod, 6, axis=-1)
        csh_m, csc_m, cgt_m, csh_f, csc_f, cgt_f = jnp.split(mod_c, 6, axis=-1)
        u = modulate(rms_norm_2(h, g_pre_mix[i]), sh_m, sc_m)
        uc = modulate(rms_norm_2(hc, g_pre_mix[i]), csh_m, csc_m)
        j = i // 2
        if i % 2 == 0:
            y, yc = even_mixer(u, uc, not last, w_in_even[j], w_out_even[j], gdn_conv[j], gdn_a_log[j],
                               gdn_dt_bias[j], gdn_out_norm[j], mla_q_norm[j], mla_w_q_up[j],
                               mla_kv_norm[j], mla_w_kv_up[j], rope_mla)
        else:
            y, yc = odd_mixer(u, uc, not last, w_in_odd[j], w_out_odd[j], na_rpb[j],
                              gqa_q_norm[j], gqa_k_norm[j], rope_gqa)
        h = h + gt_m * rms_norm_2(y, g_post_mix[i])
        f = swiglu(modulate(rms_norm_2(h, g_pre_ffn[i]), sh_f, sc_f), w_ffn_gate[i], w_ffn_up[i], w_ffn_down[i])
        h = h + gt_f * rms_norm_2(f, g_post_ffn[i])
        if not last:
            hc = hc + cgt_m * rms_norm_2(yc, g_post_mix[i])
            fc = swiglu(modulate(rms_norm_2(hc, g_pre_ffn[i]), csh_f, csc_f), w_ffn_gate[i], w_ffn_up[i], w_ffn_down[i])
            hc = hc + cgt_f * rms_norm_2(fc, g_post_ffn[i])
    return h


def setup_inputs(seed=0):
    out = dict(first_inputs(seed))
    for name, value in second_inputs(seed + 1).items():
        if name != "x":
            out[name + "_2"] = value
    return out


def reference(
    x, c, norm_pre_g, norm_post_g, w_mod, b_mod, gla_w_in, gla_w_a2, gla_b_a, gla_g_head,
    gla_w_out, sgu_w_in, sgu_ln_g, sgu_ln_b, sgu_w_s, sgu_b_s, sgu_w_out, fox_w_in, fox_b_f,
    fox_g_q, fox_g_k, fox_w_out, c_2, ctx_2, c_ctx_2, w_mod_2, b_mod_2, g_pre_mix_2,
    g_post_mix_2, g_pre_ffn_2, g_post_ffn_2, w_ffn_gate_2, w_ffn_up_2, w_ffn_down_2,
    w_in_even_2, w_out_even_2, gdn_conv_2, gdn_a_log_2, gdn_dt_bias_2, gdn_out_norm_2,
    mla_q_norm_2, mla_w_q_up_2, mla_kv_norm_2, mla_w_kv_up_2, w_in_odd_2, w_out_odd_2, na_rpb_2,
    gqa_q_norm_2, gqa_k_norm_2,
):
    x = first_block(
        x, c, norm_pre_g, norm_post_g, w_mod, b_mod, gla_w_in, gla_w_a2, gla_b_a, gla_g_head,
        gla_w_out, sgu_w_in, sgu_ln_g, sgu_ln_b, sgu_w_s, sgu_b_s, sgu_w_out, fox_w_in, fox_b_f,
        fox_g_q, fox_g_k, fox_w_out,
    )
    return second_block(
        x, c_2, ctx_2, c_ctx_2, w_mod_2, b_mod_2, g_pre_mix_2, g_post_mix_2, g_pre_ffn_2,
        g_post_ffn_2, w_ffn_gate_2, w_ffn_up_2, w_ffn_down_2, w_in_even_2, w_out_even_2,
        gdn_conv_2, gdn_a_log_2, gdn_dt_bias_2, gdn_out_norm_2, mla_q_norm_2, mla_w_q_up_2,
        mla_kv_norm_2, mla_w_kv_up_2, w_in_odd_2, w_out_odd_2, na_rpb_2, gqa_q_norm_2,
        gqa_k_norm_2,
    )


_drawn_inputs = setup_inputs


def setup_inputs(seed=0):
    import zlib

    import numpy as np

    out = dict(_drawn_inputs(seed))
    spreads = {}
    factors = {'fox_b_f': 3.976,
     'fox_g_q': 2.76,
     'fox_g_k': 2.874,
     'b_mod_2': 3.584,
     'g_pre_mix_2': 3.267,
     'g_post_mix_2': 4.303,
     'g_pre_ffn_2': 3.025,
     'g_post_ffn_2': 4.364,
     'gdn_out_norm_2': 5.771,
     'mla_q_norm_2': 8.0,
     'mla_kv_norm_2': 8.0,
     'na_rpb_2': 8.0,
     'gqa_q_norm_2': 8.0,
     'gqa_k_norm_2': 8.0}
    for name, (base, spread) in spreads.items():
        noise = np.random.default_rng([zlib.crc32(name.encode()), seed]).standard_normal(out[name].shape)
        drawn = base * np.exp(spread * noise) if base else spread * noise
        out[name] = jnp.asarray(drawn.astype(out[name].dtype))
    for name, factor in factors.items():
        out[name] = (out[name] * factor).astype(out[name].dtype)
    return out
```

```python
import numpy as np
import concourse.bass as bass
import concourse.mybir as mybir
from concourse.alu_op_type import AluOpType as ALU

F32 = mybir.dt.float32
U32 = mybir.dt.uint32
ACT = mybir.ActivationFunctionType
AX = mybir.AxisListType

P = 128
D = 1024
KT = D // P
NLAT, NCTX = 4, 2
NTOK = NLAT + NCTX
NMAX = 512
EPS = 1e-6
LEVELS = 7
DFF = 2816
FT = DFF // P
LAT, CTX = list(range(NLAT)), list(range(NLAT, NTOK))

RING = 3
SLOT = KT * NMAX
ARENA = 23600


class Program:

    ENGINES = ("pe", "act", "dve", "pool", "sp")

    def __init__(self, nc, stack):
        self.nc = nc
        self.queue = {e: [] for e in self.ENGINES}
        self.sem = {e: stack.enter_context(nc.semaphore("done_" + e)) for e in self.ENGINES}
        self.count = {e: 0 for e in self.ENGINES}
        self.waited = {e: {} for e in self.ENGINES}
        self.stack = stack
        self.names = {}

    def last(self, engine):
        return (engine, self.count[engine])

    def put(self, engine, fn, after=(), count=True):
        need = {}
        todo = list(after)
        while todo:
            x = todo.pop()
            if x is None:
                continue
            if isinstance(x, list):
                todo.extend(x)
                continue
            if x[1] > 0:
                need[x[0]] = max(need.get(x[0], 0), x[1])
        seen = self.waited[engine]
        for name, value in need.items():
            if seen.get(name, 0) < value:
                seen[name] = value
                sem = self.sem[name] if name in self.sem else self.names[name]
                self.queue[engine].append(lambda e, s=sem, v=value: e.wait_ge(s, v))
        if count:
            self.count[engine] += 1
            self.queue[engine].append(lambda e, f=fn, s=self.sem[engine]: f(e).then_inc(s, 1))
            return (engine, self.count[engine])
        self.queue[engine].append(lambda e, f=fn: f(e))
        return None

    def dma(self, engine, stream, out, in_, after=()):
        if stream not in self.names:
            self.names[stream] = self.stack.enter_context(self.nc.semaphore(stream))
            self.count[stream] = 0
        self.put(engine, lambda e, s=self.names[stream]: e.dma_start(out, in_).then_inc(s, 16), after, count=False)
        self.count[stream] += 16
        return (stream, self.count[stream])

    def mm(self, out, lhsT, rhs, start=True, stop=True, after=(), count=False):
        return self.put("pe", lambda e: e.matmul(out, lhsT, rhs, start=start, stop=stop), after, count)

    def turn(self, out, in_, ident, after=(), count=False):
        return self.put("pe", lambda e: e.transpose(out, in_, ident), after, count)

    def act(self, out, in_, func, after=(), bias=0.0, scale=1.0, accum=None):
        kw = {} if accum is None else {"accum_out": accum}
        return self.put("act", lambda e: e.activation(out, in_, func, bias=bias, scale=scale, **kw),
                        [self.last("act"), list(after)])

    def tt(self, out, a, b, op, after=(), eng="dve"):
        return self.put(eng, lambda e: e.tensor_tensor(out, a, b, op), [self.last(eng), list(after)])

    def ts(self, out, a, s1, s2, op0, op1=None, after=(), eng="dve"):
        if op1 is None:
            return self.put(eng, lambda e: e.tensor_scalar(out, a, s1, None, op0), [self.last(eng), list(after)])
        return self.put(eng, lambda e: e.tensor_scalar(out, a, s1, s2, op0, op1), [self.last(eng), list(after)])

    def stt(self, out, a, s, b, op0, op1, after=()):
        return self.put("dve", lambda e: e.scalar_tensor_tensor(out, a, s, b, op0, op1),
                        [self.last("dve"), list(after)])

    def copy(self, out, a, after=(), eng="dve"):
        if eng == "act":
            return self.act(out, a, ACT.Copy, after)
        return self.put(eng, lambda e: e.tensor_copy(out, a), [self.last(eng), list(after)])

    def recip(self, out, a, after=()):
        return self.put("dve", lambda e: e.reciprocal(out, a), [self.last("dve"), list(after)])

    def reduce(self, out, a, op, after=(), negate=False):
        return self.put("dve", lambda e: e.tensor_reduce(out, a, AX.X, op, negate=negate),
                        [self.last("dve"), list(after)])

    def memset(self, out, value, after=(), eng="dve"):
        return self.put(eng, lambda e: e.memset(out, value), [self.last(eng), list(after)])


def grid(ap, a):
    return ap.rearrange("p (a b) -> p a b", a=a)


def over(ap, n):
    p, m = ap.shape
    return ap.unsqueeze(2).broadcast_to((p, m, n))


def rows_over(ap, n):
    p, m = ap.shape
    return ap.unsqueeze(1).broadcast_to((p, n, m))


def build(nc, io, out, stop=99):
    from contextlib import ExitStack
    stack = ExitStack()
    with stack:
        program(nc, stack, io, out, stop)


def program(nc, stack, io, out, stop):
    g = Program(nc, stack)
    mm, turn, act, tt, ts, stt, copy = g.mm, g.turn, g.act, g.tt, g.ts, g.stt, g.copy

    def sb(name, n):
        return stack.enter_context(nc.sbuf_tensor(name, [P, n], F32))

    X = grid(sb("x_lat", NLAT * D)[:, :], NLAT)
    HC = grid(sb("x_ctx", NCTX * D)[:, :], NCTX)
    FEAT_t = sb("feat", KT * NTOK * P)
    FEAT = grid(FEAT_t[:, :], KT)
    RING_t = sb("weights", RING * SLOT)
    AR = sb("arena", ARENA)
    CONST = sb("const", 3 * P + 2 * LEVELS * P)
    PCOL = sb("param_cols", 4 * P)
    MODC = sb("mod_cols", 96)
    SM_t = sb("small", 330)
    PS_t = stack.enter_context(nc.psum_tensor("psum", [P, 8 * NMAX], F32))

    ident, TRI_U, TRI_L = (CONST[:, i * P:(i + 1) * P] for i in range(3))
    LEVEL_U = [CONST[:, (3 + i) * P:(4 + i) * P] for i in range(LEVELS)]
    LEVEL_L = [CONST[:, (3 + LEVELS + i) * P:(4 + LEVELS + i) * P] for i in range(LEVELS)]

    def ar(off, n):
        assert off + n <= ARENA, (off, n)
        return AR[:, off:off + n]

    def resid(t):
        return X[:, t, :] if t < NLAT else HC[:, t - NLAT, :]

    free_banks = [(i, []) for i in range(8)]

    def bank():
        i, toks = free_banks.pop(0)
        return i, PS_t[:, i * NMAX:(i + 1) * NMAX], toks

    def bank_pair():
        for i, _ in list(free_banks):
            if i % 2 == 0 and any(j == i + 1 for j, _ in free_banks):
                a = next(x for x in free_banks if x[0] == i)
                b = next(x for x in free_banks if x[0] == i + 1)
                free_banks.remove(a)
                free_banks.remove(b)
                return i, PS_t[:, i * NMAX:(i + 2) * NMAX], a[1] + b[1]
        raise AssertionError("no pair of banks")

    def free(i, *toks, n=1):
        for j in range(n):
            free_banks.append((i + j, list(toks)))

    flip = [0]

    def evac_engine():
        flip[0] ^= 1
        return "act" if flip[0] else "dve"

    slot_readers = [[] for _ in range(RING)]
    n_chunks = [0]

    def load_weights(src, kt, nc_):
        s = n_chunks[0] % RING
        n_chunks[0] += 1
        view = RING_t[:, s * SLOT:s * SLOT + kt * nc_].rearrange("p (k n) -> p k n", k=kt)
        tok = g.dma("sp", f"weights_{s}", view, src.rearrange("(k p) n -> p k n", p=P), after=slot_readers[s])
        return s, view, tok

    def linear_tok(src, nk, w, ncols, tiles, done, ready):
        for n0 in range(0, ncols, NMAX):
            n = min(NMAX, ncols - n0)
            s, wv, wt = load_weights(w[:, n0:n0 + n], nk, n)
            for t in tiles:
                b, ps, bt = bank()
                for k in range(nk):
                    tok = mm(ps[:, 0:n], src(k, t), wv[:, k, :], k == 0, k == nk - 1,
                             after=[ready, wt, bt] if k == 0 else (), count=k == nk - 1)
                free(b, *done(t, n0, n, ps[:, 0:n], tok))
            slot_readers[s] = [tok]

    def linear_feat(src, nk, w, ncols, ranges, done, ready):
        for n0 in range(0, ncols, NMAX):
            n = min(NMAX, ncols - n0)
            s, wv, wt = load_weights(w[:, n0:n0 + n], nk, n)
            for m0 in range(0, n, P):
                m = min(P, n - m0)
                for c0, c in ranges:
                    b, ps, bt = bank()
                    for k in range(nk):
                        tok = mm(ps[0:m, 0:c], wv[:, k, m0:m0 + m], src(k, c0, c), k == 0, k == nk - 1,
                                 after=[ready, wt, bt] if k == 0 else (), count=k == nk - 1)
                    free(b, *done((n0 + m0) // P, c0, c, ps[0:m, 0:c], tok))
            slot_readers[s] = [tok]

    feat_tile = lambda k, t: FEAT[:, k, t * P:(t + 1) * P]
    feat_cols = lambda k, c0, c: FEAT[:, k, c0:c0 + c]

    t_const = g.dma("sp", "const_in", CONST[:, :], io["k_const"][:, :])
    t_x = g.dma("act", "x_in", X, io["x"].rearrange("a (t p) d -> p (a t) d", p=P))
    t_hc = g.dma("act", "ctx_in", HC, io["ctx_2"].rearrange("a (t p) d -> p (a t) d", p=P))

    col_of = {}
    prow = grid(ar(0, 4 * P), 4)

    def as_rows(ap, k):
        return ap.rearrange(k, b=P) if "b" in k else ap

    groups = [
        [("norm_pre_g", "l (a b) -> (l a) b", 32), ("norm_post_g", "l (a b) -> (l a) b", 32),
         ("g_pre_mix_2", "l (a b) -> (l a) b", 16), ("g_post_mix_2", "l (a b) -> (l a) b", 16),
         ("g_pre_ffn_2", "l (a b) -> (l a) b", 16), ("g_post_ffn_2", "l (a b) -> (l a) b", 16)],
        [("c", "l (a b) -> (l a) b", 8), ("c_2", "l (a b) -> (l a) b", 8), ("c_ctx_2", "(a b) -> a b", 8),
         ("gla_b_a", "l (a b) -> (l a) b", 8), ("gdn_conv_2", "l t (a b) -> (l t a) b", 60),
         ("mla_q_norm_2", "l (a b) -> (l a) b", 2), ("mla_kv_norm_2", "l (a b) -> (l a) b", 1),
         ("sgu_b_s", "l a b -> (l a) b", 4)],
        [("b_mod", "l (a b) -> (l a) b", 96)],
        [("b_mod_2", "l (a b) -> (l a) b", 96)],
    ]
    t_pc = []
    for q, group in enumerate(groups):
        r = 0
        for name, how, n in group:
            t_row = g.dma("act", f"params_{q}", prow[r:r + n, q, :], as_rows(io[name], how))
            col_of[name] = (q, r)
            r += n
        b, ps, bt = bank()
        tok = turn(ps[:, 0:r], prow[0:r, q, :], ident[0:r, 0:r], after=[t_row, t_const, bt], count=True)
        t_pc.append(copy(PCOL[:, q * P:q * P + r], ps[:, 0:r], after=[tok]))
        free(b, t_pc[-1])

    def pcol(name, i, n=1):
        q, r = col_of[name]
        return PCOL[:, q * P + r + i:q * P + r + i + n]

    small_used = [0]

    def small(n):
        a = small_used[0]
        small_used[0] += n
        assert small_used[0] <= 330, small_used
        return SM_t[:, a:a + n]

    eps_col = small(1)
    one_col = small(1)
    g.memset(eps_col, EPS)
    g.memset(one_col, 1.0)
    COND = small(24)
    act(COND[:, 0:8], pcol("c", 0, 8), ACT.Silu, after=t_pc)
    cond2 = COND[:, 8:24].rearrange("p (k v) -> p k v", v=2)
    act(cond2[:, :, 0], pcol("c_2", 0, 8), ACT.Silu)
    t_cond = act(cond2[:, :, 1], pcol("c_ctx_2", 0, 8), ACT.Silu)
    ROW_t = sb("mod_rows", 2 * NMAX)
    row_readers = [[], []]
    n_rows = [0]

    def modulation(w, bias_name, bias_at, cond, nv, ncols):
        toks = []
        mod_free = g.last("dve")
        for n0 in range(0, ncols, NMAX):
            s, wv, wt = load_weights(w[:, n0:n0 + NMAX], KT, NMAX)
            b, ps, bt = bank()
            for k in range(KT):
                tok = mm(ps[0:nv, :], cond(k), wv[:, k, :], k == 0, k == KT - 1,
                         after=[wt, bt, t_cond] if k == 0 else (), count=k == KT - 1)
            slot_readers[s] = [tok]
            i = n_rows[0] % 2
            n_rows[0] += 1
            row = ROW_t[0:nv, i * NMAX:(i + 1) * NMAX]
            tr = copy(row, ps[0:nv, :], after=[tok, row_readers[i]], eng="act")
            free(b, tr)
            b, ps, bt = bank()
            for m in range(4):
                tok = mm(ps[:, m * nv:(m + 1) * nv], row[:, m * P:(m + 1) * P], ident[0:nv, 0:nv],
                         after=[tr, bt, t_const], count=m == 3)
            row_readers[i] = [tok]
            m0 = n0 // P
            tc = tt(MODC[:, m0 * nv:(m0 + 4) * nv].rearrange("p (m v) -> p m v", v=nv),
                    ps[:, 0:4 * nv].rearrange("p (m v) -> p m v", v=nv),
                    over(pcol(bias_name, bias_at + m0, 4), nv), ALU.add, after=[tok, mod_free])
            free(b, tc)
            toks = [tc]
        return toks

    def modc(part, v, nv):
        return MODC[:, 0:48 * nv].rearrange("p (m v) -> p m v", v=nv)[:, part * KT:(part + 1) * KT, v] if nv > 1 \
            else MODC[:, part * KT:(part + 1) * KT]

    SSQ = small(12)
    RSTD = small(12)
    PRE_A = small(16)
    PRE_B = small(16)
    GATE = small(16)
    junk_t = sb("junk", NMAX)

    def rstd_of(out, ss, n, after=()):
        a = act(out, ss, ACT.Sqrt, bias=eps_col[0:out.shape[0], :], scale=1.0 / n, after=after)
        return g.recip(out, out, after=[a])

    def prenorm(tiles, xn_off, g_name, g_at, parts, nv, ready):
        shift, scale = parts
        gcol = pcol(g_name, g_at, KT)
        for v, some in ((0, [t for t in tiles if t < NLAT]), (1, [t for t in tiles if t >= NLAT])):
            if some:
                stt(PRE_A[:, v * 8:v * 8 + 8], modc(scale, v, nv), 1.0, gcol, ALU.add, ALU.mult, after=ready)
                copy(PRE_B[:, v * 8:v * 8 + 8], modc(shift, v, nv))
        xn = grid(ar(xn_off, NTOK * D), NTOK)
        for t in tiles:
            tq = act(xn[:, t, :], resid(t), ACT.Square, accum=SSQ[:, t:t + 1], after=[g.last("dve"), t_x, t_hc])
        t0, t1 = tiles[0], tiles[-1] + 1
        tr = rstd_of(RSTD[:, t0:t1], SSQ[:, t0:t1], D, after=[tq])
        txn = {}
        for t in tiles:
            if t % 2:
                txn[t] = act(xn[:, t, :], resid(t), ACT.Copy, scale=RSTD[:, t:t + 1], after=[tr])
            else:
                txn[t] = ts(xn[:, t, :], resid(t), RSTD[:, t:t + 1], None, ALU.mult, after=[tr])
        toks = []
        for v, some in ((0, [t for t in tiles if t < NLAT]), (1, [t for t in tiles if t >= NLAT])):
            for k in range(KT if some else 0):
                b, ps, bt = bank()
                for i, t in enumerate(some):
                    tok = turn(ps[:, i * P:(i + 1) * P], xn[:, t, k * P:(k + 1) * P], ident, after=[bt, txn[t]],
                               count=i == len(some) - 1)
                n = len(some) * P
                dst = FEAT[:, k, some[0] * P:some[0] * P + n]
                a, c = PRE_A[:, v * 8 + k:v * 8 + k + 1], PRE_B[:, v * 8 + k:v * 8 + k + 1]
                if k % 2:
                    te = act(dst, ps[:, 0:n], ACT.Identity, scale=a, bias=c, after=[tok, tr])
                else:
                    te = ts(dst, ps[:, 0:n], a, c, ALU.mult, ALU.add, after=[tok])
                free(b, te)
                toks.append(te)
        return [g.last("act"), g.last("dve")]

    def post_begin(v, name, at, gate_part, nv, gb_off, after):
        gc = GATE[:, v * 8:v * 8 + 8]
        tg = tt(gc, modc(gate_part, v, nv), pcol(name, at, KT), ALU.mult, after=after)
        for h in range(2):
            b, ps, bt = bank()
            for k in range(4):
                tok = mm(ps[:, k * P:(k + 1) * P], gc[:, h * 4 + k:h * 4 + k + 1].broadcast_to((P, P)), ident,
                         after=[tg, bt], count=k == 3)
            te = copy(ar(gb_off + h * NMAX, NMAX), ps, after=[tok, after], eng="act")
            free(b, te)
        return te

    def keep_y(Y):
        def done(t, n0, n, ps, tok):
            h = n0 // NMAX
            c = copy(Y[:, t, n0:n0 + n], ps, after=[tok])
            act(junk_t[:, 0:n], Y[:, t, n0:n0 + n], ACT.Square, accum=SSQ[:, 2 * t + h:2 * t + h + 1], after=[c])
            return (c,)
        return done

    def post(tiles, Y, gb_offs):
        t0, t1 = tiles[0], tiles[-1] + 1
        pairs = SSQ[:, 2 * t0:2 * t1].rearrange("p (t h) -> p t h", h=2)
        a = tt(RSTD[:, t0:t1], pairs[:, :, 0], pairs[:, :, 1], ALU.add, after=[g.last("act")])
        rstd_of(RSTD[:, t0:t1], RSTD[:, t0:t1], D, after=[a])
        for t in tiles:
            gb = ar(gb_offs[0 if t < NLAT else 1], D)
            a = stt(Y[:, t, :], Y[:, t, :], RSTD[:, t:t + 1], gb, ALU.mult, ALU.mult, after=[g.last("act")])
            tok = tt(resid(t), resid(t), Y[:, t, :], ALU.add, after=[t_x, t_hc])
        return tok

    def to_feat(y, tiles, after):
        toks = []
        for t in tiles:
            for h in range(2):
                b, ps, bt = bank()
                for k in range(4):
                    kk = h * 4 + k
                    tok = turn(ps[:, k * P:(k + 1) * P], y(t)[:, kk * P:(kk + 1) * P], ident,
                               after=[after, bt], count=k == 3)
                e = evac_engine()
                te = copy(FEAT[:, h * 4:h * 4 + 4, t * P:(t + 1) * P], grid(ps, 4), after=[tok, after], eng=e)
                free(b, te)
                toks.append(te)
        return toks

    def first_layer_end(i, y, w_out, Y, gb_off, tiles=LAT):
        tf = to_feat(y, tiles, [g.last("act"), g.last("dve")])
        tg = post_begin(0, "norm_post_g", i * KT, 2, 1, gb_off, [g.last("dve"), g.last("pe")])
        linear_tok(feat_tile, KT, w_out, D, tiles, keep_y(Y), [tf])

    def head_rms(ps, nh, d, out, sq, ss, tok):
        a = act(sq, ps, ACT.Square, after=[tok])
        g.reduce(ss, grid(sq, nh), ALU.add, after=[a])
        r = rstd_of(ss, ss, d, after=[g.last("dve")])
        c = tt(grid(out, nh), grid(ps, nh), over(ss, d), ALU.mult, after=[r])
        return a, c

    def attention(units, tmp, nk_max):
        PR = [tmp[:, i * nk_max:(i + 1) * nk_max] for i in range(2)]
        PTR = [tmp[:, (2 + i) * nk_max:(3 + i) * nk_max] for i in range(2)]
        S = tmp[:, 4 * nk_max:5 * nk_max] if units[0]["bias"] else None
        NEGM, SUM = att_cols[:, 0:2], att_cols[:, 2:4]
        pr_readers, pt_readers = [[], []], [[], []]
        state = {}

        def stage_scores(n):
            u, i = units[n], n % 2
            nk = u["nk"]
            b, ps, bt = bank_pair()
            for j, (lt, rh, n0, m, st, sp_) in enumerate(u["scores"]):
                tok = mm(ps[:, n0:n0 + m], lt, rh, st, sp_, after=[bt, u["ready"]], count=j == len(u["scores"]) - 1)
            src = ps[:, 0:nk]
            fr = []
            if u["bias"]:
                tb = u["bias"](src, S[:, 0:nk], tok)
                src = S[:, 0:nk]
                fr = [tb]
            tm = g.reduce(NEGM[:, i:i + 1], src, ALU.max, negate=True, after=[tok, g.last("act")])
            te = act(PR[i][:, 0:nk], src, ACT.Exp, bias=NEGM[:, i:i + 1], accum=SUM[:, i:i + 1],
                     after=[tm, pr_readers[i], tok])
            free(b, tm, te, *fr, n=2)
            state[n] = te

        def stage_turn(n):
            u, i = units[n], n % 2
            nk = u["nk"]
            b, ps, bt = bank_pair()
            for j in range(nk // P):
                tok = turn(ps[:, j * P:(j + 1) * P], PR[i][:, j * P:(j + 1) * P], ident, after=[bt, state[n]],
                           count=j == nk // P - 1)
            pr_readers[i] = [tok]
            te = copy(PTR[i][:, 0:nk], ps[:, 0:nk], after=[tok, pt_readers[i]], eng=evac_engine())
            free(b, te, n=2)
            tr = g.recip(SUM[:, i:i + 1], SUM[:, i:i + 1], after=[state[n]])
            b, ps, bt = bank()
            for j, v in enumerate(u["values"]):
                tok = mm(ps[:, 0:u["dv"]], PTR[i][:, j * P:(j + 1) * P], v, j == 0, j == len(u["values"]) - 1,
                         after=[bt, te, u["ready"]], count=j == len(u["values"]) - 1)
            pt_readers[i] = [tok]
            free(b, u["done"](ps[:, 0:u["dv"]], SUM[:, i:i + 1], [tok, tr]))

        stage_scores(0)
        for n in range(len(units)):
            if n + 1 < len(units):
                stage_scores(n + 1)
            stage_turn(n)

    att_cols = small(4)

    def gla(i, j, ready):
        H, DK, DV = 4, 128, 256
        q, k = grid(ar(0, 2048), H), grid(ar(2048, 2048), H)
        v, z = grid(ar(4096, 4096), NLAT), grid(ar(8192, 4096), NLAT)
        b_, qe, e_ = ar(12288, 2048), ar(14336, 2048), ar(16384, 2048)
        S_ = grid(ar(18432, 1024), H)
        aT = ar(19456, 512)
        gh = ar(19968, 1024)
        wa2 = ar(20992, 512)
        reset = ar(21504, 512)
        ss = ar(22016, 16)
        AT, QK0, QK1 = (FEAT_t[:, n * 2048:(n + 1) * 2048] for n in range(3))
        w = io["gla_w_in"][j]
        t_par = g.dma("pool", "layer_params", gh, io["gla_g_head"][j].rearrange("h d -> (h d)").partition_broadcast(P),
                      after=ready)
        t_par = g.dma("pool", "layer_params", wa2[0:16, :], io["gla_w_a2"][j], after=ready)
        t_par = g.dma("pool", "layer_params", reset, io["k_reset"][:, :], after=ready)
        lat = [(0, NLAT * P)]

        def keep_a(m, c0, c, ps, tok):
            return (copy(aT[0:16, c0:c0 + c], ps, after=[tok]),)

        linear_feat(feat_cols, KT, w[:, 3072:3088], 16, lat, keep_a, ready)
        t_aT = g.last("dve")

        for h in range(H):
            b, ps, bt = bank()
            tok = mm(ps, wa2[0:16, h * DK:(h + 1) * DK], aT[0:16, :], after=[bt, t_aT, t_par], count=True)
            xs, es = b_[:, h * 512:(h + 1) * 512], e_[:, h * 512:(h + 1) * 512]
            tx = ts(xs, ps, pcol("gla_b_a", j * 4 + h), None, ALU.add, after=[tok])
            free(b, tx)
        act(e_, b_, ACT.Abs, after=[tx])
        act(e_, e_, ACT.Exp, scale=-1.0)
        tl = act(e_, e_, ACT.Ln, bias=one_col)
        ta = stt(b_, b_, 0.0, e_, ALU.min, ALU.subtract, after=[tl])
        for h in range(H):
            xs = b_[:, h * 512:(h + 1) * 512]
            tb = g.put("dve", lambda e, xs=xs: e.tensor_tensor_scan(xs, reset, xs, 0.0, ALU.mult, ALU.add),
                       [g.last("dve"), t_par])
        tqe = act(qe, b_, ACT.Exp, scale=1.0 / 16, after=[tb])

        def keep_qk(m, c0, c, ps, tok):
            if m < 4:
                return (act(q[:, m, c0:c0 + c], ps, ACT.Copy, scale=DK ** -0.5, after=[tok]),)
            return (copy(k[:, m - 4, c0:c0 + c], ps, after=[tok]),)

        linear_feat(feat_cols, KT, w, 1024, lat, keep_qk, ready)
        t_qk = [g.last("act"), g.last("dve")]

        def keep_vz(t, n0, n, ps, tok):
            if n0 < 1024:
                return (copy(v[:, t, n0:n0 + n], ps, after=[tok], eng=evac_engine()),)
            a = act(z[:, t, n0 - 1024:n0 - 1024 + n], ps, ACT.Silu, after=[tok])
            tt(z[:, t, n0 - 1024:n0 - 1024 + n], z[:, t, n0 - 1024:n0 - 1024 + n], gh[:, n0 - 1024:n0 - 1024 + n],
               ALU.mult, after=[a, t_par], eng="pool")
            return (a,)

        linear_tok(feat_tile, KT, w[:, 1024:3072], 2048, LAT, keep_vz, ready)
        t_in = [g.last("pe"), g.last("act"), g.last("dve")]

        qf, kf = ar(0, 2048), ar(2048, 2048)
        ATg = AT.rearrange("p (n j) -> p n j", j=P)
        g.memset(AT, 0.0, after=[t_in])
        readers = [[], []]
        for lv in range(-1, LEVELS):
            if lv < 0:
                lhs, rhs, tq, mask = kf, qf, t_qk, ident
            else:
                s = 1 << lv
                QK = (QK0, QK1)[lv % 2]
                e4, b4, q4, k4, o4 = (x.rearrange("p (n h s) -> p n h s", h=2, s=s) for x in (e_, b_, qf, kf, QK))
                mid = b4[:, :, 0, s - 1:s].broadcast_to((P, 2048 // (2 * s), s))
                tt(e4[:, :, 0, :], mid, b4[:, :, 0, :], ALU.subtract, after=[g.last("act"), t_in])
                td = tt(e4[:, :, 1, :], b4[:, :, 1, :], mid, ALU.subtract)
                te = act(e_, e_, ACT.Exp, scale=1.0 / 16, after=[td])
                tt(o4[:, :, 0, :], k4[:, :, 0, :], e4[:, :, 0, :], ALU.mult, after=[te, readers[lv % 2]])
                tq = tt(o4[:, :, 1, :], q4[:, :, 1, :], e4[:, :, 1, :], ALU.mult)
                lhs = rhs = QK
                mask = LEVEL_U[lv]
            for h in range(H):
                b, ps, bt = bank()
                for c in range(NLAT):
                    at = slice((h * NLAT + c) * P, (h * NLAT + c + 1) * P)
                    tok = mm(ps[:, c * P:(c + 1) * P], lhs[:, at], rhs[:, at], after=[bt, tq], count=c == NLAT - 1)
                tm = g.put("dve", lambda e, h=h, ps=ps, mask=mask: e.copy_predicated(
                    ATg[:, h * NLAT:(h + 1) * NLAT, :], rows_over(mask.bitcast(U32), NLAT), grid(ps, NLAT)),
                    [g.last("dve"), tok])
                free(b, tm)
            readers[lv % 2] = [tok]
        t_at = tm

        blast = b_.rearrange("p (n t) -> p n t", t=P)
        tt(e_.rearrange("p (n t) -> p n t", t=P), blast[:, :, P - 1:P].broadcast_to((P, 16, P)), blast, ALU.subtract,
           after=[g.last("act")])
        te = act(e_, e_, ACT.Exp, scale=1.0 / 16, after=[g.last("dve")])
        tk = tt(e_, e_, kf, ALU.mult, after=[te])
        last_decay = ar(22032, 16)
        tc = copy(last_decay, qe.rearrange("p (n t) -> p n t", t=P)[:, :, P - 1])
        tqe = tt(qe, qe, qf, ALU.mult)
        ktok = QK0
        for n in range(4):
            b, ps, bt = bank()
            for m in range(4):
                tok = turn(ps[:, m * P:(m + 1) * P], e_[:, (4 * n + m) * P:(4 * n + m + 1) * P], ident,
                           after=[bt, tk], count=m == 3)
            t_kt = copy(ktok[:, n * 512:(n + 1) * 512], ps, after=[tok, readers], eng="act")
            free(b, t_kt)

        t_S = None
        t_pool = g.last("pool")
        for c in range(NLAT):
            t_s2 = []
            for h in range(H):
                n = h * NLAT + c
                at = slice(n * P, (n + 1) * P)
                vh = v[:, c, h * DV:(h + 1) * DV]
                b, ps, bt = bank()
                if c:
                    mm(ps[:, 0:DV], qe[:, at], S_[:, h, :], True, False, after=[bt, t_S, tqe])
                tok = mm(ps[:, 0:DV], AT[:, at], vh, c == 0, True, after=[bt, t_at], count=True)
                a = act(junk_t[:, 0:DV], ps[:, 0:DV], ACT.Square, accum=ss[:, n:n + 1], after=[tok])
                r = rstd_of(ss[:, n:n + 1], ss[:, n:n + 1], DV, after=[a])
                zh = z[:, c, h * DV:(h + 1) * DV]
                o = stt(zh, ps[:, 0:DV], ss[:, n:n + 1], zh, ALU.mult, ALU.mult, after=[r, t_pool])
                free(b, o)
                if c < NLAT - 1:
                    b, ps, bt = bank()
                    tok = mm(ps[:, 0:DV], ktok[:, at], vh, after=[bt, t_kt], count=True)
                    if c == 0:
                        t_s2 = copy(S_[:, h, :], ps[:, 0:DV], after=[tok])
                    else:
                        t_s2 = stt(S_[:, h, :], S_[:, h, :], last_decay[:, n:n + 1], ps[:, 0:DV], ALU.mult, ALU.add,
                                   after=[tok])
                    free(b, t_s2)
            t_S = t_s2
        first_layer_end(i, lambda t: z[:, t, :], io["gla_w_out"][j], v, 0)
        return v, 0

    def sgu(i, ready):
        u, v, z = (grid(ar(n * 4096, 4096), NLAT) for n in range(3))
        lng, lnb = ar(12288, 1024), ar(13312, 1024)
        ws, wsT = grid(ar(14336, 512), 4), grid(ar(14848, 512), 4)
        st, mv = ar(15360, 12), ar(15372, 8)
        tmp = ar(15384, 512)
        t_par = g.dma("pool", "layer_params", lng, io["sgu_ln_g"][0].partition_broadcast(P), after=ready)
        t_par = g.dma("pool", "layer_params", lnb, io["sgu_ln_b"][0].partition_broadcast(P), after=ready)
        t_par = g.dma("pool", "layer_params", ws, io["sgu_w_s"][0].rearrange("g t s -> t g s"), after=ready)
        b, ps, bt = bank()
        for n in range(4):
            tok = turn(ps[:, n * P:(n + 1) * P], ws[:, n, :], ident, after=[bt, t_par], count=n == 3)
        t_ws = tt(wsT, grid(ps, 4), rows_over(TRI_U, 4), ALU.mult, after=[tok])
        free(b, t_ws)

        def keep(t, n0, n, ps, tok):
            dst = (u, v, z)[n0 // D][:, t, n0 % D:n0 % D + n]
            return (act(dst, ps, ACT.Silu if n0 >= 2 * D else ACT.Gelu_apprx_tanh, after=[tok]),)

        w = io["sgu_w_in"][0]
        linear_tok(feat_tile, KT, w[:, D:2 * D], D, LAT, lambda t, n0, n, ps, tok: keep(t, n0 + D, n, ps, tok), ready)
        tv = g.last("act")
        for t in LAT:
            for h in range(2):
                g.put("dve", lambda e, t=t, h=h: e.bn_stats(st[:, 6 * h:6 * h + 6], v[:, t, h * 512:(h + 1) * 512]),
                      [g.last("dve"), tv])
            g.put("dve", lambda e: e.bn_aggr(mv[:, 0:2], st[:, 0:12].rearrange("p (a b) -> p a b", a=2)),
                  [g.last("dve")])
            rstd_of(mv[:, 2:3], mv[:, 1:2], 1, after=[g.last("dve")])
            ts(v[:, t, :], v[:, t, :], mv[:, 0:1], mv[:, 2:3], ALU.subtract, ALU.mult)
            tt(v[:, t, :], v[:, t, :], lng, ALU.mult, after=[t_par])
            tln = tt(v[:, t, :], v[:, t, :], lnb, ALU.add)
        linear_tok(feat_tile, KT, w[:, 0:D], D, LAT, keep, ready)
        linear_tok(feat_tile, KT, w[:, 2 * D:3 * D], D, LAT,
                   lambda t, n0, n, ps, tok: keep(t, n0 + 2 * D, n, ps, tok), ready)
        tz = g.last("act")
        for t in LAT:
            tuz = tt(z[:, t, :], z[:, t, :], u[:, t, :], ALU.mult, after=[tz], eng="pool")
            for h in range(2):
                b, ps, bt = bank()
                for n in range(2):
                    gr = 2 * h + n
                    tok = mm(ps[:, n * 256:(n + 1) * 256], wsT[:, gr, :], v[:, t, gr * 256:(gr + 1) * 256],
                             after=[bt, tln, t_ws], count=n == 1)
                for n in range(2):
                    gr = 2 * h + n
                    zz = z[:, t, gr * 256:(gr + 1) * 256]
                    o = stt(zz, ps[:, n * 256:(n + 1) * 256], pcol("sgu_b_s", gr), zz, ALU.add, ALU.mult,
                            after=[tok, tuz])
                free(b, o)
        first_layer_end(i, lambda t: z[:, t, :], io["sgu_w_out"][0], v, 0)
        return v, 0

    def fox(i, ready):
        H, DH = 16, 64
        qT, kT = grid(ar(0, 4096), 8), grid(ar(4096, 4096), 8)
        v, z = grid(ar(8192, 4096), NLAT), grid(ar(12288, 4096), NLAT)
        F, negF = ar(16384, 512), ar(16896, 512)
        Ftok = grid(ar(17408, 64), NLAT)
        qn, sq = [ar(17472, 512), ar(17984, 512)], ar(18496, 512)
        ss = ar(19008, 8)
        gq, gk, bf = ar(19016, 1), ar(19017, 1), ar(19018, 1)
        neg = ar(19020, 128)
        att = 19148
        for n in range(2):
            g.dma("pool", "layer_params", gq[64 * n:64 * n + 64, :], io["fox_g_q"].rearrange("a d -> d a"), after=ready)
            g.dma("pool", "layer_params", gk[64 * n:64 * n + 64, :], io["fox_g_k"].rearrange("a d -> d a"), after=ready)
        g.dma("pool", "layer_params", bf[0:16, :], io["fox_b_f"].rearrange("a d -> d a"), after=ready)
        t_par = g.dma("pool", "layer_params", neg, io["k_neg"][:, :], after=ready)
        gqs = ar(att + 5 * 512, 1)
        t_gq = ts(gqs, gq, DH ** -0.5, None, ALU.mult, after=[t_par])
        w = io["fox_w_in"][0]

        def keep_f(m, c0, c, ps, tok):
            return (ts(F[0:16, c0:c0 + c], ps, bf[0:16, :], None, ALU.add, after=[tok, t_par]),)

        linear_feat(feat_cols, KT, w[:, 4096:4112], 16, [(0, 512)], keep_f, ready)
        F_, N_ = F[0:16, :], negF[0:16, :]
        act(N_, F_, ACT.Abs, after=[g.last("dve")])
        act(N_, N_, ACT.Exp, scale=-1.0)
        tl = act(N_, N_, ACT.Ln, bias=one_col[0:16, :])
        stt(F_, F_, 0.0, N_, ALU.min, ALU.subtract, after=[tl])
        g.memset(N_, 1.0)
        g.put("dve", lambda e: e.tensor_tensor_scan(F_, N_, F_, 0.0, ALU.mult, ALU.add), [g.last("dve")])
        tF = ts(N_, F_, -1.0, None, ALU.mult)
        b, ps, bt = bank()
        for t in LAT:
            tok = turn(ps[:, t * 16:(t + 1) * 16], F_[:, t * P:(t + 1) * P], ident[0:16, 0:16], after=[bt, tF],
                       count=t == NLAT - 1)
        tFt = copy(Ftok, ps[:, 0:64].rearrange("p (t h) -> p t h", h=16), after=[tok])
        free(b, tFt)
        rd = [[], []]
        cnt = [0]

        def keep(t, n0, n, ps, tok):
            if n0 >= 3072:
                return (act(z[:, t, n0 - 3072:n0 - 3072 + n], ps, ACT.Silu, after=[tok]),)
            if n0 >= 2048:
                return (copy(v[:, t, n0 - 2048:n0 - 2048 + n], ps, after=[tok], eng=evac_engine()),)
            r = cnt[0] % 2
            cnt[0] += 1
            a, c = head_rms(ps, 8, DH, qn[r], sq, ss, [tok, rd[r], g.last("dve")])
            pending.append((t, n0, r, c))
            if len(pending) > 1:
                turn_q(*pending.pop(0))
            return a, c

        pending = []

        def turn_q(t, n0, r, c):
            b, ps, bt = bank()
            for m in range(4):
                tk = turn(ps[:, m * P:(m + 1) * P], qn[r][:, m * P:(m + 1) * P], ident, after=[bt, c], count=m == 3)
            rd[r] = [tk]
            dst, gcol = (qT, gqs) if n0 < D else (kT, gk)
            p0 = (n0 % D) // P
            te = act(dst[:, p0:p0 + 4, t * P:(t + 1) * P], grid(ps, 4), ACT.Copy, scale=gcol, after=[tk, t_par, t_gq])
            free(b, te)

        linear_tok(feat_tile, KT, w[:, 0:4096], 4096, LAT, keep, ready)
        while pending:
            turn_q(*pending.pop(0))
        t_in = [g.last("act"), g.last("dve"), g.last("pe")]
        units = []
        for t in LAT:
            for h in range(H):
                base, pr = 64 * (h % 2), h // 2
                nk = (t + 1) * P

                def bias(src, dst, tok, t=t, h=h, nk=nk):
                    if t:
                        ts(dst[:, 0:t * P], src[:, 0:t * P], Ftok[:, t, h:h + 1], None, ALU.add,
                           after=[tok, g.last("act")])
                    return stt(dst[:, t * P:nk], src[:, t * P:nk], Ftok[:, t, h:h + 1], neg, ALU.add, ALU.add,
                               after=[tok, g.last("act"), t_par])

                def done(ps, rinv, toks, t=t, h=h):
                    zz = z[:, t, h * DH:(h + 1) * DH]
                    return stt(zz, ps, rinv, zz, ALU.mult, ALU.mult, after=toks)

                units.append(dict(
                    nk=nk, ready=t_in, bias=bias, dv=DH, done=done,
                    scores=[(qT[base:base + 64, pr, t * P:(t + 1) * P], kT[base:base + 64, pr, 0:nk], 0, nk, True, False),
                            (ident[0:16, h:h + 1].broadcast_to((16, P)), N_[:, 0:nk], 0, nk, False, True)],
                    values=[v[:, s, h * DH:(h + 1) * DH] for s in range(t + 1)]))
        attention(units, ar(att, 5 * 512), 512)
        first_layer_end(i, lambda t: z[:, t, :], io["fox_w_out"][0], v, 0)
        return v, 0

    def ffn(i, tiles, nv, ready):
        HT = grid(ar(0, FT * NTOK * P), FT)
        sil = [ar(FT * NTOK * P + n * 512, 512) for n in range(2)]
        ranges = [(0, 512), (512, 256)] if len(tiles) == NTOK else [(0, 512)]
        Y = grid(FEAT_t[:, :], NTOK)
        wg, wu, wd = io["w_ffn_gate_2"][i], io["w_ffn_up_2"][i], io["w_ffn_down_2"][i]
        cnt = 0
        tok_s = [None, None]
        for n0 in range(0, DFF, NMAX):
            n = min(NMAX, DFF - n0)
            s1, w1, wt1 = load_weights(wg[:, n0:n0 + n], KT, n)
            s2, w2, wt2 = load_weights(wu[:, n0:n0 + n], KT, n)
            for m0 in range(0, n, P):
                for c0, c in ranges:
                    b1, ps1, bt1 = bank()
                    for k in range(KT):
                        tok1 = mm(ps1[:, 0:c], w1[:, k, m0:m0 + P], feat_cols(k, c0, c), k == 0, k == KT - 1,
                                  after=[ready, wt1, bt1] if k == 0 else (), count=k == KT - 1)
                    r = cnt % 2
                    cnt += 1
                    ta = act(sil[r][:, 0:c], ps1[:, 0:c], ACT.Silu, after=[tok1, tok_s[r], ready])
                    free(b1, ta)
                    b2, ps2, bt2 = bank()
                    for k in range(KT):
                        tok2 = mm(ps2[:, 0:c], w2[:, k, m0:m0 + P], feat_cols(k, c0, c), k == 0, k == KT - 1,
                                  after=[wt2, bt2] if k == 0 else (), count=k == KT - 1)
                    td = tt(HT[:, (n0 + m0) // P, c0:c0 + c], sil[r][:, 0:c], ps2[:, 0:c], ALU.mult, after=[ta, tok2])
                    tok_s[r] = td
                    free(b2, td)
            slot_readers[s1] = [tok1]
            slot_readers[s2] = [tok2]
        done = keep_y(Y)
        for n0 in range(0, D, NMAX):
            banks = [bank() for _ in tiles]
            for k0 in range(0, FT, KT):
                kn = min(KT, FT - k0)
                s, wv, wt = load_weights(wd[k0 * P:(k0 + kn) * P, n0:n0 + NMAX], kn, NMAX)
                for t, (b, ps, bt) in zip(tiles, banks):
                    for k in range(kn):
                        kk = k0 + k
                        tok = mm(ps, HT[:, kk, t * P:(t + 1) * P], wv[:, k, :], kk == 0, kk == FT - 1,
                                 after=[td, wt, bt] if k == 0 else (), count=k == kn - 1)
                    if kk == FT - 1:
                        free(b, *done(t, n0, NMAX, ps, [tok, tok2]))
                slot_readers[s] = [tok]
        return Y

    def rope(x1, x2, o1, o2, cs, sn, t1, t2, after):
        nh, h = x1.shape[1], x1.shape[2]
        c, s = rows_over(cs, nh), rows_over(sn, nh)
        tt(t1, x2, s, ALU.mult, after=after)
        tt(t2, x1, s, ALU.mult)
        tt(o1, x1, c, ALU.mult)
        tt(o1, o1, t1, ALU.subtract)
        tt(o2, x2, c, ALU.mult)
        return tt(o2, o2, t2, ALU.add)

    def even(ready):
        w = io["w_in_even_2"][0]
        O = grid(ar(0, NTOK * D), NTOK)
        H, NOPE, ROPE, DQK = 8, 64, 32, 96
        o0 = NTOK * D
        qd = grid(ar(o0, NTOK * 256), NTOK)
        kvd = grid(ar(o0 + 1536, NTOK * 160), NTOK)
        qnT, kvT = grid(ar(o0 + 2496, 1536), 2), ar(o0 + 4032, 768)
        qT = grid(ar(o0 + 4800, 3072), 4)
        kT = grid(ar(o0 + 7872, 3072), 4)
        vt = grid(ar(o0 + 10944, 1536), NTOK)
        cs, sn = grid(ar(o0 + 12480, 64), NLAT), grid(ar(o0 + 12544, 64), NLAT)
        ss = ar(o0 + 12608, 16)
        t1, t2 = ar(o0 + 12640, 64).rearrange("p (h d) -> p h d", d=16), \
            ar(o0 + 12704, 64).rearrange("p (h d) -> p h d", d=16)
        kpe = grid(ar(o0 + 12768, NTOK * 32), NTOK)
        qk_tok = [ar(o0 + 12960 + n * 384, 384) for n in range(2)]
        att = o0 + 13728
        g.dma("pool", "layer_params", cs, io["k_cos_mla"][:, :, :], after=ready)
        t_par = g.dma("pool", "layer_params", sn, io["k_sin_mla"][:, :, :], after=ready)

        def keep_down(t, n0, n, ps, tok):
            a = copy(qd[:, t, :], ps[:, 0:256], after=[tok])
            c = copy(kvd[:, t, :], ps[:, 256:416], after=[a], eng="act")
            return a, c

        linear_tok(feat_tile, KT, w[:, 2080:2496], 416, range(NTOK), keep_down, ready)
        for t in range(NTOK):
            act(junk_t[:, 0:256], qd[:, t, :], ACT.Square, accum=ss[:, t:t + 1], after=[g.last("dve")])
            a = act(junk_t[:, 0:128], kvd[:, t, 0:128], ACT.Square, accum=ss[:, 8 + t:9 + t])
        rstd_of(ss[:, 0:6], ss[:, 0:6], 256, after=[a])
        r = rstd_of(ss[:, 8:14], ss[:, 8:14], 128)
        for t in range(NTOK):
            ts(qd[:, t, :], qd[:, t, :], ss[:, t:t + 1], None, ALU.mult, after=[r])
            ts(kvd[:, t, 0:128], kvd[:, t, 0:128], ss[:, 8 + t:9 + t], None, ALU.mult)
            if t < NLAT:
                a1, a2 = kvd[:, t, 128:144].unsqueeze(1), kvd[:, t, 144:160].unsqueeze(1)
                tn = rope(a1, a2, kpe[:, t, 0:16].unsqueeze(1), kpe[:, t, 16:32].unsqueeze(1), cs[:, t, :],
                          sn[:, t, :], t1[:, 0:1, :], t2[:, 0:1, :], [t_par])
            else:
                tn = copy(kpe[:, t, :], kvd[:, t, 128:160])
            b, ps, bt = bank()
            turn(ps[:, 0:P], qd[:, t, 0:P], ident, after=[bt, tn])
            turn(ps[:, P:2 * P], qd[:, t, P:2 * P], ident)
            tok = turn(ps[:, 2 * P:3 * P], kvd[:, t, 0:P], ident, count=True)
            for m in range(2):
                act(qnT[:, m, t * P:(t + 1) * P], ps[:, m * P:(m + 1) * P], ACT.Copy, scale=pcol("mla_q_norm_2", m),
                    after=[tok])
            te = act(kvT[:, t * P:(t + 1) * P], ps[:, 2 * P:3 * P], ACT.Copy, scale=pcol("mla_kv_norm_2", 0))
            free(b, te)
        t_down = [te]
        for grp in range(2):
            rd = [[], []]

            def up_q(t, n0, n, ps, tok):
                r = t % 2
                qk = qk_tok[r].rearrange("p (h d) -> p h d", d=DQK)
                psv = ps.rearrange("p (h d) -> p h d", d=DQK)
                if t < NLAT:
                    a = act(qk, psv, ACT.Copy, scale=DQK ** -0.5, after=[tok, rd[r], g.last("dve")])
                    x1, x2 = qk[:, :, 64:80], qk[:, :, 80:96]
                    tt(t1, x2, rows_over(sn[:, t, :], 4), ALU.mult, after=[a, t_par])
                    tt(t2, x1, rows_over(sn[:, t, :], 4), ALU.mult)
                    tt(x1, x1, rows_over(cs[:, t, :], 4), ALU.mult)
                    tt(x1, x1, t1, ALU.subtract)
                    tt(x2, x2, rows_over(cs[:, t, :], 4), ALU.mult)
                    c = tt(x2, x2, t2, ALU.add)
                else:
                    a = c = act(qk, psv, ACT.Copy, scale=DQK ** -0.5, after=[tok, rd[r], g.last("dve")])
                b, p2, bt = bank()
                for h in range(4):
                    tk = turn(p2[0:DQK, h * P:(h + 1) * P], qk[:, h, :], ident, after=[bt, c], count=h == 3)
                rd[r] = [tk]
                te = copy(qT[0:DQK, :, t * P:(t + 1) * P], grid(p2[0:DQK, :], 4), after=[tk, g.last("pe")], eng="act")
                free(b, te)
                return (a,)

            def up_kv(t, n0, n, ps, tok):
                r = t % 2
                psv = ps.rearrange("p (h d) -> p h d", d=128)
                qk = qk_tok[r].rearrange("p (h d) -> p h d", d=DQK)
                a1 = copy(qk[:, :, 0:64], psv[:, :, 0:64], after=[tok, rd[r], g.last("act")])
                c = copy(qk[:, :, 64:96], rows_over(kpe[:, t, :], 4))
                a2 = copy(vt[:, t, :].rearrange("p (h d) -> p h d", d=64), psv[:, :, 64:128], after=[tok, a1], eng="act")
                b, p2, bt = bank()
                for h in range(4):
                    tk = turn(p2[0:DQK, h * P:(h + 1) * P], qk[:, h, :], ident, after=[bt, c], count=h == 3)
                rd[r] = [tk]
                te = copy(kT[0:DQK, :, t * P:(t + 1) * P], grid(p2[0:DQK, :], 4), after=[tk], eng="dve")
                free(b, te)
                return a1, a2

            src_q = lambda k, t: qnT[:, k, t * P:(t + 1) * P]
            src_k = lambda k, t: kvT[:, t * P:(t + 1) * P]
            prev = [t_down, g.last("pe"), g.last("act"), g.last("dve")]
            g.put("act", lambda e: e.activation(ss[:, 14:15], one_col, ACT.Copy), prev)
            g.put("dve", lambda e: e.tensor_copy(ss[:, 15:16], one_col), prev)
            linear_tok(src_q, 2, io["mla_w_q_up_2"][0][:, grp * 384:(grp + 1) * 384], 384, range(NTOK), up_q, prev)
            rd = [list(rd[0]), list(rd[1])]
            linear_tok(src_k, 1, io["mla_w_kv_up_2"][0][:, grp * 512:(grp + 1) * 512], 512, range(NTOK), up_kv, prev)
            t_up = [g.last("act"), g.last("dve"), g.last("pe")]
            units = []
            for t in range(NTOK):
                for h in range(4):
                    hh = grp * 4 + h

                    def done(ps, rinv, toks, t=t, hh=hh):
                        return ts(O[:, t, 512 + hh * 64:512 + hh * 64 + 64], ps, rinv, None, ALU.mult, after=toks)

                    q_ = qT[0:DQK, h, t * P:(t + 1) * P]
                    if t < NLAT:
                        sc = [(q_, kT[0:DQK, h, 0:512], 0, 512, True, True),
                              (q_, kT[0:DQK, h, 512:768], 512, 256, True, True)]
                        keys = range(NTOK)
                    else:
                        sc = [(q_, kT[0:DQK, h, 512:768], 0, 256, True, True)]
                        keys = CTX
                    units.append(dict(nk=len(keys) * P, ready=t_up, bias=None, dv=64, done=done, scores=sc,
                                      values=[vt[:, s, h * 64:(h + 1) * 64] for s in keys]))
            attention(units, ar(att, 4 * 768), 768)

        t_mla = [g.last("act"), g.last("dve"), g.last("pe")]
        QT, KTT = grid(ar(o0, 3072), 4), grid(ar(o0 + 3072, 3072), 4)
        ktok, vtok = grid(ar(o0 + 6144, 3072), NTOK), grid(ar(o0 + 9216, 3072), NTOK)
        c0_ = o0 + 12288
        PADW = 776
        raw = [ar(c0_ + n * PADW, PADW) for n in range(2)]
        acc, sqb = ar(c0_ + 2 * PADW, 768), ar(c0_ + 2 * PADW + 768, 768)
        onescol = ar(c0_ + 2 * PADW + 1536, P)
        g.memset(onescol, 0.0, after=t_mla)
        g.memset(onescol[0:64, 0:64], 1.0)
        t_ones = g.memset(onescol[64:128, 64:128], 1.0)
        t_rz = [g.memset(raw[n], 0.0) for n in range(2)]
        GA, BETA = grid(small(96), NTOK), grid(small(96), NTOK)
        dtb, nega = ar(c0_ + 3216, 16), ar(c0_ + 3232, 16)
        abt = grid(ar(c0_ + 3248, NTOK * 16), NTOK)
        onb = ar(c0_ + 3344, 64)
        g.dma("pool", "layer_params", dtb, io["gdn_dt_bias_2"][0].rearrange("a b -> (a b)").partition_broadcast(P),
              after=t_mla)
        t_par = g.dma("pool", "layer_params", nega, io["gdn_a_log_2"][0].rearrange("a b -> (a b)")
                      .partition_broadcast(P), after=t_mla)
        act(nega, nega, ACT.Exp, after=[t_par])
        gate_dram = nc.dram_tensor("gate_spill", [P, NTOK, 512], F32, kind="Internal")
        gate_sb = [raw[0][:, 0:512], raw[1][:, 0:512]]

        def keep_ab(t, n0, n, ps, tok):
            a = tt(GA[:, t, :], ps[:, 0:16], dtb, ALU.add, after=[tok, t_par])
            c = act(BETA[:, t, :], ps[:, 16:32], ACT.Sigmoid, after=[tok, a])
            return a, c

        linear_tok(feat_tile, KT, w[:, 2048:2080], 32, range(NTOK), keep_ab, ready)
        act(abt, GA, ACT.Abs, after=[g.last("dve")])
        act(abt, abt, ACT.Exp, scale=-1.0)
        tl = act(abt, abt, ACT.Ln, bias=one_col)
        stt(GA, GA, 0.0, abt, ALU.max, ALU.add, after=[tl])
        stt(GA, GA, -1.0, rows_over(nega, NTOK), ALU.mult, ALU.mult)
        gate_readers = [[], []]

        def keep_gate(t, n0, n, ps, tok):
            a = act(gate_sb[t % 2], ps, ACT.Silu, after=[tok, gate_readers[t % 2], t_rz])
            gate_readers[t % 2] = [g.dma("act", f"gate_out_{t % 2}", gate_dram[:, t, :], gate_sb[t % 2], after=[a])]
            return (a,)

        linear_tok(feat_tile, KT, w[:, 1536:2048], 512, range(NTOK), keep_gate, ready)
        t_gate = [list(x) for x in gate_readers]
        for n in range(2):
            g.memset(raw[n], 0.0, after=[gate_readers[n]])
        t_rz = g.last("dve")
        raw_readers = [[], []]
        spans = [(2, 0, 512), (518, 512, 256)]
        tail = []

        def conv_tail(m, ta):
            if m < 8:
                a = act(sqb, acc, ACT.Square, after=[ta, g.last("dve")])
                for c0, c in ((0, 512), (512, 256)):
                    b, ps, bt = bank()
                    tok = mm(ps[:, 0:c], onescol, sqb[:, c0:c0 + c], after=[bt, a, t_ones], count=True)
                    te = act(sqb[:, c0:c0 + c], ps[:, 0:c], ACT.Sqrt, bias=eps_col, after=[tok])
                    free(b, te)
                g.recip(sqb, sqb, after=[te])
                if m < 4:
                    return stt(QT[:, m, :], acc, 0.125, sqb, ALU.mult, ALU.mult)
                dst = KTT[:, m - 4, :]
                td = tt(dst, acc, sqb, ALU.mult)
                tokdst, mm_ = ktok, m - 4
            else:
                dst, td, tokdst, mm_ = acc, ta, vtok, m - 8
            for ts0, nt in ((0, 4), (4, 2)):
                b, ps, bt = bank()
                for t in range(nt):
                    tok = turn(ps[:, t * P:(t + 1) * P], dst[:, (ts0 + t) * P:(ts0 + t + 1) * P], ident,
                               after=[bt, td], count=t == nt - 1)
                te = copy(tokdst[:, ts0:ts0 + nt, mm_ * P:(mm_ + 1) * P],
                          grid(ps[:, 0:nt * P], nt), after=[tok], eng="act")
                free(b, te)
            return te

        state = {"acc": None}

        def keep_conv(m, c0, c, ps, tok):
            r = m % 2
            off = 2 if c0 == 0 else 518
            a = copy(raw[r][:, off:off + c], ps, after=[tok, raw_readers[r], t_rz], eng="act")
            if c0:
                for o, d0, n in spans:
                    for j in range(5):
                        src = raw[r][:, o - 2 + j:o - 2 + j + n]
                        wj = pcol("gdn_conv_2", j * 12 + m)
                        if j == 0:
                            ts(acc[:, d0:d0 + n], src, wj, None, ALU.mult, after=[a, g.last("pe"), g.last("act")])
                        else:
                            stt(acc[:, d0:d0 + n], src, wj, acc[:, d0:d0 + n], ALU.mult, ALU.add)
                raw_readers[r] = [g.last("dve")]
                ta = act(acc, acc, ACT.Silu, after=[g.last("dve")])
                conv_tail(m, ta)
            return (a,)

        linear_feat(feat_cols, KT, w[:, 0:1536], 1536, [(0, 512), (512, 256)], keep_conv, ready)
        t_conv = [g.last("act"), g.last("dve"), g.last("pe")]

        GC, EG, KD, BEG, GL = (grid(ar(c0_ + n * 96, 96), NTOK) for n in range(5))
        r0 = c0_ + 480
        ones = ar(r0, P)
        u_, wT, qdT, kd = (ar(r0 + 128 + n * 512, 512) for n in range(4))
        vb, kb = ar(r0 + 2176, 512), ar(r0 + 2688, 512)
        S2 = [ar(r0 + 3200 + n * 256, 256) for n in range(2)]
        Gh = ar(r0 + 3712, 24)
        DIF, DD, DU, XX, XT, VV = (FEAT_t[:, n * 1024:(n + 1) * 1024] for n in range(6))
        h8 = lambda ap: ap.rearrange("p (h n) -> p h n", h=8)
        g.memset(ones, 1.0, after=t_conv)
        b, ps, bt = bank()
        for t in range(NTOK):
            for d in range(2):
                tok = mm(ps[:, t * 16 + d * 8:t * 16 + d * 8 + 8], (TRI_U, TRI_L)[d], GA[:, t, d * 8:d * 8 + 8],
                         after=[bt, t_conv])
        tok = mm(ps[:, 96:192], ones, GA.rearrange("p t d -> p (t d)"), after=[g.last("dve")], count=True)
        f = lambda x: x.rearrange("p t d -> p (t d)")
        copy(f(GC), ps[:, 0:96], after=[tok])
        a = tt(f(KD), ps[:, 96:192], f(GC), ALU.subtract)
        act(f(EG), f(GC), ACT.Exp, after=[a])
        act(f(KD), f(KD), ACT.Exp)
        te = act(f(GL), ps[:, 96:192], ACT.Exp)
        free(b, te, a)
        tb = tt(f(BEG), f(BETA), f(EG), ALU.mult, after=[te])
        step_done = [None, None]
        started = [False, False]
        order = [(d, t) for pair in zip([4, 5, 0, 1, 2, 3], [5, 4, 3, 2, 1, 0]) for d, t in enumerate(pair)]
        seen = set()
        for d, t in order:
            lv, tri = (LEVEL_L, TRI_U) if d == 0 else (LEVEL_U, TRI_L)
            gs = slice(d * 8, d * 8 + 8)
            tile = slice(t * P, (t + 1) * P)
            for hb in range(2):
                b, ps, bt = bank()
                for h in range(4):
                    hh = hb * 4 + h
                    tok = mm(ps[:, h * P:(h + 1) * P],
                             GA[:, t, d * 8 + hh:d * 8 + hh + 1].broadcast_to((P, P)), tri,
                             after=[bt], count=h == 3)
                half = slice(hb * 512, (hb + 1) * 512)
                a = tt(grid(DIF[:, half], 4), grid(ps, 4), over(GC[:, t, d * 8 + hb * 4:d * 8 + hb * 4 + 4], P),
                       ALU.subtract, after=[tok, step_done])
                for par in range(2):
                    rows = slice(64 * par, 64 * par + 64)
                    src = grid(ps, 4)[rows, par::2, :]
                    c = act(grid(qdT, 4)[rows, hb * 2:hb * 2 + 2, :], src, ACT.Exp, after=[tok, a, step_done])
                free(b, a, c)
            tt(qdT.rearrange("p (m n) -> p m n", m=4), qdT.rearrange("p (m n) -> p m n", m=4), QT[:, :, tile],
               ALU.mult, after=[c])
            ts(DD, DIF, 0.0, None, ALU.min)
            a = ts(DU, DIF, 0.0, None, ALU.max)
            act(DD, DD, ACT.Exp, after=[a])
            td = act(DU, DU, ACT.Exp, scale=-1.0)
            for par in range(2):
                mine = lambda ap: h8(ap)[:, par::2, :]
                for which in range(2):
                    b, ps, bt = bank()
                    for h in range(4):
                        hh = 2 * h + par
                        rows = slice(64 * par, 64 * par + 64)
                        kk = KTT[rows, hh // 2, tile]
                        tok = mm(ps[:, h * P:(h + 1) * P], kk, (kk, QT[rows, hh // 2, tile])[which],
                                 after=[bt, t_conv], count=h == 3)
                    if which == 0:
                        tt(mine(DU), mine(DU), grid(ps, 4), ALU.mult, after=[tok, td])
                        a = tt(mine(DU), mine(DU), over(BETA[:, t, d * 8 + par:d * 8 + 8:2], P), ALU.mult)
                    else:
                        tt(mine(DD), mine(DD), grid(ps, 4), ALU.mult, after=[tok, td])
                        a = tt(mine(DD), mine(DD), rows_over(tri, 4), ALU.mult)
                    free(b, a)
            tM = a
            stt(h8(DIF), h8(DU), -1.0, rows_over(lv[0], 8), ALU.mult, ALU.mult)
            tx = tt(h8(XX), h8(DIF), rows_over(ident, 8), ALU.add)
            for hb in range(2):
                b, ps, bt = bank()
                for h in range(4):
                    at = slice((hb * 4 + h) * P, (hb * 4 + h + 1) * P)
                    tok = turn(ps[:, h * P:(h + 1) * P], XX[:, at], ident, after=[bt, tx], count=h == 3)
                txt = copy(XT[:, hb * 512:(hb + 1) * 512], ps, after=[tok], eng="act")
                free(b, txt)
            for level in range(1, LEVELS):
                tc = tt(h8(DIF), h8(DU), rows_over(lv[level], 8), ALU.mult, after=[tM, tx, g.last("pe")], eng="pool")
                tv = []
                for hb in range(2):
                    b, ps, bt = bank()
                    for h in range(4):
                        at = slice((hb * 4 + h) * P, (hb * 4 + h + 1) * P)
                        tok = mm(ps[:, h * P:(h + 1) * P], DIF[:, at], XT[:, at], after=[bt, tc, tx, txt],
                                 count=h == 3)
                    tv.append(copy(VV[:, hb * 512:(hb + 1) * 512], ps, after=[tok], eng="act"))
                    free(b, tv[-1])
                zz = []
                for hb in range(2):
                    for which in range(2 if level < LEVELS - 1 else 1):
                        b, ps, bt = bank()
                        for h in range(4):
                            at = slice((hb * 4 + h) * P, (hb * 4 + h + 1) * P)
                            l_, r_ = ((XX, VV), (VV, XX))[which]
                            tok = mm(ps[:, h * P:(h + 1) * P], l_[:, at], r_[:, at], after=[bt, tv[hb]], count=h == 3)
                        zz.append((hb, which, b, ps, tok))
                for hb, which, b, ps, tok in zz:
                    half = slice(hb * 512, (hb + 1) * 512)
                    dst = (XT, XX)[which]
                    tx = txt = tt(dst[:, half], dst[:, half], ps, ALU.subtract, after=[tok, zz[-1][4]])
                    free(b, tx)
            v3, k3 = grid(vtok[:, t, :], 8), grid(ktok[:, t, :], 8)
            tt(grid(vb, 8), v3, over(BETA[:, t, gs], 64), ALU.mult)
            tt(grid(kb, 8), k3, over(BEG[:, t, gs], 64), ALU.mult, after=[tb])
            tk = tt(grid(kd, 8), k3, over(KD[:, t, gs], 64), ALU.mult)
            b, ps, bt = bank()
            for h in range(8):
                at = slice(h * P, (h + 1) * P)
                tok = mm(ps[:, h * 64:(h + 1) * 64], XT[:, at], vb[:, h * 64:(h + 1) * 64], after=[bt, tk], count=h == 7)
            tu = copy(u_, ps, after=[tok], eng="act")
            free(b, tu)
            b, ps, bt = bank()
            for h in range(8):
                at = slice(h * P, (h + 1) * P)
                tok = mm(ps[64 * (h % 2):64 * (h % 2) + 64, (h // 2) * P:(h // 2 + 1) * P], kb[:, h * 64:(h + 1) * 64],
                         XT[:, at], after=[bt], count=h == 7)
            tw = copy(wT, ps, after=[tok], eng="act")
            free(b, tw)
            S = S2[d]
            rows = lambda h: slice(64 * (h % 2), 64 * (h % 2) + 64)
            if started[d]:
                for par in range(2):
                    b, ps, bt = bank()
                    for m in range(4):
                        tok = mm(ps[:, m * 64:(m + 1) * 64], wT[rows(par), m * P:(m + 1) * P],
                                 S[rows(par), m * 64:(m + 1) * 64], after=[bt, tw, step_done], count=m == 3)
                    mine = grid(u_, 8)[:, par::2, :]
                    tn = tt(mine, mine, grid(ps[:, 0:256], 4), ALU.subtract, after=[tok, tu])
                    free(b, tn)
            else:
                tn = tu
            for par in range(2):
                b, ps, bt = bank()
                for m in range(4):
                    h = 2 * m + par
                    if started[d]:
                        mm(ps[:, m * 64:(m + 1) * 64], qdT[rows(h), m * P:(m + 1) * P],
                           S[rows(h), m * 64:(m + 1) * 64], True, False, after=[bt, tn])
                    tok = mm(ps[:, m * 64:(m + 1) * 64], DD[:, h * P:(h + 1) * P], u_[:, h * 64:(h + 1) * 64],
                             not started[d], True, after=[bt, tn, tk], count=m == 3)
                dst, src = grid(O[:, t, 0:512], 8)[:, par::2, :], grid(ps[:, 0:256], 4)
                if t in seen:
                    a = tt(dst, dst, src, ALU.add, after=[tok])
                else:
                    a = copy(dst, src, after=[tok])
                free(b, a)
            seen.add(t)
            b, ps, bt = bank()
            for h in range(8):
                tok = mm(ps[rows(h), (h // 2) * 64:(h // 2 + 1) * 64], kd[:, h * 64:(h + 1) * 64],
                         u_[:, h * 64:(h + 1) * 64], after=[bt, tn], count=h == 7)
            if started[d]:
                for par in range(2):
                    copy(Gh[64 * par:64 * par + 64, 0:4], GL[64 * par:64 * par + 64, t, d * 8 + par:d * 8 + 8:2])
                tt(S.rearrange("p (m n) -> p m n", m=4), S.rearrange("p (m n) -> p m n", m=4), over(Gh[:, 0:4], 64),
                   ALU.mult, after=[tok])
                a = tt(S, S, ps[:, 0:256], ALU.add)
            else:
                a = copy(S, ps[:, 0:256], after=[tok])
            free(b, a)
            started[d] = True
            step_done = [a, tok, g.last("act")]
        GB = ar(o0, NTOK * 512).rearrange("p (t n) -> p t n", t=NTOK)
        onb = ar(o0 + 3072, 64)
        sq, ssg = ar(o0 + 3136, 512), ar(o0 + 3648, 8)
        g.dma("pool", "layer_params", onb, io["gdn_out_norm_2"][0].partition_broadcast(P), after=[step_done])
        t_par = g.dma("pool", "layer_params", GB, gate_dram[:, :, :], after=[step_done, t_gate])
        for t in range(NTOK):
            o_ = O[:, t, 0:512]
            head_rms(o_, 8, 64, o_, sq, ssg, [g.last("dve")])
            tt(grid(o_, 8), grid(o_, 8), rows_over(onb, 8), ALU.mult, after=[t_par])
            tt(o_, o_, GB[:, t, :], ALU.mult)
        return O

    def odd(ready):
        w = io["w_in_odd_2"][0]
        H, DH = 8, 64
        naq, nak = grid(ar(0, 2048), 4), grid(ar(2048, 3072), 4)
        nav = grid(ar(5120, 3072), NTOK)
        gq, gk = grid(ar(8192, 2048), 4), grid(ar(10240, 1536), 2)
        gv = grid(ar(11776, 768), NTOK)
        O = grid(ar(12544, 4096), NLAT)
        TB = ar(16640, 4 * 14 * 64)
        o1 = 16640 + 3584
        cs, sn = grid(ar(o1, 128), NLAT), grid(ar(o1 + 128, 128), NLAT)
        nam = ar(o1 + 256, 64)
        qg, kg = ar(o1 + 320, 64), ar(o1 + 384, 64)
        ss = ar(o1 + 448, 8)
        att = o1 + 456
        qn = [ar(att + n * 512, 512) for n in range(2)]
        sq = ar(att + 1024, 512)
        t1, t2 = ar(att + 1536, 256).rearrange("p (h d) -> p h d", d=32), \
            ar(att + 1792, 256).rearrange("p (h d) -> p h d", d=32)
        kn = [ar(att + 2048 + n * 256, 256) for n in range(2)]
        kt_ = ar(att + 2560, 128)
        g.dma("pool", "layer_params", cs, io["k_cos_gqa"][:, :, :], after=ready)
        g.dma("pool", "layer_params", sn, io["k_sin_gqa"][:, :, :], after=ready)
        g.dma("pool", "layer_params", nam, io["k_window"][:, :], after=ready)
        g.dma("pool", "layer_params", qg, io["gqa_q_norm_2"][0].partition_broadcast(P), after=ready)
        t_par = g.dma("pool", "layer_params", kg, io["gqa_k_norm_2"][0].partition_broadcast(P), after=ready)
        W = 127
        rp = ar(att + 2688, W)
        tz = g.memset(rp[0:120, :], 0.0, after=ready)
        t_rp = g.dma("pool", "rpb_in", rp[0:120, 48:79], io["na_rpb_2"][0].rearrange("h r c -> (h r) c"), after=[tz])
        skew = nc.dram_tensor("rpb_rows", [8 * 15, 64, W], F32, kind="Internal")
        t_sk = g.dma("pool", "rpb_out", skew[:, :, :], rp[0:120, :].unsqueeze(1).broadcast_to((120, 64, W)),
                     after=[t_rp])

        def read_bias(grp, after):
            for par in range(2):
                for h in range(4):
                    src = bass.AP(tensor=skew.ap().tensor if hasattr(skew, "ap") else skew,
                                  offset=((grp * 4 + h) * 15 + 1 - par) * 64 * W + 63,
                                  ap=[[W - 1, 64], [64 * W, 14], [1, 64]])
                    dst = TB[64 * par:64 * par + 64, h * 896:(h + 1) * 896].rearrange("p (r c) -> p r c", r=14)
                    tok = g.dma("pool", "bias_in", dst, src, after=[t_sk, after])
            tv = TB.rearrange("p (n c) -> p n c", c=64)
            return tt(tv, tv, rows_over(nam, 56), ALU.add, after=[tok, t_par])

        def keep_feat(dst, scale):
            def done(m, c0, c, ps, tok):
                if scale != 1.0:
                    return (act(dst[:, m, c0:c0 + c], ps, ACT.Copy, scale=scale, after=[tok]),)
                return (copy(dst[:, m, c0:c0 + c], ps, after=[tok], eng=evac_engine()),)
            return done

        all_ = [(0, 512), (512, 256)]
        linear_feat(feat_cols, KT, w[:, 0:512], 512, [(0, 512)], keep_feat(naq, DH ** -0.5), ready)
        linear_feat(feat_cols, KT, w[:, 512:1024], 512, all_, keep_feat(nak, 1.0), ready)
        linear_tok(feat_tile, KT, w[:, 1024:1536], 512, range(NTOK),
                   lambda t, n0, n, ps, tok: (copy(nav[:, t, :], ps, after=[tok], eng=evac_engine()),), ready)
        rd = [[], []]
        pending = []

        def rot(x, nh, t, c):
            a1, a2 = x[:, :, 0:32], x[:, :, 32:64]
            tt(t1[:, 0:nh, :], a2, rows_over(sn[:, t, :], nh), ALU.mult, after=[c, t_par])
            tt(t2[:, 0:nh, :], a1, rows_over(sn[:, t, :], nh), ALU.mult)
            tt(a1, a1, rows_over(cs[:, t, :], nh), ALU.mult)
            tt(a1, a1, t1[:, 0:nh, :], ALU.subtract)
            tt(a2, a2, rows_over(cs[:, t, :], nh), ALU.mult)
            return tt(a2, a2, t2[:, 0:nh, :], ALU.add)

        def turn_q(t, r, c):
            b, ps, bt = bank()
            for m in range(4):
                tk = turn(ps[:, m * P:(m + 1) * P], qn[r][:, m * P:(m + 1) * P], ident, after=[bt, c], count=m == 3)
            rd[r] = [tk]
            te = act(gq[:, :, t * P:(t + 1) * P], grid(ps, 4), ACT.Copy, scale=DH ** -0.5, after=[tk])
            free(b, te)

        def keep_gq(t, n0, n, ps, tok):
            r = t % 2
            a, c = head_rms(ps, 8, DH, qn[r], sq, ss, [tok, rd[r], g.last("dve")])
            x = grid(qn[r], 8)
            tt(x, x, rows_over(qg, 8), ALU.mult, after=[t_par])
            pending.append((t, r, rot(x, 8, t, c)))
            if len(pending) > 1:
                turn_q(*pending.pop(0))
            return a, c

        linear_tok(feat_tile, KT, w[:, 1536:2048], 512, LAT, keep_gq, ready)
        while pending:
            turn_q(*pending.pop(0))
        rk = [[], []]

        def turn_k(t, r, c):
            b, ps, bt = bank()
            for m in range(2):
                tk = turn(ps[:, m * P:(m + 1) * P], kn[r][:, m * P:(m + 1) * P], ident, after=[bt, c], count=m == 1)
            rk[r] = [tk]
            te = copy(gk[:, :, t * P:(t + 1) * P], grid(ps[:, 0:256], 2), after=[tk], eng="act")
            free(b, te)

        def keep_gkv(t, n0, n, ps, tok):
            r = t % 2
            a2 = copy(gv[:, t, :], ps[:, 128:256], after=[tok], eng="act")
            a, c = head_rms(ps[:, 0:128], 2, DH, kt_, sq[:, 0:128], ss[:, 0:2], [tok, g.last("dve")])
            x = grid(kt_, 2)
            c = tt(x, x, rows_over(kg, 2), ALU.mult, after=[t_par])
            if t < NLAT:
                c = rot(x, 2, t, c)
            k4 = kn[r].rearrange("p (h c d) -> p h c d", h=2, c=2)
            copy(k4[:, :, 0, :], x, after=[rk[r]])
            c = copy(k4[:, :, 1, :], x)
            pending.append((t, r, c))
            if len(pending) > 1:
                turn_k(*pending.pop(0))
            return a, a2, c

        linear_tok(feat_tile, KT, w[:, 2048:2304], 256, range(NTOK), keep_gkv, ready)
        while pending:
            turn_k(*pending.pop(0))
        t_in = [g.last("act"), g.last("dve"), g.last("pe"), t_sk]
        for grp in range(2):
            t_b = read_bias(grp, [g.last("dve")] if grp == 0 else [t_in])
            units = []
            for t in LAT:
                for h in range(4):
                    hh = grp * 4 + h
                    rows = slice(64 * (hh % 2), 64 * (hh % 2) + 64)

                    def bias(src, dst, tok, t=t, h=h):
                        a0 = h * 896 + (7 - 2 * t - 1) * 64
                        tt(dst[:, 0:512], src[:, 0:512], TB[:, a0:a0 + 512], ALU.add, after=[tok, g.last("act")])
                        return copy(dst[:, 512:768], src[:, 512:768], after=[tok], eng="dve")

                    def done(ps, rinv, toks, t=t, hh=hh):
                        return ts(O[:, t, hh * 64:hh * 64 + 64], ps, rinv, None, ALU.mult, after=toks)

                    q_ = naq[rows, hh // 2, t * P:(t + 1) * P]
                    units.append(dict(nk=768, ready=[t_in, t_b], bias=bias, dv=64, done=done,
                                      scores=[(q_, nak[rows, hh // 2, 0:512], 0, 512, True, True),
                                              (q_, nak[rows, hh // 2, 512:768], 512, 256, True, True)],
                                      values=[nav[:, s, hh * 64:(hh + 1) * 64] for s in range(NTOK)]))
            attention(units, FEAT_t[:, 0:5 * 768], 768)
            t_in = [g.last("act"), g.last("dve"), g.last("pe")]
        units = []
        for t in LAT:
            for hh in range(8):
                rows = slice(64 * (hh % 2), 64 * (hh % 2) + 64)
                kv = hh // 4

                def done(ps, rinv, toks, t=t, hh=hh):
                    return ts(O[:, t, 512 + hh * 64:512 + hh * 64 + 64], ps, rinv, None, ALU.mult, after=toks)

                q_ = gq[rows, hh // 2, t * P:(t + 1) * P]
                units.append(dict(nk=768, ready=t_in, bias=None, dv=64, done=done,
                                  scores=[(q_, gk[rows, kv, 0:512], 0, 512, True, True),
                                          (q_, gk[rows, kv, 512:768], 512, 256, True, True)],
                                  values=[gv[:, s, kv * 64:(kv + 1) * 64] for s in range(NTOK)]))
        attention(units, FEAT_t[:, 0:5 * 768], 768)
        return O

    def cond1(k):
        return COND[:, k:k + 1]

    def c2(k):
        return cond2[:, k, :]

    finish = lambda: [g.last("dve")]

    def mod_first(i):
        return modulation(io["w_mod"][i], "b_mod", i * 24, cond1, 1, 3072)

    def mod_second(i):
        return modulation(io["w_mod_2"][i], "b_mod_2", i * 48, c2, 2, 6144)

    t_mod = mod_first(0)
    for i in range(4):
        if stop <= i:
            break
        ready = prenorm(LAT, 0, "norm_pre_g", i * KT, (0, 1), 1, t_mod)
        if i % 3 == 0:
            Y, gb = gla(i, i // 3, ready)
        elif i == 1:
            Y, gb = sgu(i, ready)
        else:
            Y, gb = fox(i, ready)
        if i < 3:
            t_mod = mod_first(i + 1)
        else:
            t_mod = mod_second(0)
        post(LAT, Y, [gb, gb])
    for i in range(2):
        if stop <= 4 + i:
            break
        both = list(range(NTOK)) if i == 0 else LAT
        ready = prenorm(list(range(NTOK)), 0, "g_pre_mix_2", i * KT, (0, 1), 2, t_mod)
        O = even(ready) if i == 0 else odd(ready)
        tf = to_feat(lambda t: O[:, t, :], both, [g.last("act"), g.last("dve"), g.last("pe")])
        gb = [14000, 15024]
        done_all = [g.last("dve"), g.last("pe"), g.last("act")]
        post_begin(0, "g_post_mix_2", i * KT, 2, 2, gb[0], done_all + [tf])
        if i == 0:
            post_begin(1, "g_post_mix_2", i * KT, 2, 2, gb[1], done_all)
        Yv = grid(ar(7000, NTOK * D), NTOK)
        linear_tok(feat_tile, KT, io["w_out_even_2" if i == 0 else "w_out_odd_2"][0], D, both, keep_y(Yv), [tf])
        post(both, Yv, gb)
        ready = prenorm(both, 0, "g_pre_ffn_2", i * KT, (3, 4), 2, [])
        Yf = ffn(i, both, 2, ready)
        gb = [FT * NTOK * P + 1024, FT * NTOK * P + 2048]
        post_begin(0, "g_post_ffn_2", i * KT, 5, 2, gb[0], [g.last("dve")])
        if i == 0:
            post_begin(1, "g_post_ffn_2", i * KT, 5, 2, gb[1], [g.last("dve")])
            t_mod = mod_second(1)
        post(both, Yf, gb)

    t_out = g.dma("sp", "x_out", out.rearrange("a (t p) d -> p (a t) d", p=P), X, after=[g.last("dve"), t_x])
    g.put("sp", lambda e: e.wait_ge(g.names["x_out"], 16), [], count=False)

    block = stack.enter_context(nc.Block())
    for name, deco in (("sp", block.sync), ("pe", block.tensor), ("act", block.scalar), ("dve", block.vector),
                       ("pool", block.gpsimd)):
        def run(eng, name=name):
            for f in g.queue[name]:
                f(eng)
        deco(run)


def constants():
    i = np.arange(P)
    r, c = i[:, None], i[None, :]
    up = []
    for lv in range(LEVELS):
        s = 1 << lv
        up.append(((r // (2 * s) == c // (2 * s)) & ((r // s) % 2 == 0) & ((c // s) % 2 == 1)))
    mats = [r == c, r <= c, r >= c] + up + [m.T for m in up]
    const = np.concatenate([m.astype(np.float32) for m in mats], 1)
    reset = np.broadcast_to((np.arange(512) % P != 0).astype(np.float32), (P, 512))
    neg = np.where(c > r, np.float32(-1e30), np.float32(0))
    col, kc = (i % 64)[:, None], np.arange(64)[None, :]
    st = np.clip(col - 8, 0, 48)
    window = np.where((kc >= st) & (kc < st + 16), np.float32(0), np.float32(-1e30))

    def rope_tables(dim):
        t = np.arange(512)
        nf = dim // 4
        inv = (np.float32(10000.0) ** (-np.arange(nf, dtype=np.float32) / np.float32(nf))).astype(np.float32)
        ang = np.concatenate([(t // 64).astype(np.float32)[:, None] * inv, (t % 64).astype(np.float32)[:, None] * inv], 1)
        f = lambda a: np.ascontiguousarray(a.astype(np.float32).reshape(4, P, dim // 2).transpose(1, 0, 2))
        return f(np.cos(ang)), f(np.sin(ang))

    cm, sm = rope_tables(32)
    cg, sg = rope_tables(64)
    out = {"k_const": const, "k_reset": reset, "k_neg": neg, "k_window": window, "k_cos_mla": cm, "k_sin_mla": sm,
           "k_cos_gqa": cg, "k_sin_gqa": sg}
    return {k: np.ascontiguousarray(v, dtype=np.float32) for k, v in out.items()}


STOP = 99


def kernel(**inputs):
    import numpy as _np
    import concourse.bacc as _bacc
    from concourse import mybir as _mybir
    from concourse.bass_utils import run_bass_kernel_spmd as _run

    nc = _bacc.Bacc("TRN2", target_bir_lowering=False, num_devices=1)
    arrays, io = {}, {}
    for name, a in list(inputs.items()) + list(constants().items()):
        a = _np.ascontiguousarray(a)
        arrays[f"in_{name}"] = a
        io[name] = nc.dram_tensor(f"in_{name}", a.shape, _mybir.dt.from_np(a.dtype), kind="ExternalInput").ap()
    out = nc.dram_tensor("out_x", (1, 512, D), F32, kind="ExternalOutput").ap()
    build(nc, io, out, STOP)
    r = _run(nc, [arrays], core_ids=[0])
    return r.results[0]["out_x"]
```

```python
import numpy as np
import concourse.bass as bass
import concourse.mybir as mybir
from concourse.alu_op_type import AluOpType as ALU

F32 = mybir.dt.float32
F32R = mybir.dt.float32r
U32 = mybir.dt.uint32
ACT = mybir.ActivationFunctionType
AX = mybir.AxisListType

P = 128
D = 1024
KT = D // P
NLAT, NCTX = 4, 2
NTOK = NLAT + NCTX
NMAX = 512
EPS = 1e-6
LEVELS = 7
DFF = 2816
FT = DFF // P
LAT, CTX = list(range(NLAT)), list(range(NLAT, NTOK))

RING = 4
HALF = KT * NMAX // 2
SLOT = 2 * HALF
FEATS = KT * NTOK * P
ARENA = 13280


class Program:

    ENGINES = ("pe", "act", "dve", "pool", "sp")

    def __init__(self, nc, stack):
        self.nc = nc
        self.queue = {e: [] for e in self.ENGINES}
        self.sem = {e: stack.enter_context(nc.semaphore("done_" + e)) for e in self.ENGINES}
        self.count = {e: 0 for e in self.ENGINES}
        self.waited = {e: {} for e in self.ENGINES}
        self.stack = stack
        self.names = {}

    def last(self, engine):
        return (engine, self.count[engine])

    def put(self, engine, fn, after=(), count=True):
        need = {}
        todo = list(after)
        while todo:
            x = todo.pop()
            if x is None:
                continue
            if isinstance(x, list):
                todo.extend(x)
                continue
            if x[1] > 0:
                need[x[0]] = max(need.get(x[0], 0), x[1])
        seen = self.waited[engine]
        for name, value in need.items():
            if seen.get(name, 0) < value:
                seen[name] = value
                sem = self.sem[name] if name in self.sem else self.names[name]
                self.queue[engine].append(lambda e, s=sem, v=value: e.wait_ge(s, v))
        if count:
            self.count[engine] += 1
            self.queue[engine].append(lambda e, f=fn, s=self.sem[engine]: f(e).then_inc(s, 1))
            return (engine, self.count[engine])
        self.queue[engine].append(lambda e, f=fn: f(e))
        return None

    def dma(self, engine, stream, out, in_, after=()):
        if stream not in self.names:
            self.names[stream] = self.stack.enter_context(self.nc.semaphore(stream))
            self.count[stream] = 0
        self.put(engine, lambda e, s=self.names[stream]: e.dma_start(out, in_).then_inc(s, 16), after, count=False)
        self.count[stream] += 16
        return (stream, self.count[stream])

    def mm(self, out, lhsT, rhs, start=True, stop=True, after=(), count=False):
        return self.put("pe", lambda e: e.matmul(out, lhsT, rhs, start=start, stop=stop), after, count)

    def turn(self, out, in_, ident, after=(), count=False):
        return self.put("pe", lambda e: e.transpose(out, in_, ident), after, count)

    def act(self, out, in_, func, after=(), bias=0.0, scale=1.0, accum=None):
        kw = {} if accum is None else {"accum_out": accum}
        return self.put("act", lambda e: e.activation(out, in_, func, bias=bias, scale=scale, **kw),
                        [self.last("act"), list(after)])

    def tt(self, out, a, b, op, after=(), eng="dve"):
        return self.put(eng, lambda e: e.tensor_tensor(out, a, b, op), [self.last(eng), list(after)])

    def ts(self, out, a, s1, s2, op0, op1=None, after=(), eng="dve"):
        if op1 is None:
            return self.put(eng, lambda e: e.tensor_scalar(out, a, s1, None, op0), [self.last(eng), list(after)])
        return self.put(eng, lambda e: e.tensor_scalar(out, a, s1, s2, op0, op1), [self.last(eng), list(after)])

    def stt(self, out, a, s, b, op0, op1, after=()):
        return self.put("dve", lambda e: e.scalar_tensor_tensor(out, a, s, b, op0, op1),
                        [self.last("dve"), list(after)])

    def copy(self, out, a, after=(), eng="dve"):
        if eng == "act":
            return self.act(out, a, ACT.Copy, after)
        return self.put(eng, lambda e: e.tensor_copy(out, a), [self.last(eng), list(after)])

    def recip(self, out, a, after=()):
        return self.put("dve", lambda e: e.reciprocal(out, a), [self.last("dve"), list(after)])

    def reduce(self, out, a, op, after=(), negate=False):
        return self.put("dve", lambda e: e.tensor_reduce(out, a, AX.X, op, negate=negate),
                        [self.last("dve"), list(after)])

    def memset(self, out, value, after=(), eng="dve"):
        return self.put(eng, lambda e: e.memset(out, value), [self.last(eng), list(after)])


def grid(ap, a):
    return ap.rearrange("p (a b) -> p a b", a=a)


def over(ap, n):
    p, m = ap.shape
    return ap.unsqueeze(2).broadcast_to((p, m, n))


def rows_over(ap, n):
    p, m = ap.shape
    return ap.unsqueeze(1).broadcast_to((p, n, m))


def build(nc, io, out, stop=99):
    from contextlib import ExitStack
    stack = ExitStack()
    with stack:
        program(nc, stack, io, out, stop)


def program(nc, stack, io, out, stop):
    g = Program(nc, stack)
    mm, turn, act, tt, ts, stt, copy = g.mm, g.turn, g.act, g.tt, g.ts, g.stt, g.copy

    def sb(name, n):
        return stack.enter_context(nc.sbuf_tensor(name, [P, n], F32))

    def two_names(name, n):
        at = -(-nc.sbuf_base // 32) * 32
        plain = sb(name, n)
        assert nc.sbuf_base == at + 4 * n
        rounded = nc.alloc_sbuf_tensor_at(name + "_r", [P, n], F32R, offset=at)
        return plain, rounded

    X = grid(sb("x_lat", NLAT * D)[:, :], NLAT)
    HC_t = sb("x_ctx", NCTX * D)
    HC = grid(HC_t[:, :], NCTX)
    FEAT_t, FEAT_r = two_names("feat", 2 * FEATS)
    FH, FL = grid(FEAT_r[:, 0:FEATS], KT), grid(FEAT_r[:, FEATS:2 * FEATS], KT)
    WEI_t, WEI_r = two_names("weights", RING * SLOT)
    AR, AR_r = two_names("arena", ARENA)
    CONST = sb("const", 3 * P + 2 * LEVELS * P + 2)
    PCOL = sb("param_cols", 3 * P + 96)
    MODC = sb("mod_cols", 96)
    SM_t = sb("small", 276)
    COND = sb("cond", 2 * KT * 32)
    ROW_t = sb("rows", 2 * NMAX)
    PS_t = stack.enter_context(nc.psum_tensor("psum", [P, 8 * NMAX], F32))
    row_readers = [[], []]
    n_rows = [0]

    ident, TRI_U, TRI_L = (CONST[:, i * P:(i + 1) * P] for i in range(3))
    LEVEL_U = [CONST[:, (3 + i) * P:(4 + i) * P] for i in range(LEVELS)]
    LEVEL_L = [CONST[:, (3 + LEVELS + i) * P:(4 + LEVELS + i) * P] for i in range(LEVELS)]
    FOLD = CONST[:, (3 + 2 * LEVELS) * P:(3 + 2 * LEVELS) * P + 2]

    def ar(off, n):
        assert off + n <= ARENA, (off, n)
        return AR[:, off:off + n]

    def resid(t):
        return X[:, t, :] if t < NLAT else HC[:, t - NLAT, :]

    free_banks = [(i, []) for i in range(8)]

    def bank():
        i, toks = free_banks.pop(0)
        return i, PS_t[:, i * NMAX:(i + 1) * NMAX], toks

    def bank_pair():
        for i, _ in list(free_banks):
            if i % 2 == 0 and any(j == i + 1 for j, _ in free_banks):
                a = next(x for x in free_banks if x[0] == i)
                b = next(x for x in free_banks if x[0] == i + 1)
                free_banks.remove(a)
                free_banks.remove(b)
                return i, PS_t[:, i * NMAX:(i + 2) * NMAX], a[1] + b[1]
        raise AssertionError("no pair of banks")

    def free(i, *toks, n=1):
        for j in range(n):
            free_banks.append((i + j, list(toks)))

    flip = [0]

    def evac_engine():
        flip[0] ^= 1
        return "act" if flip[0] else "dve"

    plan = weight_plan(io)
    slot_readers = [[] for _ in range(RING)]
    taken = [0]
    next_slot = [0]
    ahead = []

    def start_chunk():
        name, index, k0, kt, n0, n, split = plan[len(started_chunks)]
        started_chunks.append(name)
        src = io[name][index] if index is not None else io[name]
        src = src[k0 * P:(k0 + kt) * P, n0:n0 + n].rearrange("(k p) n -> p k n", p=P)
        parts = []
        step = HALF // NMAX if split else kt
        for q0 in range(0, kt, step):
            q = min(step, kt - q0)
            s = next_slot[0] % RING
            next_slot[0] += 1
            size = q * n
            raw = WEI_t[:, s * SLOT:s * SLOT + size]
            tok = g.dma("sp", f"weights_{s}", raw.rearrange("p (k n) -> p k n", k=q), src[:, q0:q0 + q, :],
                        after=slot_readers[s])
            if not split:
                parts.append((s, q0, q, grid(raw, q), None, [tok]))
                continue
            hi = WEI_r[:, s * SLOT + HALF:s * SLOT + HALF + size]
            lo = WEI_r[:, s * SLOT:s * SLOT + size]
            th = act(hi, raw, ACT.Copy, after=[tok])
            tl = tt(lo, raw, hi.bitcast(F32), ALU.subtract, after=[th])
            parts.append((s, q0, q, grid(hi, q), grid(lo, q), [th, tl]))
        ahead.append(parts)

    started_chunks = []

    def take_weights(name, k0, kt, n0, n):
        assert plan[taken[0]][0] == name and plan[taken[0]][2:6] == (k0, kt, n0, n), (plan[taken[0]], name, k0, kt, n0, n)
        taken[0] += 1
        if not ahead:
            start_chunk()
        if len(started_chunks) < len(plan):
            start_chunk()
        parts = ahead.pop(0)
        where = {}
        for s, q0, q, hi, lo, toks in parts:
            for k in range(q):
                where[q0 + k] = (hi[:, k, :], lo[:, k, :] if lo is not None else None, toks)

        def release(tok):
            for p_ in parts:
                slot_readers[p_[0]] = [tok]

        return where, release

    def product(ps, terms, first, last, after=()):
        for i, ((lh, ll), (rh, rl), toks) in enumerate(terms):
            a, z = first and i == 0, last and i == len(terms) - 1
            wait = [toks, after if i == 0 else None]
            if ll is None:
                tok = mm(ps, lh, rh, a, z, after=wait, count=i == len(terms) - 1)
            else:
                mm(ps, lh, rh, a, False, after=wait)
                mm(ps, lh, rl, False, False)
                tok = mm(ps, ll, rh, False, z, count=i == len(terms) - 1)
        return tok

    def linear_tok(src, nk, name, c0, ncols, tiles, done, ready, k0=0):
        for n0 in range(0, ncols, NMAX):
            n = min(NMAX, ncols - n0)
            where, release = take_weights(name, k0, nk, c0 + n0, n)
            for t in tiles:
                b, ps, bt = bank()
                tok = product(ps[:, 0:n], [(src(k, t), where[k][0:2], where[k][2]) for k in range(nk)], True, True,
                              after=[ready, bt])
                free(b, *done(t, n0, n, ps[:, 0:n], tok))
            release(tok)

    def linear_feat(name, c0w, ncols, ranges, done, ready):
        for n0 in range(0, ncols, NMAX):
            n = min(NMAX, ncols - n0)
            where, release = take_weights(name, 0, KT, c0w + n0, n)
            for m0 in range(0, n, P):
                m = min(P, n - m0)
                for c0, c in ranges:
                    b, ps, bt = bank()
                    tok = product(ps[0:m, 0:c], [((where[k][0][:, m0:m0 + m], where[k][1][:, m0:m0 + m]),
                                                  feat_cols(k, c0, c), where[k][2]) for k in range(KT)], True, True,
                                  after=[ready, bt])
                    free(b, *done((n0 + m0) // P, c0, c, ps[0:m, 0:c], tok))
            release(tok)

    feat_tile = lambda k, t: (FH[:, k, t * P:(t + 1) * P], FL[:, k, t * P:(t + 1) * P])
    feat_cols = lambda k, c0, c: (FH[:, k, c0:c0 + c], FL[:, k, c0:c0 + c])

    def split_feat(evac, hi, lo, shape):
        i = n_rows[0] % 2
        n_rows[0] += 1
        n = shape[0] * shape[1]
        v = ROW_t[:, i * NMAX:i * NMAX + n]
        tv = evac(v, row_readers[i])
        v3 = grid(v, shape[0]) if shape[0] > 1 else v
        copy(hi, v3, after=[tv])
        tok = tt(lo, v3, hi.bitcast(F32), ALU.subtract)
        row_readers[i] = [tok]
        return tv, tok

    t_const = g.dma("sp", "const_in", CONST[:, :], io["k_const"][:, :])
    t_x = g.dma("act", "x_in", X, io["x"].rearrange("a (t p) d -> p (a t) d", p=P))
    ctx_in = []

    col_of = {}
    prow = grid(ar(0, 4 * P), 4)

    def as_rows(ap, k):
        return ap.rearrange(k, b=P) if "b" in k else ap

    groups = [
        [("norm_pre_g", "l (a b) -> (l a) b", 32), ("norm_post_g", "l (a b) -> (l a) b", 32),
         ("g_pre_mix_2", "l (a b) -> (l a) b", 16), ("g_post_mix_2", "l (a b) -> (l a) b", 16),
         ("g_pre_ffn_2", "l (a b) -> (l a) b", 16), ("g_post_ffn_2", "l (a b) -> (l a) b", 16)],
        [("c", "l (a b) -> (l a) b", 8), ("c_2", "l (a b) -> (l a) b", 8), ("c_ctx_2", "(a b) -> a b", 8),
         ("gla_b_a", "l (a b) -> (l a) b", 8), ("gdn_conv_2", "l t (a b) -> (l t a) b", 60),
         ("mla_q_norm_2", "l (a b) -> (l a) b", 2), ("mla_kv_norm_2", "l (a b) -> (l a) b", 1),
         ("sgu_b_s", "l a b -> (l a) b", 4)],
        [("b_mod", "l (a b) -> (l a) b", 96)],
        [("b_mod_2", "l (a b) -> (l a) b", 96)],
    ]
    t_pc = []
    for q, group in enumerate(groups):
        r = 0
        for name, how, n in group:
            t_row = g.dma("act", f"params_{q}", prow[r:r + n, q, :], as_rows(io[name], how))
            col_of[name] = (q, r)
            r += n
        b, ps, bt = bank()
        tok = turn(ps[:, 0:r], prow[0:r, q, :], ident[0:r, 0:r], after=[t_row, t_const, bt], count=True)
        t_pc.append(copy(PCOL[:, q * P:q * P + r], ps[:, 0:r], after=[tok]))
        free(b, t_pc[-1])

    def pcol(name, i, n=1):
        q, r = col_of[name]
        return PCOL[:, q * P + r + i:q * P + r + i + n]

    small_used = [0]

    def small(n):
        a = small_used[0]
        small_used[0] += n
        assert small_used[0] <= 276, small_used
        return SM_t[:, a:a + n]

    eps_col = small(1)
    one_col = small(1)
    g.memset(eps_col, EPS)
    g.memset(one_col, 1.0)
    cond1, cond2 = (COND[:, i * 256:(i + 1) * 256].rearrange("p (k v) -> p k v", v=32) for i in range(2))
    tz = g.memset(COND[:, :], 0.0)
    act(cond1[:, :, 0], pcol("c", 0, 8), ACT.Silu, after=[t_pc, tz])
    act(cond2[:, :, 0], pcol("c_2", 0, 8), ACT.Silu)
    t_cond = act(cond2[:, :, 1], pcol("c_ctx_2", 0, 8), ACT.Silu)

    def modulation(name, index, bias_name, bias_at, cond, nv, ncols):
        toks = []
        mod_free = g.last("dve")
        for n0 in range(0, ncols, NMAX):
            where, release = take_weights(name, 0, KT, n0, NMAX)
            b, ps, bt = bank()
            for k in range(KT):
                j = k % 4
                tok = mm(ps[32 * j:32 * j + 32, :], cond[:, k, :], where[k][0], k < 4, k >= 4,
                         after=[where[k][2], bt, t_cond] if k == 0 else (), count=k == KT - 1)
            release(tok)
            i = n_rows[0] % 2
            n_rows[0] += 1
            row = ROW_t[:, i * NMAX:(i + 1) * NMAX]
            tr = copy(row, ps, after=[tok, row_readers[i]], eng="act")
            free(b, tr)
            b, ps, bt = bank()
            for m in range(4):
                tok = mm(ps[:, m * nv:(m + 1) * nv], row[:, m * P:(m + 1) * P], FOLD[:, 0:nv],
                         after=[tr, bt, t_const], count=m == 3)
            row_readers[i] = [tok]
            m0 = n0 // P
            tc = tt(MODC[:, m0 * nv:(m0 + 4) * nv].rearrange("p (m v) -> p m v", v=nv),
                    ps[:, 0:4 * nv].rearrange("p (m v) -> p m v", v=nv),
                    over(pcol(bias_name, bias_at + m0, 4), nv), ALU.add, after=[tok, mod_free])
            free(b, tc)
            toks = [tc]
        return toks

    def modc(part, v, nv):
        return MODC[:, 0:48 * nv].rearrange("p (m v) -> p m v", v=nv)[:, part * KT:(part + 1) * KT, v] if nv > 1 \
            else MODC[:, part * KT:(part + 1) * KT]

    SSQ = small(12)
    RSTD = small(12)
    PRE_A = small(16)
    PRE_B = small(16)
    GATE = small(16)
    junk_t = sb("junk", NMAX)

    def rstd_of(out, ss, n, after=()):
        a = act(out, ss, ACT.Sqrt, bias=eps_col[0:out.shape[0], :], scale=1.0 / n, after=after)
        return g.recip(out, out, after=[a])

    def prenorm(tiles, xn_off, g_name, g_at, parts, nv, ready):
        shift, scale = parts
        gcol = pcol(g_name, g_at, KT)
        for v, some in ((0, [t for t in tiles if t < NLAT]), (1, [t for t in tiles if t >= NLAT])):
            if some:
                stt(PRE_A[:, v * 8:v * 8 + 8], modc(scale, v, nv), 1.0, gcol, ALU.add, ALU.mult, after=ready)
                copy(PRE_B[:, v * 8:v * 8 + 8], modc(shift, v, nv))
        xn = grid(ar(xn_off, NTOK * D), NTOK)
        for t in tiles:
            tq = act(xn[:, t, :], resid(t), ACT.Square, accum=SSQ[:, t:t + 1], after=[g.last("dve"), t_x, ctx_in])
        t0, t1 = tiles[0], tiles[-1] + 1
        tr = rstd_of(RSTD[:, t0:t1], SSQ[:, t0:t1], D, after=[tq])
        txn = {}
        for t in tiles:
            if t % 2:
                txn[t] = act(xn[:, t, :], resid(t), ACT.Copy, scale=RSTD[:, t:t + 1], after=[tr])
            else:
                txn[t] = ts(xn[:, t, :], resid(t), RSTD[:, t:t + 1], None, ALU.mult, after=[tr])
        toks = []
        for v, some in ((0, [t for t in tiles if t < NLAT]), (1, [t for t in tiles if t >= NLAT])):
            for k in range(KT if some else 0):
                b, ps, bt = bank()
                for i, t in enumerate(some):
                    tok = turn(ps[:, i * P:(i + 1) * P], xn[:, t, k * P:(k + 1) * P], ident, after=[bt, txn[t]],
                               count=i == len(some) - 1)
                n = len(some) * P
                a, c = PRE_A[:, v * 8 + k:v * 8 + k + 1], PRE_B[:, v * 8 + k:v * 8 + k + 1]
                t0_ = some[0] * P

                def evac(dst, wait, ps=ps, n=n, a=a, c=c, tok=tok):
                    return act(dst, ps[:, 0:n], ACT.Identity, scale=a, bias=c, after=[tok, tr, wait])

                tv, te = split_feat(evac, FH[:, k, t0_:t0_ + n], FL[:, k, t0_:t0_ + n], (1, n))
                free(b, tv)
        return [g.last("act"), g.last("dve")]

    def post_begin(v, name, at, gate_part, nv, gb_off, after):
        gc = GATE[:, v * 8:v * 8 + 8]
        tg = tt(gc, modc(gate_part, v, nv), pcol(name, at, KT), ALU.mult, after=after)
        for h in range(2):
            b, ps, bt = bank()
            for k in range(4):
                tok = mm(ps[:, k * P:(k + 1) * P], gc[:, h * 4 + k:h * 4 + k + 1].broadcast_to((P, P)), ident,
                         after=[tg, bt], count=k == 3)
            te = copy(ar(gb_off + h * NMAX, NMAX), ps, after=[tok, after], eng="act")
            free(b, te)
        return te

    def keep_y(Y):
        def done(t, n0, n, ps, tok):
            h = n0 // NMAX
            c = copy(Y[:, t, n0:n0 + n], ps, after=[tok])
            act(junk_t[:, 0:n], Y[:, t, n0:n0 + n], ACT.Square, accum=SSQ[:, 2 * t + h:2 * t + h + 1], after=[c])
            return (c,)
        return done

    def post(tiles, Y, gb_offs):
        t0, t1 = tiles[0], tiles[-1] + 1
        pairs = SSQ[:, 2 * t0:2 * t1].rearrange("p (t h) -> p t h", h=2)
        a = tt(RSTD[:, t0:t1], pairs[:, :, 0], pairs[:, :, 1], ALU.add, after=[g.last("act")])
        rstd_of(RSTD[:, t0:t1], RSTD[:, t0:t1], D, after=[a])
        for t in tiles:
            gb = ar(gb_offs[0 if t < NLAT else 1], D)
            a = stt(Y[:, t, :], Y[:, t, :], RSTD[:, t:t + 1], gb, ALU.mult, ALU.mult, after=[g.last("act")])
            tok = tt(resid(t), resid(t), Y[:, t, :], ALU.add, after=[t_x, ctx_in])
        return tok

    def to_feat(y, tiles, after):
        toks = []
        for t in tiles:
            for h in range(2):
                b, ps, bt = bank()
                for k in range(4):
                    kk = h * 4 + k
                    tok = turn(ps[:, k * P:(k + 1) * P], y(t, kk), ident, after=[after, bt], count=k == 3)
                tv, te = split_feat(lambda dst, wait, ps=ps, tok=tok: copy(dst, ps, after=[tok, wait], eng="act"),
                                    FH[:, h * 4:h * 4 + 4, t * P:(t + 1) * P],
                                    FL[:, h * 4:h * 4 + 4, t * P:(t + 1) * P], (4, P))
                free(b, tv)
                toks.append(te)
        return toks

    def first_layer_end(i, y, name, Y, gb_off, tiles=LAT):
        tf = to_feat(y, tiles, [g.last("act"), g.last("dve")])
        tg = post_begin(0, "norm_post_g", i * KT, 2, 1, gb_off, [g.last("dve"), g.last("pe")])
        linear_tok(feat_tile, KT, name, 0, D, tiles, keep_y(Y), [tf])

    def head_rms(ps, nh, d, out, sq, ss, tok):
        a = act(sq, ps, ACT.Square, after=[tok])
        g.reduce(ss, grid(sq, nh), ALU.add, after=[a])
        r = rstd_of(ss, ss, d, after=[g.last("dve")])
        c = tt(grid(out, nh), grid(ps, nh), over(ss, d), ALU.mult, after=[r])
        return a, c

    def attention(units, bufs):
        PR, PTR, S = bufs[0:3], bufs[3:5], bufs[-1]
        NEGM, SUM = att_cols[:, 0:3], att_cols[:, 3:6]
        pr_readers, pt_readers = [[], [], []], [[], []]
        toks_of = dict(free_banks)
        assert len(toks_of) == 8
        pair_free = [toks_of[2 * i] + toks_of[2 * i + 1] for i in range(3)]
        one_free = [toks_of[6], toks_of[7]]
        n_pair = [0]
        state = {}

        def pair():
            i = n_pair[0] % 3
            n_pair[0] += 1
            return i, PS_t[:, 2 * i * NMAX:(2 * i + 2) * NMAX], pair_free[i]

        def stage_scores(n):
            u, i = units[n], n % 3
            nk = u["nk"]
            b, ps, bt = pair()
            for j, (lt, rh, n0, m, st, sp_) in enumerate(u["scores"]):
                tok = mm(ps[:, n0:n0 + m], lt, rh, st, sp_, after=[bt, u["ready"]], count=j == len(u["scores"]) - 1)
            src = ps[:, 0:nk]
            if u["bias"]:
                u["bias"](src, S[:, 0:nk], tok)
                src = S[:, 0:nk]
            tm = g.reduce(NEGM[:, i:i + 1], src, ALU.max, negate=True, after=[tok, g.last("act")])
            te = act(PR[i][:, 0:nk], src, ACT.Exp, bias=NEGM[:, i:i + 1], accum=SUM[:, i:i + 1],
                     after=[tm, pr_readers[i], tok])
            pair_free[b] = [tm, te]
            state[n] = te

        def stage_turn(n):
            u, i = units[n], n % 3
            nk = u["nk"]
            b, ps, bt = pair()
            for j in range(nk // P):
                tok = turn(ps[:, j * P:(j + 1) * P], PR[i][:, j * P:(j + 1) * P], ident, after=[bt, state[n]],
                           count=j == nk // P - 1)
            pr_readers[i] = [tok]
            te = copy(PTR[n % 2][:, 0:nk], ps[:, 0:nk], after=[tok, pt_readers[n % 2]],
                      eng="act" if u["bias"] or n % 2 else "dve")
            pair_free[b] = [te]
            tr = g.recip(SUM[:, i:i + 1], SUM[:, i:i + 1], after=[state[n]])
            state[n] = [te, tr]

        def stage_values(n):
            u, i = units[n], n % 3
            ps = PS_t[:, (6 + n % 2) * NMAX:(7 + n % 2) * NMAX]
            for j, v in enumerate(u["values"]):
                tok = mm(ps[:, 0:u["dv"]], PTR[n % 2][:, j * P:(j + 1) * P], v, j == 0, j == len(u["values"]) - 1,
                         after=[one_free[n % 2], state[n], u["ready"]], count=j == len(u["values"]) - 1)
            pt_readers[n % 2] = [tok]
            one_free[n % 2] = [u["done"](ps[:, 0:u["dv"]], SUM[:, i:i + 1], [tok, state[n]])]

        for n in range(len(units) + 2):
            if n < len(units):
                stage_scores(n)
            if 1 <= n <= len(units):
                stage_turn(n - 1)
            if n >= 2:
                stage_values(n - 2)
        free_banks[:] = [(2 * i + j, list(pair_free[i])) for i in range(3) for j in range(2)] + \
            [(6 + i, list(one_free[i])) for i in range(2)]

    att_cols = small(6)

    def gla(i, j, ready):
        H, DK, DV = 4, 128, 256
        q, k = grid(ar(0, 2048), H), grid(ar(2048, 2048), H)
        v, z = grid(ar(4096, 4096), NLAT), grid(ar(8192, 4096), NLAT)
        b_ = HC_t[:, :]
        aT = ar(12288, 512)
        ff = lambda off, n: FEAT_t[:, off:off + n]
        AT, QK0, QK1, e_, qe = (ff(n * 2048, 2048) for n in range(5))
        S_ = grid(ff(10240, 1024), H)
        gh = ff(11264, 1024)
        reset = aT
        ss, last_decay = junk_t[:, 256:272], junk_t[:, 272:288]
        wa2 = ROW_t[:, 0:512]
        t_par = g.dma("pool", "layer_params", wa2[0:16, :], io["gla_w_a2"][j], after=ready)
        lat = [(0, NLAT * P)]

        def keep_a(m, c0, c, ps, tok):
            return (copy(aT[0:16, c0:c0 + c], ps, after=[tok]),)

        linear_feat("gla_w_in", 3072, 16, lat, keep_a, ready)
        t_aT = g.last("dve")

        for h in range(H):
            b, ps, bt = bank()
            tok = mm(ps, wa2[0:16, h * DK:(h + 1) * DK], aT[0:16, :], after=[bt, t_aT, t_par], count=True)
            xs = b_[:, h * 512:(h + 1) * 512]
            tx = ts(xs, ps, pcol("gla_b_a", j * 4 + h), None, ALU.add, after=[tok])
            free(b, tx)
        t_wa = [tok]

        def keep_qk(m, c0, c, ps, tok):
            if m < 4:
                return (act(q[:, m, c0:c0 + c], ps, ACT.Copy, scale=DK ** -0.5, after=[tok]),)
            return (copy(k[:, m - 4, c0:c0 + c], ps, after=[tok]),)

        linear_feat("gla_w_in", 0, 1024, lat, keep_qk, ready)
        t_qk = [g.last("act"), g.last("dve")]

        def keep_vz(t, n0, n, ps, tok):
            if n0 < 1024:
                return (copy(v[:, t, n0:n0 + n], ps, after=[tok], eng=evac_engine()),)
            return (act(z[:, t, n0 - 1024:n0 - 1024 + n], ps, ACT.Silu, after=[tok]),)

        linear_tok(feat_tile, KT, "gla_w_in", 1024, 2048, LAT, keep_vz, ready)
        t_in = [g.last("pe"), g.last("act"), g.last("dve")]
        g.dma("pool", "layer_params", gh, io["gla_g_head"][j].rearrange("h d -> (h d)").partition_broadcast(P),
              after=t_in)
        t_par = g.dma("pool", "layer_params", reset, io["k_reset"][:, :], after=t_in)
        act(e_, b_, ACT.Abs, after=t_in)
        act(e_, e_, ACT.Exp, scale=-1.0)
        tl = act(e_, e_, ACT.Ln, bias=one_col)
        stt(b_, b_, 0.0, e_, ALU.min, ALU.subtract, after=[tl])
        for h in range(H):
            xs = b_[:, h * 512:(h + 1) * 512]
            tb = g.put("dve", lambda e, xs=xs: e.tensor_tensor_scan(xs, reset, xs, 0.0, ALU.mult, ALU.add),
                       [g.last("dve"), t_par])
        act(qe, b_, ACT.Exp, scale=1.0 / 16, after=[tb])
        for t in LAT:
            tt(z[:, t, :], z[:, t, :], gh, ALU.mult, after=[t_par, t_in], eng="pool")

        qf, kf = ar(0, 2048), ar(2048, 2048)
        ATg = AT.rearrange("p (n j) -> p n j", j=P)
        g.memset(AT, 0.0, after=[t_in])
        readers = [[], []]
        for lv in range(-1, LEVELS):
            if lv < 0:
                lhs, rhs, tq, mask = kf, qf, t_qk, ident
            else:
                s = 1 << lv
                QK = (QK0, QK1)[lv % 2]
                e4, b4, q4, k4, o4 = (x.rearrange("p (n h s) -> p n h s", h=2, s=s) for x in (e_, b_, qf, kf, QK))
                mid = b4[:, :, 0, s - 1:s].broadcast_to((P, 2048 // (2 * s), s))
                tt(e4[:, :, 0, :], mid, b4[:, :, 0, :], ALU.subtract, after=[g.last("act"), t_in])
                td = tt(e4[:, :, 1, :], b4[:, :, 1, :], mid, ALU.subtract)
                te = act(e_, e_, ACT.Exp, scale=1.0 / 16, after=[td])
                tt(o4[:, :, 0, :], k4[:, :, 0, :], e4[:, :, 0, :], ALU.mult, after=[te, readers[lv % 2]])
                tq = tt(o4[:, :, 1, :], q4[:, :, 1, :], e4[:, :, 1, :], ALU.mult)
                lhs = rhs = QK
                mask = LEVEL_U[lv]
            for h in range(H):
                b, ps, bt = bank()
                for c in range(NLAT):
                    at = slice((h * NLAT + c) * P, (h * NLAT + c + 1) * P)
                    tok = mm(ps[:, c * P:(c + 1) * P], lhs[:, at], rhs[:, at], after=[bt, tq], count=c == NLAT - 1)
                tm = g.put("dve", lambda e, h=h, ps=ps, mask=mask: e.copy_predicated(
                    ATg[:, h * NLAT:(h + 1) * NLAT, :], rows_over(mask.bitcast(U32), NLAT), grid(ps, NLAT)),
                    [g.last("dve"), tok])
                free(b, tm)
            readers[lv % 2] = [tok]
        t_at = tm

        blast = b_.rearrange("p (n t) -> p n t", t=P)
        tt(e_.rearrange("p (n t) -> p n t", t=P), blast[:, :, P - 1:P].broadcast_to((P, 16, P)), blast, ALU.subtract,
           after=[g.last("act")])
        te = act(e_, e_, ACT.Exp, scale=1.0 / 16, after=[g.last("dve")])
        tk = tt(e_, e_, kf, ALU.mult, after=[te])
        tc = copy(last_decay, qe.rearrange("p (n t) -> p n t", t=P)[:, :, P - 1])
        tqe = tt(qe, qe, qf, ALU.mult)
        ktok = QK0
        for n in range(4):
            b, ps, bt = bank()
            for m in range(4):
                tok = turn(ps[:, m * P:(m + 1) * P], e_[:, (4 * n + m) * P:(4 * n + m + 1) * P], ident,
                           after=[bt, tk], count=m == 3)
            t_kt = copy(ktok[:, n * 512:(n + 1) * 512], ps, after=[tok, readers], eng="act")
            free(b, t_kt)

        t_S = None
        t_pool = g.last("pool")
        for c in range(NLAT):
            t_s2 = []
            for h in range(H):
                n = h * NLAT + c
                at = slice(n * P, (n + 1) * P)
                vh = v[:, c, h * DV:(h + 1) * DV]
                b, ps, bt = bank()
                if c:
                    mm(ps[:, 0:DV], qe[:, at], S_[:, h, :], True, False, after=[bt, t_S, tqe])
                tok = mm(ps[:, 0:DV], AT[:, at], vh, c == 0, True, after=[bt, t_at], count=True)
                a = act(junk_t[:, 0:DV], ps[:, 0:DV], ACT.Square, accum=ss[:, n:n + 1], after=[tok])
                r = rstd_of(ss[:, n:n + 1], ss[:, n:n + 1], DV, after=[a])
                zh = z[:, c, h * DV:(h + 1) * DV]
                o = stt(zh, ps[:, 0:DV], ss[:, n:n + 1], zh, ALU.mult, ALU.mult, after=[r, t_pool])
                free(b, o)
                if c < NLAT - 1:
                    b, ps, bt = bank()
                    tok = mm(ps[:, 0:DV], ktok[:, at], vh, after=[bt, t_kt], count=True)
                    if c == 0:
                        t_s2 = copy(S_[:, h, :], ps[:, 0:DV], after=[tok])
                    else:
                        t_s2 = stt(S_[:, h, :], S_[:, h, :], last_decay[:, n:n + 1], ps[:, 0:DV], ALU.mult, ALU.add,
                                   after=[tok])
                    free(b, t_s2)
            t_S = t_s2
        first_layer_end(i, lambda t, k: z[:, t, k * P:(k + 1) * P], "gla_w_out", v, 0)
        return v, 0

    def sgu(i, ready):
        u, v, z = (grid(ar(n * 4096, 4096), NLAT) for n in range(3))
        lng, lnb = HC_t[:, 0:1024], HC_t[:, 1024:2048]
        ws, wsT = grid(ROW_t[:, 0:512], 4), grid(ar(12288, 512), 4)
        st, mv = ar(12800, 12), ar(12812, 8)
        t_par = g.dma("pool", "layer_params", lng, io["sgu_ln_g"][0].partition_broadcast(P), after=ready)
        t_par = g.dma("pool", "layer_params", lnb, io["sgu_ln_b"][0].partition_broadcast(P), after=ready)
        t_par = g.dma("pool", "layer_params", ws, io["sgu_w_s"][0].rearrange("g t s -> t g s"), after=ready)
        b, ps, bt = bank()
        for n in range(4):
            tok = turn(ps[:, n * P:(n + 1) * P], ws[:, n, :], ident, after=[bt, t_par], count=n == 3)
        t_ws = tt(wsT, grid(ps, 4), rows_over(TRI_U, 4), ALU.mult, after=[tok])
        free(b, t_ws)

        def keep(t, n0, n, ps, tok):
            dst = (u, v, z)[n0 // D][:, t, n0 % D:n0 % D + n]
            return (act(dst, ps, ACT.Silu if n0 >= 2 * D else ACT.Gelu_apprx_tanh, after=[tok]),)

        linear_tok(feat_tile, KT, "sgu_w_in", D, D, LAT, lambda t, n0, n, ps, tok: keep(t, n0 + D, n, ps, tok), ready)
        tv = g.last("act")
        for t in LAT:
            for h in range(2):
                g.put("dve", lambda e, t=t, h=h: e.bn_stats(st[:, 6 * h:6 * h + 6], v[:, t, h * 512:(h + 1) * 512]),
                      [g.last("dve"), tv])
            g.put("dve", lambda e: e.bn_aggr(mv[:, 0:2], st[:, 0:12].rearrange("p (a b) -> p a b", a=2)),
                  [g.last("dve")])
            rstd_of(mv[:, 2:3], mv[:, 1:2], 1, after=[g.last("dve")])
            ts(v[:, t, :], v[:, t, :], mv[:, 0:1], mv[:, 2:3], ALU.subtract, ALU.mult)
            tt(v[:, t, :], v[:, t, :], lng, ALU.mult, after=[t_par])
            tln = tt(v[:, t, :], v[:, t, :], lnb, ALU.add)
        linear_tok(feat_tile, KT, "sgu_w_in", 0, D, LAT, keep, ready)
        linear_tok(feat_tile, KT, "sgu_w_in", 2 * D, D, LAT,
                   lambda t, n0, n, ps, tok: keep(t, n0 + 2 * D, n, ps, tok), ready)
        tz = g.last("act")
        for t in LAT:
            tuz = tt(z[:, t, :], z[:, t, :], u[:, t, :], ALU.mult, after=[tz], eng="pool")
            for h in range(2):
                b, ps, bt = bank()
                for n in range(2):
                    gr = 2 * h + n
                    tok = mm(ps[:, n * 256:(n + 1) * 256], wsT[:, gr, :], v[:, t, gr * 256:(gr + 1) * 256],
                             after=[bt, tln, t_ws], count=n == 1)
                for n in range(2):
                    gr = 2 * h + n
                    zz = z[:, t, gr * 256:(gr + 1) * 256]
                    o = stt(zz, ps[:, n * 256:(n + 1) * 256], pcol("sgu_b_s", gr), zz, ALU.add, ALU.mult,
                            after=[tok, tuz])
                free(b, o)
        first_layer_end(i, lambda t, k: z[:, t, k * P:(k + 1) * P], "sgu_w_out", v, 0)
        return v, 0

    def fox(i, ready):
        H, DH = 16, 64
        qT, kT = grid(ar(0, 4096), 8), grid(ar(4096, 4096), 8)
        v = grid(ar(8192, 4096), NLAT)
        O = [qT[:, :, t * P:(t + 1) * P] for t in LAT]
        F, negF = ROW_t[:, 0:512], ROW_t[:, 512:1024]
        neg, Ftok = ar(12288, 128), grid(ar(12416, 64), NLAT)
        ss = ar(12480, 8)
        gq, gk, bf, gqs = (ar(12488 + n, 1) for n in range(4))
        qn, sq = [HC_t[:, 0:512], HC_t[:, 512:1024]], HC_t[:, 1024:1536]
        zs = [HC_t[:, 0:512], HC_t[:, 512:1024]]
        att = [HC_t[:, n * 512:(n + 1) * 512] for n in range(4)] + [ar(12496, 512), junk_t[:, :]]
        for n in range(2):
            g.dma("pool", "layer_params", gq[64 * n:64 * n + 64, :], io["fox_g_q"].rearrange("a d -> d a"), after=ready)
            g.dma("pool", "layer_params", gk[64 * n:64 * n + 64, :], io["fox_g_k"].rearrange("a d -> d a"), after=ready)
        g.dma("pool", "layer_params", bf[0:16, :], io["fox_b_f"].rearrange("a d -> d a"), after=ready)
        t_par = g.dma("pool", "layer_params", neg, io["k_neg"][:, :], after=ready)
        t_gq = ts(gqs, gq, DH ** -0.5, None, ALU.mult, after=[t_par])
        def keep_f(m, c0, c, ps, tok):
            return (ts(F[0:16, c0:c0 + c], ps, bf[0:16, :], None, ALU.add, after=[tok, t_par]),)

        linear_feat("fox_w_in", 4096, 16, [(0, 512)], keep_f, ready)
        F_, N_ = F[0:16, :], negF[0:16, :]
        act(N_, F_, ACT.Abs, after=[g.last("dve")])
        act(N_, N_, ACT.Exp, scale=-1.0)
        tl = act(N_, N_, ACT.Ln, bias=one_col[0:16, :])
        stt(F_, F_, 0.0, N_, ALU.min, ALU.subtract, after=[tl])
        g.memset(N_, 1.0)
        g.put("dve", lambda e: e.tensor_tensor_scan(F_, N_, F_, 0.0, ALU.mult, ALU.add), [g.last("dve")])
        tF = ts(N_, F_, -1.0, None, ALU.mult)
        b, ps, bt = bank()
        for t in LAT:
            tok = turn(ps[:, t * 16:(t + 1) * 16], F_[:, t * P:(t + 1) * P], ident[0:16, 0:16], after=[bt, tF],
                       count=t == NLAT - 1)
        tFt = copy(Ftok, ps[:, 0:64].rearrange("p (t h) -> p t h", h=16), after=[tok])
        free(b, tFt)
        rd = [[], []]
        cnt = [0]

        def keep(t, n0, n, ps, tok):
            if n0 >= 2048:
                return (copy(v[:, t, n0 - 2048:n0 - 2048 + n], ps, after=[tok], eng=evac_engine()),)
            r = cnt[0] % 2
            cnt[0] += 1
            a, c = head_rms(ps, 8, DH, qn[r], sq, ss, [tok, rd[r], g.last("dve")])
            pending.append((t, n0, r, c))
            if len(pending) > 1:
                turn_q(*pending.pop(0))
            return a, c

        pending = []

        def turn_q(t, n0, r, c):
            b, ps, bt = bank()
            for m in range(4):
                tk = turn(ps[:, m * P:(m + 1) * P], qn[r][:, m * P:(m + 1) * P], ident, after=[bt, c], count=m == 3)
            rd[r] = [tk]
            dst, gcol = (qT, gqs) if n0 < D else (kT, gk)
            p0 = (n0 % D) // P
            te = act(dst[:, p0:p0 + 4, t * P:(t + 1) * P], grid(ps, 4), ACT.Copy, scale=gcol, after=[tk, t_par, t_gq])
            free(b, te)

        linear_tok(feat_tile, KT, "fox_w_in", 0, 3072, LAT, keep, ready)
        while pending:
            turn_q(*pending.pop(0))
        t_in = [g.last("act"), g.last("dve"), g.last("pe")]
        units = []
        for t in LAT:
            for h in range(H):
                base, pr = 64 * (h % 2), h // 2
                nk = (t + 1) * P

                def bias(src, dst, tok, t=t, h=h, nk=nk):
                    if t:
                        ts(dst[:, 0:t * P], src[:, 0:t * P], Ftok[:, t, h:h + 1], None, ALU.add,
                           after=[tok, g.last("act")])
                    return stt(dst[:, t * P:nk], src[:, t * P:nk], Ftok[:, t, h:h + 1], neg, ALU.add, ALU.add,
                               after=[tok, g.last("act"), t_par])

                def done(ps, rinv, toks, t=t, h=h):
                    return ts(O[t][:, h // 2, 64 * (h % 2):64 * (h % 2) + 64], ps, rinv, None, ALU.mult, after=toks)

                units.append(dict(
                    nk=nk, ready=t_in, bias=bias, dv=DH, done=done,
                    scores=[(qT[base:base + 64, pr, t * P:(t + 1) * P], kT[base:base + 64, pr, 0:nk], 0, nk, True, False),
                            (ident[0:16, h:h + 1].broadcast_to((16, P)), N_[:, 0:nk], 0, nk, False, True)],
                    values=[v[:, s, h * DH:(h + 1) * DH] for s in range(t + 1)]))
        attention(units, att)
        z_readers = [[], []]
        t_att = [g.last("act"), g.last("dve"), g.last("pe")]

        def gate_o(t, n0, n, ps, tok):
            a = act(zs[t % 2], ps, ACT.Silu, after=[tok, z_readers[t % 2], t_att])
            o = O[t][:, n0 // P:n0 // P + 4, :]
            z_readers[t % 2] = [tt(o, o, grid(zs[t % 2], 4), ALU.mult, after=[a])]
            return (a,)

        linear_tok(feat_tile, KT, "fox_w_in", 3072, 1024, LAT, gate_o, ready)
        first_layer_end(i, lambda t, k: O[t][:, k, :], "fox_w_out", v, 4096)
        return v, 4096

    def ffn(tiles, ready):
        T = len(tiles) * P
        Y = grid(ar(0, NTOK * D), NTOK)
        h0 = NTOK * D
        G = grid(ar(h0, 4 * T), 4)
        HH = grid(AR_r[:, h0:h0 + 4 * T], 4)
        HL = grid(AR_r[:, h0 + 4 * T:h0 + 8 * T], 4)
        ranges = [(0, 512), (512, 256)] if T > 512 else [(0, 512)]

        def keep_gate(m, c0, c, ps, tok):
            return (act(G[:, m, c0:c0 + c], ps, ACT.Silu, after=[tok]),)

        def keep_hidden(m, c0, c, ps, tok):
            tv, te = split_feat(lambda dst, wait: tt(dst, G[:, m, c0:c0 + c], ps, ALU.mult,
                                                     after=[tok, wait, g.last("act")]),
                                HH[:, m, c0:c0 + c], HL[:, m, c0:c0 + c], (1, c))
            return (tv,)

        def add_y(t, n0, n, ps, tok):
            y = Y[:, t, n0:n0 + n]
            c = copy(y, ps, after=[tok]) if f0 == 0 else tt(y, y, ps, ALU.add, after=[tok])
            if f0 + NMAX >= DFF:
                h = n0 // NMAX
                act(junk_t[:, 0:n], y, ACT.Square, accum=SSQ[:, 2 * t + h:2 * t + h + 1], after=[c])
            return (c,)

        for f0 in range(0, DFF, NMAX):
            nf = min(NMAX, DFF - f0)
            linear_feat("w_ffn_gate_2", f0, nf, ranges, keep_gate, ready)
            linear_feat("w_ffn_up_2", f0, nf, ranges, keep_hidden, ready)
            linear_tok(lambda k, t: (HH[:, k, t * P:(t + 1) * P], HL[:, k, t * P:(t + 1) * P]), nf // P,
                       "w_ffn_down_2", 0, D, tiles, add_y, [g.last("dve")], k0=f0 // P)
        return Y

    def rope(x1, x2, o1, o2, cs, sn, t1, t2, after):
        nh, h = x1.shape[1], x1.shape[2]
        c, s = rows_over(cs, nh), rows_over(sn, nh)
        tt(t1, x2, s, ALU.mult, after=after)
        tt(t2, x1, s, ALU.mult)
        tt(o1, x1, c, ALU.mult)
        tt(o1, o1, t1, ALU.subtract)
        tt(o2, x2, c, ALU.mult)
        return tt(o2, o2, t2, ALU.add)

    def even(ready):
        QT, KTT = grid(ar(0, 3072), 4), grid(ar(3072, 3072), 4)
        vtok = grid(ar(6144, 3072), NTOK)
        c0_ = 9216
        PADW = 776
        raw = [ar(c0_ + n * PADW, PADW) for n in range(2)]
        acc, sqb = ar(c0_ + 2 * PADW, 768), ar(c0_ + 2 * PADW + 768, 768)
        onescol = ar(c0_ + 2 * PADW + 1536, P)
        g.memset(onescol, 0.0, after=ready)
        g.memset(onescol[0:64, 0:64], 1.0)
        t_ones = g.memset(onescol[64:128, 64:128], 1.0)
        t_rz = [g.memset(raw[n], 0.0) for n in range(2)]
        GA, BETA = grid(small(96), NTOK), grid(small(96), NTOK)
        dtb, nega = ar(c0_ + 3216, 16), ar(c0_ + 3232, 16)
        abt = grid(ar(c0_ + 3248, NTOK * 16), NTOK)
        g.dma("pool", "layer_params", dtb, io["gdn_dt_bias_2"][0].rearrange("a b -> (a b)").partition_broadcast(P),
              after=ready)
        t_par = g.dma("pool", "layer_params", nega, io["gdn_a_log_2"][0].rearrange("a b -> (a b)")
                      .partition_broadcast(P), after=ready)
        act(nega, nega, ACT.Exp, after=[t_par])
        gate_dram = nc.dram_tensor("gate_spill", [P, NTOK, 512], F32, kind="Internal")
        down_dram = nc.dram_tensor("down_spill", [P, NTOK, 416], F32, kind="Internal")
        gate_sb = [raw[0][:, 0:512], raw[1][:, 0:512]]

        def keep_ab(t, n0, n, ps, tok):
            a = tt(GA[:, t, :], ps[:, 0:16], dtb, ALU.add, after=[tok, t_par])
            c = act(BETA[:, t, :], ps[:, 16:32], ACT.Sigmoid, after=[tok, a])
            return a, c

        linear_tok(feat_tile, KT, "w_in_even_2", 2048, 32, range(NTOK), keep_ab, ready)
        act(abt, GA, ACT.Abs, after=[g.last("dve")])
        act(abt, abt, ACT.Exp, scale=-1.0)
        tl = act(abt, abt, ACT.Ln, bias=one_col)
        stt(GA, GA, 0.0, abt, ALU.max, ALU.add, after=[tl])
        stt(GA, GA, -1.0, rows_over(nega, NTOK), ALU.mult, ALU.mult)
        gate_readers = [[], []]

        def keep_gate(t, n0, n, ps, tok):
            a = act(gate_sb[t % 2], ps, ACT.Silu, after=[tok, gate_readers[t % 2], t_rz])
            gate_readers[t % 2] = [g.dma("act", f"gate_out_{t % 2}", gate_dram[:, t, :], gate_sb[t % 2], after=[a])]
            return (a,)

        def keep_down(t, n0, n, ps, tok):
            a = copy(gate_sb[t % 2][:, 0:416], ps, after=[tok, gate_readers[t % 2], t_rz], eng="act")
            gate_readers[t % 2] = [g.dma("act", f"gate_out_{t % 2}", down_dram[:, t, :], gate_sb[t % 2][:, 0:416],
                                         after=[a])]
            return (a,)

        linear_tok(feat_tile, KT, "w_in_even_2", 1536, 512, range(NTOK), keep_gate, ready)
        linear_tok(feat_tile, KT, "w_in_even_2", 2080, 416, range(NTOK), keep_down, ready)
        t_down_out = [list(x) for x in gate_readers]
        for n in range(2):
            g.memset(raw[n], 0.0, after=[gate_readers[n]])
        t_rz = g.last("dve")
        raw_readers = [[], []]
        spans = [(2, 0, 512), (518, 512, 256)]
        tail = []

        def conv_tail(m, ta):
            if m < 8:
                a = act(sqb, acc, ACT.Square, after=[ta, g.last("dve")])
                for c0, c in ((0, 512), (512, 256)):
                    b, ps, bt = bank()
                    tok = mm(ps[:, 0:c], onescol, sqb[:, c0:c0 + c], after=[bt, a, t_ones], count=True)
                    te = act(sqb[:, c0:c0 + c], ps[:, 0:c], ACT.Sqrt, bias=eps_col, after=[tok])
                    free(b, te)
                g.recip(sqb, sqb, after=[te])
                if m < 4:
                    return stt(QT[:, m, :], acc, 0.125, sqb, ALU.mult, ALU.mult)
                return tt(KTT[:, m - 4, :], acc, sqb, ALU.mult)
            return to_tokens(acc, ta, vtok, m - 8)

        def to_tokens(src, td, dst, m):
            for ts0, nt in ((0, 4), (4, 2)):
                b, ps, bt = bank()
                for t in range(nt):
                    tok = turn(ps[:, t * P:(t + 1) * P], src[:, (ts0 + t) * P:(ts0 + t + 1) * P], ident,
                               after=[bt, td], count=t == nt - 1)
                te = copy(dst[:, ts0:ts0 + nt, m * P:(m + 1) * P],
                          grid(ps[:, 0:nt * P], nt), after=[tok], eng="act")
                free(b, te)
            return te

        def keep_conv(m, c0, c, ps, tok):
            r = m % 2
            off = 2 if c0 == 0 else 518
            a = copy(raw[r][:, off:off + c], ps, after=[tok, raw_readers[r], t_rz], eng="act")
            if c0:
                for o, d0, n in spans:
                    for j in range(5):
                        src = raw[r][:, o - 2 + j:o - 2 + j + n]
                        wj = pcol("gdn_conv_2", j * 12 + m)
                        if j == 0:
                            ts(acc[:, d0:d0 + n], src, wj, None, ALU.mult, after=[a, g.last("pe"), g.last("act")])
                        else:
                            stt(acc[:, d0:d0 + n], src, wj, acc[:, d0:d0 + n], ALU.mult, ALU.add)
                raw_readers[r] = [g.last("dve")]
                ta = act(acc, acc, ACT.Silu, after=[g.last("dve")])
                conv_tail(m, ta)
            return (a,)

        linear_feat("w_in_even_2", 0, 1536, [(0, 512), (512, 256)], keep_conv, ready)
        t_conv = [g.last("act"), g.last("dve"), g.last("pe")]

        GC, EG, KD, BEG, GL = (grid(ar(c0_ + n * 96, 96), NTOK) for n in range(5))
        r0 = c0_ + 480
        ones = ROW_t[:, 0:P]
        u_, wT, qdT, kd = (ar(r0 + n * 512, 512) for n in range(4))
        vb, kb, C2 = ar(r0 + 2048, 512), ar(r0 + 2560, 512), ar(r0 + 2048, 1024)
        S2 = [ar(r0 + 3072 + n * 256, 256) for n in range(2)]
        Gh = junk_t[:, 0:4]
        ktok, OG = grid(FEAT_t[:, 6144:9216], NTOK), grid(FEAT_t[:, 9216:12288], NTOK)
        DIF, DD, DU, XX, XT, VV = (FEAT_t[:, n * 1024:(n + 1) * 1024] for n in range(6))
        h8 = lambda ap: ap.rearrange("p (h n) -> p h n", h=8)
        g.memset(ones, 1.0, after=t_conv)
        for m in range(4):
            to_tokens(KTT[:, m, :], t_conv, ktok, m)
        b, ps, bt = bank()
        for t in range(NTOK):
            for d in range(2):
                tok = mm(ps[:, t * 16 + d * 8:t * 16 + d * 8 + 8], (TRI_U, TRI_L)[d], GA[:, t, d * 8:d * 8 + 8],
                         after=[bt, t_conv])
        tok = mm(ps[:, 96:192], ones, GA.rearrange("p t d -> p (t d)"), after=[g.last("dve")], count=True)
        f = lambda x: x.rearrange("p t d -> p (t d)")
        copy(f(GC), ps[:, 0:96], after=[tok])
        a = tt(f(KD), ps[:, 96:192], f(GC), ALU.subtract)
        act(f(EG), f(GC), ACT.Exp, after=[a])
        act(f(KD), f(KD), ACT.Exp)
        te = act(f(GL), ps[:, 96:192], ACT.Exp)
        free(b, te, a)
        tb = tt(f(BEG), f(BETA), f(EG), ALU.mult, after=[te])
        step_done = [None, None]
        started = [False, False]
        order = [(d, t) for pair in zip([4, 5, 0, 1, 2, 3], [5, 4, 3, 2, 1, 0]) for d, t in enumerate(pair)]
        seen = set()
        for d, t in order:
            lv, tri = (LEVEL_L, TRI_U) if d == 0 else (LEVEL_U, TRI_L)
            gs = slice(d * 8, d * 8 + 8)
            tile = slice(t * P, (t + 1) * P)
            for hb in range(2):
                b, ps, bt = bank()
                for h in range(4):
                    hh = hb * 4 + h
                    tok = mm(ps[:, h * P:(h + 1) * P],
                             GA[:, t, d * 8 + hh:d * 8 + hh + 1].broadcast_to((P, P)), tri,
                             after=[bt], count=h == 3)
                half = slice(hb * 512, (hb + 1) * 512)
                a = tt(grid(DIF[:, half], 4), grid(ps, 4), over(GC[:, t, d * 8 + hb * 4:d * 8 + hb * 4 + 4], P),
                       ALU.subtract, after=[tok, step_done])
                for par in range(2):
                    rows = slice(64 * par, 64 * par + 64)
                    src = grid(ps, 4)[rows, par::2, :]
                    c = act(grid(qdT, 4)[rows, hb * 2:hb * 2 + 2, :], src, ACT.Exp, after=[tok, a, step_done])
                free(b, a, c)
            tt(qdT.rearrange("p (m n) -> p m n", m=4), qdT.rearrange("p (m n) -> p m n", m=4), QT[:, :, tile],
               ALU.mult, after=[c])
            ts(DD, DIF, 0.0, None, ALU.min)
            a = ts(DU, DIF, 0.0, None, ALU.max)
            act(DD, DD, ACT.Exp, after=[a])
            td = act(DU, DU, ACT.Exp, scale=-1.0)
            for par in range(2):
                mine = lambda ap: h8(ap)[:, par::2, :]
                for which in range(2):
                    b, ps, bt = bank()
                    for h in range(4):
                        hh = 2 * h + par
                        rows = slice(64 * par, 64 * par + 64)
                        kk = KTT[rows, hh // 2, tile]
                        tok = mm(ps[:, h * P:(h + 1) * P], kk, (kk, QT[rows, hh // 2, tile])[which],
                                 after=[bt, t_conv], count=h == 3)
                    if which == 0:
                        tt(mine(DU), mine(DU), grid(ps, 4), ALU.mult, after=[tok, td])
                        a = tt(mine(DU), mine(DU), over(BETA[:, t, d * 8 + par:d * 8 + 8:2], P), ALU.mult)
                    else:
                        tt(mine(DD), mine(DD), grid(ps, 4), ALU.mult, after=[tok, td])
                        a = tt(mine(DD), mine(DD), rows_over(tri, 4), ALU.mult)
                    free(b, a)
            tM = a
            stt(h8(DIF), h8(DU), -1.0, rows_over(lv[0], 8), ALU.mult, ALU.mult)
            tx = tt(h8(XX), h8(DIF), rows_over(ident, 8), ALU.add)
            for hb in range(2):
                b, ps, bt = bank()
                for h in range(4):
                    at = slice((hb * 4 + h) * P, (hb * 4 + h + 1) * P)
                    tok = turn(ps[:, h * P:(h + 1) * P], XX[:, at], ident, after=[bt, tx], count=h == 3)
                txt = copy(XT[:, hb * 512:(hb + 1) * 512], ps, after=[tok], eng="act")
                free(b, txt)
            readers_c = [[tM, tx, g.last("pe")], [step_done, g.last("dve")]]
            txs = [tx, tx]
            for level in range(1, LEVELS):
                C = (DIF, C2)[level % 2]
                tc = tt(h8(C), h8(DU), rows_over(lv[level], 8), ALU.mult, after=[tM, readers_c[level % 2]], eng="pool")
                tv = []
                for hb in range(2):
                    b, ps, bt = bank()
                    for h in range(4):
                        at = slice((hb * 4 + h) * P, (hb * 4 + h + 1) * P)
                        tok = mm(ps[:, h * P:(h + 1) * P], C[:, at], XT[:, at], after=[bt, tc, txs[hb], txt],
                                 count=h == 3)
                    tv.append(copy(VV[:, hb * 512:(hb + 1) * 512], ps, after=[tok], eng="act"))
                    free(b, tv[-1])
                readers_c[level % 2] = [tok]
                for hb in range(2):
                    zz = []
                    for which in range(2 if level < LEVELS - 1 else 1):
                        b, ps, bt = bank()
                        for h in range(4):
                            at = slice((hb * 4 + h) * P, (hb * 4 + h + 1) * P)
                            l_, r_ = ((XX, VV), (VV, XX))[which]
                            tok = mm(ps[:, h * P:(h + 1) * P], l_[:, at], r_[:, at], after=[bt, tv[hb]], count=h == 3)
                        zz.append((b, ps, tok))
                    half = slice(hb * 512, (hb + 1) * 512)
                    for (b, ps, tok), dst in zip(zz, (XT, XX)):
                        txs[hb] = tt(dst[:, half], dst[:, half], ps, ALU.subtract, after=[tok])
                        free(b, txs[hb])
            tx = txs[1]
            v3, k3 = grid(vtok[:, t, :], 8), grid(ktok[:, t, :], 8)
            tt(grid(vb, 8), v3, over(BETA[:, t, gs], 64), ALU.mult, after=[readers_c])
            tt(grid(kb, 8), k3, over(BEG[:, t, gs], 64), ALU.mult, after=[tb])
            tk = tt(grid(kd, 8), k3, over(KD[:, t, gs], 64), ALU.mult)
            b, ps, bt = bank()
            for h in range(8):
                at = slice(h * P, (h + 1) * P)
                tok = mm(ps[:, h * 64:(h + 1) * 64], XT[:, at], vb[:, h * 64:(h + 1) * 64], after=[bt, tk], count=h == 7)
            tu = copy(u_, ps, after=[tok], eng="act")
            free(b, tu)
            b, ps, bt = bank()
            for h in range(8):
                at = slice(h * P, (h + 1) * P)
                tok = mm(ps[64 * (h % 2):64 * (h % 2) + 64, (h // 2) * P:(h // 2 + 1) * P], kb[:, h * 64:(h + 1) * 64],
                         XT[:, at], after=[bt], count=h == 7)
            tw = copy(wT, ps, after=[tok], eng="act")
            free(b, tw)
            S = S2[d]
            rows = lambda h: slice(64 * (h % 2), 64 * (h % 2) + 64)
            if started[d]:
                for par in range(2):
                    b, ps, bt = bank()
                    for m in range(4):
                        tok = mm(ps[:, m * 64:(m + 1) * 64], wT[rows(par), m * P:(m + 1) * P],
                                 S[rows(par), m * 64:(m + 1) * 64], after=[bt, tw, step_done], count=m == 3)
                    mine = grid(u_, 8)[:, par::2, :]
                    tn = tt(mine, mine, grid(ps[:, 0:256], 4), ALU.subtract, after=[tok, tu])
                    free(b, tn)
            else:
                tn = tu
            for par in range(2):
                b, ps, bt = bank()
                for m in range(4):
                    h = 2 * m + par
                    if started[d]:
                        mm(ps[:, m * 64:(m + 1) * 64], qdT[rows(h), m * P:(m + 1) * P],
                           S[rows(h), m * 64:(m + 1) * 64], True, False, after=[bt, tn])
                    tok = mm(ps[:, m * 64:(m + 1) * 64], DD[:, h * P:(h + 1) * P], u_[:, h * 64:(h + 1) * 64],
                             not started[d], True, after=[bt, tn, tk], count=m == 3)
                dst, src = grid(OG[:, t, :], 8)[:, par::2, :], grid(ps[:, 0:256], 4)
                if t in seen:
                    a = tt(dst, dst, src, ALU.add, after=[tok])
                else:
                    a = copy(dst, src, after=[tok])
                free(b, a)
            seen.add(t)
            b, ps, bt = bank()
            for h in range(8):
                tok = mm(ps[rows(h), (h // 2) * 64:(h // 2 + 1) * 64], kd[:, h * 64:(h + 1) * 64],
                         u_[:, h * 64:(h + 1) * 64], after=[bt, tn], count=h == 7)
            if started[d]:
                for par in range(2):
                    copy(Gh[64 * par:64 * par + 64, 0:4], GL[64 * par:64 * par + 64, t, d * 8 + par:d * 8 + 8:2])
                tt(S.rearrange("p (m n) -> p m n", m=4), S.rearrange("p (m n) -> p m n", m=4), over(Gh[:, 0:4], 64),
                   ALU.mult, after=[tok])
                a = tt(S, S, ps[:, 0:256], ALU.add)
            else:
                a = copy(S, ps[:, 0:256], after=[tok])
            free(b, a)
            started[d] = True
            step_done = [a, tok, g.last("act")]
        O = grid(ar(0, NTOK * D), NTOK)
        GB = grid(ar(6144, 3072), NTOK)
        onb = ar(9216, 64)
        sq, ssg = ar(9280, 512), ar(9792, 8)
        down = grid(ar(9904, NTOK * 416), NTOK)
        t_dn = g.dma("pool", "down_in", down, down_dram[:, :, :], after=[step_done, t_down_out])
        g.dma("pool", "layer_params", onb, io["gdn_out_norm_2"][0].partition_broadcast(P), after=[step_done])
        t_par = g.dma("pool", "layer_params", GB, gate_dram[:, :, :], after=[step_done, t_down_out])
        for t in range(NTOK):
            o_ = O[:, t, 0:512]
            head_rms(OG[:, t, :], 8, 64, o_, sq, ssg, [g.last("dve"), step_done])
            tt(grid(o_, 8), grid(o_, 8), rows_over(onb, 8), ALU.mult, after=[t_par])
            tt(o_, o_, GB[:, t, :], ALU.mult)
        t_gdn = [g.last("act"), g.last("dve"), g.last("pe")]
        H, NOPE, ROPE, DQK = 8, 64, 32, 96
        o0 = NTOK * D
        qd, kvd = down[:, :, 0:256], down[:, :, 256:416]
        qnT, kvT = grid(ar(6144, 1536), 2), ar(7680, 768)
        cs, sn = grid(ar(8448, 64), NLAT), grid(ar(8512, 64), NLAT)
        ss = ar(8576, 16)
        t1, t2 = (ar(8592 + 64 * n, 64).rearrange("p (h d) -> p h d", d=16) for n in range(2))
        kpe = grid(ar(8720, NTOK * 32), NTOK)
        qk_tok = [ar(8912 + n * 384, 384) for n in range(2)]
        qT, kT = grid(FEAT_t[:, 0:3072], 4), grid(FEAT_t[:, 3072:6144], 4)
        vt = grid(FEAT_t[:, 6144:7680], NTOK)
        att = [FEAT_t[:, 7680 + n * 768:8448 + n * 768] for n in range(5)]
        g.dma("pool", "layer_params", cs, io["k_cos_mla"][:, :, :], after=t_gdn)
        t_par = g.dma("pool", "layer_params", sn, io["k_sin_mla"][:, :, :], after=t_gdn)
        for t in range(NTOK):
            act(junk_t[:, 0:256], qd[:, t, :], ACT.Square, accum=ss[:, t:t + 1], after=[t_gdn, t_dn])
            a = act(junk_t[:, 0:128], kvd[:, t, 0:128], ACT.Square, accum=ss[:, 8 + t:9 + t])
        rstd_of(ss[:, 0:6], ss[:, 0:6], 256, after=[a])
        r = rstd_of(ss[:, 8:14], ss[:, 8:14], 128)
        for t in range(NTOK):
            ts(qd[:, t, :], qd[:, t, :], ss[:, t:t + 1], None, ALU.mult, after=[r, t_dn])
            ts(kvd[:, t, 0:128], kvd[:, t, 0:128], ss[:, 8 + t:9 + t], None, ALU.mult)
            if t < NLAT:
                a1, a2 = kvd[:, t, 128:144].unsqueeze(1), kvd[:, t, 144:160].unsqueeze(1)
                tn = rope(a1, a2, kpe[:, t, 0:16].unsqueeze(1), kpe[:, t, 16:32].unsqueeze(1), cs[:, t, :],
                          sn[:, t, :], t1[:, 0:1, :], t2[:, 0:1, :], [t_par])
            else:
                tn = copy(kpe[:, t, :], kvd[:, t, 128:160])
            b, ps, bt = bank()
            turn(ps[:, 0:P], qd[:, t, 0:P], ident, after=[bt, tn])
            turn(ps[:, P:2 * P], qd[:, t, P:2 * P], ident)
            tok = turn(ps[:, 2 * P:3 * P], kvd[:, t, 0:P], ident, count=True)
            for m in range(2):
                act(qnT[:, m, t * P:(t + 1) * P], ps[:, m * P:(m + 1) * P], ACT.Copy, scale=pcol("mla_q_norm_2", m),
                    after=[tok])
            te = act(kvT[:, t * P:(t + 1) * P], ps[:, 2 * P:3 * P], ACT.Copy, scale=pcol("mla_kv_norm_2", 0))
            free(b, te)
        t_down = [te]
        for grp in range(2):
            rd = [[], []]

            def up_q(t, n0, n, ps, tok):
                r = t % 2
                qk = qk_tok[r].rearrange("p (h d) -> p h d", d=DQK)
                psv = ps.rearrange("p (h d) -> p h d", d=DQK)
                if t < NLAT:
                    a = act(qk, psv, ACT.Copy, scale=DQK ** -0.5, after=[tok, rd[r], g.last("dve")])
                    x1, x2 = qk[:, :, 64:80], qk[:, :, 80:96]
                    tt(t1, x2, rows_over(sn[:, t, :], 4), ALU.mult, after=[a, t_par])
                    tt(t2, x1, rows_over(sn[:, t, :], 4), ALU.mult)
                    tt(x1, x1, rows_over(cs[:, t, :], 4), ALU.mult)
                    tt(x1, x1, t1, ALU.subtract)
                    tt(x2, x2, rows_over(cs[:, t, :], 4), ALU.mult)
                    c = tt(x2, x2, t2, ALU.add)
                else:
                    a = c = act(qk, psv, ACT.Copy, scale=DQK ** -0.5, after=[tok, rd[r], g.last("dve")])
                b, p2, bt = bank()
                for h in range(4):
                    tk = turn(p2[0:DQK, h * P:(h + 1) * P], qk[:, h, :], ident, after=[bt, c], count=h == 3)
                rd[r] = [tk]
                te = copy(qT[0:DQK, :, t * P:(t + 1) * P], grid(p2[0:DQK, :], 4), after=[tk, g.last("pe")], eng="act")
                free(b, te)
                return (a,)

            def up_kv(t, n0, n, ps, tok):
                r = t % 2
                psv = ps.rearrange("p (h d) -> p h d", d=128)
                qk = qk_tok[r].rearrange("p (h d) -> p h d", d=DQK)
                a1 = copy(qk[:, :, 0:64], psv[:, :, 0:64], after=[tok, rd[r], g.last("act")])
                c = copy(qk[:, :, 64:96], rows_over(kpe[:, t, :], 4))
                a2 = copy(vt[:, t, :].rearrange("p (h d) -> p h d", d=64), psv[:, :, 64:128], after=[tok, a1], eng="act")
                b, p2, bt = bank()
                for h in range(4):
                    tk = turn(p2[0:DQK, h * P:(h + 1) * P], qk[:, h, :], ident, after=[bt, c], count=h == 3)
                rd[r] = [tk]
                te = copy(kT[0:DQK, :, t * P:(t + 1) * P], grid(p2[0:DQK, :], 4), after=[tk], eng="dve")
                free(b, te)
                return a1, a2

            src_q = lambda k, t: (qnT[:, k, t * P:(t + 1) * P], None)
            src_k = lambda k, t: (kvT[:, t * P:(t + 1) * P], None)
            prev = [t_down, t_gdn, g.last("pe"), g.last("act"), g.last("dve")]
            g.put("act", lambda e: e.activation(ss[:, 14:15], one_col, ACT.Copy), prev)
            g.put("dve", lambda e: e.tensor_copy(ss[:, 15:16], one_col), prev)
            linear_tok(src_q, 2, "mla_w_q_up_2", grp * 384, 384, range(NTOK), up_q, prev)
            rd = [list(rd[0]), list(rd[1])]
            linear_tok(src_k, 1, "mla_w_kv_up_2", grp * 512, 512, range(NTOK), up_kv, prev)
            t_up = [g.last("act"), g.last("dve"), g.last("pe")]
            units = []
            for t in range(NTOK):
                for h in range(4):
                    hh = grp * 4 + h

                    def done(ps, rinv, toks, t=t, hh=hh):
                        return ts(O[:, t, 512 + hh * 64:512 + hh * 64 + 64], ps, rinv, None, ALU.mult, after=toks)

                    q_ = qT[0:DQK, h, t * P:(t + 1) * P]
                    if t < NLAT:
                        sc = [(q_, kT[0:DQK, h, 0:512], 0, 512, True, True),
                              (q_, kT[0:DQK, h, 512:768], 512, 256, True, True)]
                        keys = range(NTOK)
                    else:
                        sc = [(q_, kT[0:DQK, h, 512:768], 0, 256, True, True)]
                        keys = CTX
                    units.append(dict(nk=len(keys) * P, ready=t_up, bias=None, dv=64, done=done, scores=sc,
                                      values=[vt[:, s, h * 64:(h + 1) * 64] for s in keys]))
            attention(units, att)
        return O

    def odd(ready):
        DH = 64
        naq, nak = grid(ar(0, 2048), 4), grid(ar(2048, 3072), 4)
        nav = grid(ar(5120, 3072), NTOK)
        gq, gk = grid(ar(8192, 2048), 4), grid(ar(10240, 1536), 2)
        gv = grid(ar(11776, 768), NTOK)
        cs, sn = grid(ar(12544, 128), NLAT), grid(ar(12672, 128), NLAT)
        qg, kg, nam = (ar(12800 + 64 * n, 64) for n in range(3))
        kt_, ss = ar(12992, 128), ar(13120, 8)
        qn, sq = [HC_t[:, 0:512], HC_t[:, 512:1024]], HC_t[:, 1024:1536]
        kn = [HC_t[:, 1536:1792], HC_t[:, 1792:2048]]
        t1, t2 = (junk_t[:, n * 256:(n + 1) * 256].rearrange("p (h d) -> p h d", d=32) for n in range(2))
        att = [FEAT_t[:, n * 768:(n + 1) * 768] for n in range(6)]
        TB = FEAT_t[:, 4608:4608 + 3584]
        ON, OD = ([x[:, :, t * P:(t + 1) * P] for t in LAT] for x in (naq, gq))
        g.dma("pool", "layer_params", cs, io["k_cos_gqa"][:, :, :], after=ready)
        g.dma("pool", "layer_params", sn, io["k_sin_gqa"][:, :, :], after=ready)
        g.dma("pool", "layer_params", nam, io["k_window"][:, :], after=ready)
        g.dma("pool", "layer_params", qg, io["gqa_q_norm_2"][0].partition_broadcast(P), after=ready)
        t_par = g.dma("pool", "layer_params", kg, io["gqa_k_norm_2"][0].partition_broadcast(P), after=ready)
        W = 127
        rp = ROW_t[:, 0:W]
        tz = g.memset(rp[0:120, :], 0.0, after=ready)
        t_rp = g.dma("pool", "rpb_in", rp[0:120, 48:79], io["na_rpb_2"][0].rearrange("h r c -> (h r) c"), after=[tz])
        skew = nc.dram_tensor("rpb_rows", [8 * 15, 64, W], F32, kind="Internal")
        t_sk = g.dma("pool", "rpb_out", skew[:, :, :], rp[0:120, :].unsqueeze(1).broadcast_to((120, 64, W)),
                     after=[t_rp])

        def read_bias(grp, after):
            for par in range(2):
                for h in range(4):
                    src = bass.AP(tensor=skew.ap().tensor if hasattr(skew, "ap") else skew,
                                  offset=((grp * 4 + h) * 15 + 1 - par) * 64 * W + 63,
                                  ap=[[W - 1, 64], [64 * W, 14], [1, 64]])
                    dst = TB[64 * par:64 * par + 64, h * 896:(h + 1) * 896].rearrange("p (r c) -> p r c", r=14)
                    tok = g.dma("pool", "bias_in", dst, src, after=[t_sk, after])
            tv = TB.rearrange("p (n c) -> p n c", c=64)
            return tt(tv, tv, rows_over(nam, 56), ALU.add, after=[tok, t_par])

        def keep_feat(dst, scale):
            def done(m, c0, c, ps, tok):
                if scale != 1.0:
                    return (act(dst[:, m, c0:c0 + c], ps, ACT.Copy, scale=scale, after=[tok]),)
                return (copy(dst[:, m, c0:c0 + c], ps, after=[tok], eng=evac_engine()),)
            return done

        all_ = [(0, 512), (512, 256)]
        linear_feat("w_in_odd_2", 0, 512, [(0, 512)], keep_feat(naq, DH ** -0.5), ready)
        linear_feat("w_in_odd_2", 512, 512, all_, keep_feat(nak, 1.0), ready)
        linear_tok(feat_tile, KT, "w_in_odd_2", 1024, 512, range(NTOK),
                   lambda t, n0, n, ps, tok: (copy(nav[:, t, :], ps, after=[tok], eng=evac_engine()),), ready)
        rd = [[], []]
        pending = []

        def rot(x, nh, t, c):
            a1, a2 = x[:, :, 0:32], x[:, :, 32:64]
            tt(t1[:, 0:nh, :], a2, rows_over(sn[:, t, :], nh), ALU.mult, after=[c, t_par])
            tt(t2[:, 0:nh, :], a1, rows_over(sn[:, t, :], nh), ALU.mult)
            tt(a1, a1, rows_over(cs[:, t, :], nh), ALU.mult)
            tt(a1, a1, t1[:, 0:nh, :], ALU.subtract)
            tt(a2, a2, rows_over(cs[:, t, :], nh), ALU.mult)
            return tt(a2, a2, t2[:, 0:nh, :], ALU.add)

        def turn_q(t, r, c):
            b, ps, bt = bank()
            for m in range(4):
                tk = turn(ps[:, m * P:(m + 1) * P], qn[r][:, m * P:(m + 1) * P], ident, after=[bt, c], count=m == 3)
            rd[r] = [tk]
            te = act(gq[:, :, t * P:(t + 1) * P], grid(ps, 4), ACT.Copy, scale=DH ** -0.5, after=[tk])
            free(b, te)

        def keep_gq(t, n0, n, ps, tok):
            r = t % 2
            a, c = head_rms(ps, 8, DH, qn[r], sq, ss, [tok, rd[r], g.last("dve")])
            x = grid(qn[r], 8)
            tt(x, x, rows_over(qg, 8), ALU.mult, after=[t_par])
            pending.append((t, r, rot(x, 8, t, c)))
            if len(pending) > 1:
                turn_q(*pending.pop(0))
            return a, c

        linear_tok(feat_tile, KT, "w_in_odd_2", 1536, 512, LAT, keep_gq, ready)
        while pending:
            turn_q(*pending.pop(0))
        rk = [[], []]

        def turn_k(t, r, c):
            b, ps, bt = bank()
            for m in range(2):
                tk = turn(ps[:, m * P:(m + 1) * P], kn[r][:, m * P:(m + 1) * P], ident, after=[bt, c], count=m == 1)
            rk[r] = [tk]
            te = copy(gk[:, :, t * P:(t + 1) * P], grid(ps[:, 0:256], 2), after=[tk], eng="act")
            free(b, te)

        def keep_gkv(t, n0, n, ps, tok):
            r = t % 2
            a2 = copy(gv[:, t, :], ps[:, 128:256], after=[tok], eng="act")
            a, c = head_rms(ps[:, 0:128], 2, DH, kt_, sq[:, 0:128], ss[:, 0:2], [tok, g.last("dve")])
            x = grid(kt_, 2)
            c = tt(x, x, rows_over(kg, 2), ALU.mult, after=[t_par])
            if t < NLAT:
                c = rot(x, 2, t, c)
            k4 = kn[r].rearrange("p (h c d) -> p h c d", h=2, c=2)
            copy(k4[:, :, 0, :], x, after=[rk[r]])
            c = copy(k4[:, :, 1, :], x)
            pending.append((t, r, c))
            if len(pending) > 1:
                turn_k(*pending.pop(0))
            return a, a2, c

        linear_tok(feat_tile, KT, "w_in_odd_2", 2048, 256, range(NTOK), keep_gkv, ready)
        while pending:
            turn_k(*pending.pop(0))
        t_in = [g.last("act"), g.last("dve"), g.last("pe"), t_sk]
        row_readers[0].append(t_sk)
        t_b0 = read_bias(0, t_in)
        units = []
        for t in LAT:
            for hh in range(8):
                rows = slice(64 * (hh % 2), 64 * (hh % 2) + 64)
                kv = hh // 4

                def done(ps, rinv, toks, t=t, hh=hh):
                    return ts(OD[t][:, hh // 2, 64 * (hh % 2):64 * (hh % 2) + 64], ps, rinv, None, ALU.mult, after=toks)

                q_ = gq[rows, hh // 2, t * P:(t + 1) * P]
                units.append(dict(nk=768, ready=t_in, bias=None, dv=64, done=done,
                                  scores=[(q_, gk[rows, kv, 0:512], 0, 512, True, True),
                                          (q_, gk[rows, kv, 512:768], 512, 256, True, True)],
                                  values=[gv[:, s, kv * 64:(kv + 1) * 64] for s in range(NTOK)]))
        attention(units, att)
        for grp in range(2):
            t_b = t_b0 if grp == 0 else read_bias(1, t_in)
            units = []
            for t in LAT:
                for h in range(4):
                    hh = grp * 4 + h
                    rows = slice(64 * (hh % 2), 64 * (hh % 2) + 64)

                    def bias(src, dst, tok, t=t, h=h):
                        a0 = h * 896 + (7 - 2 * t - 1) * 64
                        tt(dst[:, 0:512], src[:, 0:512], TB[:, a0:a0 + 512], ALU.add, after=[tok, g.last("act")])
                        return copy(dst[:, 512:768], src[:, 512:768], after=[tok], eng="dve")

                    def done(ps, rinv, toks, t=t, hh=hh):
                        return ts(ON[t][:, hh // 2, 64 * (hh % 2):64 * (hh % 2) + 64], ps, rinv, None, ALU.mult, after=toks)

                    q_ = naq[rows, hh // 2, t * P:(t + 1) * P]
                    units.append(dict(nk=768, ready=[t_in, t_b], bias=bias, dv=64, done=done,
                                      scores=[(q_, nak[rows, hh // 2, 0:512], 0, 512, True, True),
                                              (q_, nak[rows, hh // 2, 512:768], 512, 256, True, True)],
                                      values=[nav[:, s, hh * 64:(hh + 1) * 64] for s in range(NTOK)]))
            attention(units, att)
            t_in = [g.last("act"), g.last("dve"), g.last("pe")]
        return lambda t, k: (ON if k < 4 else OD)[t][:, k % 4, :]

    def mod_first(i):
        return modulation("w_mod", i, "b_mod", i * 24, cond1, 1, 3072)

    def mod_second(i):
        return modulation("w_mod_2", i, "b_mod_2", i * 48, cond2, 2, 6144)

    t_mod = mod_first(0)
    for i in range(4):
        if stop <= i:
            break
        ready = prenorm(LAT, 0, "norm_pre_g", i * KT, (0, 1), 1, t_mod)
        if i % 3 == 0:
            Y, gb = gla(i, i // 3, ready)
        elif i == 1:
            Y, gb = sgu(i, ready)
        else:
            Y, gb = fox(i, ready)
        t_mod = mod_first(i + 1) if i < 3 else mod_second(0)
        post(LAT, Y, [gb, gb])
    for i in range(2):
        if stop <= 4 + i:
            break
        both = list(range(NTOK)) if i == 0 else LAT
        if i == 0:
            ctx_in.append(g.dma("act", "ctx_in", HC, io["ctx_2"].rearrange("a (t p) d -> p (a t) d", p=P),
                                after=[g.last("dve"), g.last("pe")]))
        ready = prenorm(list(range(NTOK)), 0, "g_pre_mix_2", i * KT, (0, 1), 2, t_mod)
        if i == 0:
            O = even(ready)
            y = lambda t, k: O[:, t, k * P:(k + 1) * P]
        else:
            y = odd(ready)
        tf = to_feat(y, both, [g.last("act"), g.last("dve"), g.last("pe")])
        gb = [6144, 7168]
        done_all = [g.last("dve"), g.last("pe"), g.last("act")]
        for v in range(2 - i):
            post_begin(v, "g_post_mix_2", i * KT, 2, 2, gb[v], done_all)
        Yv = grid(ar(0, NTOK * D), NTOK)
        linear_tok(feat_tile, KT, "w_out_even_2" if i == 0 else "w_out_odd_2", 0, D, both, keep_y(Yv), [tf])
        post(both, Yv, gb)
        ready = prenorm(both, 0, "g_pre_ffn_2", i * KT, (3, 4), 2, [])
        Yf = ffn(both, ready)
        for v in range(2 - i):
            post_begin(v, "g_post_ffn_2", i * KT, 5, 2, gb[v], [g.last("dve"), g.last("pe")])
        if i == 0:
            t_mod = mod_second(1)
        post(both, Yf, gb)

    t_out = g.dma("sp", "x_out", out.rearrange("a (t p) d -> p (a t) d", p=P), X, after=[g.last("dve"), t_x])
    g.put("sp", lambda e: e.wait_ge(g.names["x_out"], 16), [], count=False)

    block = stack.enter_context(nc.Block())
    for name, deco in (("sp", block.sync), ("pe", block.tensor), ("act", block.scalar), ("dve", block.vector),
                       ("pool", block.gpsimd)):
        def run(eng, name=name):
            for f in g.queue[name]:
                f(eng)
        deco(run)


def weight_plan(io):
    plan = []

    def add(name, index, c0, cols, kt=KT, split=True, k0=0):
        for n0 in range(0, cols, NMAX):
            plan.append((name, index, k0, kt, c0 + n0, min(NMAX, cols - n0), split))

    add("w_mod", 0, 0, 3 * D, split=False)
    for i in range(4):
        if i % 3 == 0:
            j = i // 3
            add("gla_w_in", j, 3072, 16)
            add("gla_w_in", j, 0, 1024)
            add("gla_w_in", j, 1024, 2048)
            add("gla_w_out", j, 0, D)
        elif i == 1:
            for c0 in (D, 0, 2 * D):
                add("sgu_w_in", 0, c0, D)
            add("sgu_w_out", 0, 0, D)
        else:
            add("fox_w_in", 0, 4096, 16)
            add("fox_w_in", 0, 0, 3072)
            add("fox_w_in", 0, 3072, 1024)
            add("fox_w_out", 0, 0, D)
        if i < 3:
            add("w_mod", i + 1, 0, 3 * D, split=False)
    add("w_mod_2", 0, 0, 6 * D, split=False)
    for i in range(2):
        if i == 0:
            for c0, cols in ((2048, 32), (1536, 512), (2080, 416), (0, 1536)):
                add("w_in_even_2", 0, c0, cols)
            for grp in range(2):
                add("mla_w_q_up_2", 0, grp * 384, 384, kt=2, split=False)
                add("mla_w_kv_up_2", 0, grp * 512, 512, kt=1, split=False)
            add("w_out_even_2", 0, 0, D)
        else:
            for c0, cols in ((0, 512), (512, 512), (1024, 512), (1536, 512), (2048, 256)):
                add("w_in_odd_2", 0, c0, cols)
            add("w_out_odd_2", 0, 0, D)
        for f0 in range(0, DFF, NMAX):
            nf = min(NMAX, DFF - f0)
            add("w_ffn_gate_2", i, f0, nf)
            add("w_ffn_up_2", i, f0, nf)
            add("w_ffn_down_2", i, 0, D, kt=nf // P, k0=f0 // P)
        if i == 0:
            add("w_mod_2", 1, 0, 6 * D, split=False)
    return plan


def constants():
    i = np.arange(P)
    r, c = i[:, None], i[None, :]
    up = []
    for lv in range(LEVELS):
        s = 1 << lv
        up.append(((r // (2 * s) == c // (2 * s)) & ((r // s) % 2 == 0) & ((c // s) % 2 == 1)))
    mats = [r == c, r <= c, r >= c] + up + [m.T for m in up]
    fold = (i % 32)[:, None] == np.arange(2)[None, :]
    const = np.concatenate([m.astype(np.float32) for m in mats + [fold]], 1)
    reset = np.broadcast_to((np.arange(512) % P != 0).astype(np.float32), (P, 512))
    neg = np.where(c > r, np.float32(-1e30), np.float32(0))
    col, kc = (i % 64)[:, None], np.arange(64)[None, :]
    st = np.clip(col - 8, 0, 48)
    window = np.where((kc >= st) & (kc < st + 16), np.float32(0), np.float32(-1e30))

    def rope_tables(dim):
        t = np.arange(512)
        nf = dim // 4
        inv = (np.float32(10000.0) ** (-np.arange(nf, dtype=np.float32) / np.float32(nf))).astype(np.float32)
        ang = np.concatenate([(t // 64).astype(np.float32)[:, None] * inv, (t % 64).astype(np.float32)[:, None] * inv], 1)
        f = lambda a: np.ascontiguousarray(a.astype(np.float32).reshape(4, P, dim // 2).transpose(1, 0, 2))
        return f(np.cos(ang)), f(np.sin(ang))

    cm, sm = rope_tables(32)
    cg, sg = rope_tables(64)
    out = {"k_const": const, "k_reset": reset, "k_neg": neg, "k_window": window, "k_cos_mla": cm, "k_sin_mla": sm,
           "k_cos_gqa": cg, "k_sin_gqa": sg}
    return {k: np.ascontiguousarray(v, dtype=np.float32) for k, v in out.items()}


STOP = 99


def kernel(**inputs):
    import numpy as _np
    import concourse.bacc as _bacc
    from concourse import mybir as _mybir
    from concourse.bass_utils import run_bass_kernel_spmd as _run

    nc = _bacc.Bacc("TRN2", target_bir_lowering=False, num_devices=1)
    arrays, io = {}, {}
    for name, a in list(inputs.items()) + list(constants().items()):
        a = _np.ascontiguousarray(a)
        arrays[f"in_{name}"] = a
        io[name] = nc.dram_tensor(f"in_{name}", a.shape, _mybir.dt.from_np(a.dtype), kind="ExternalInput").ap()
    out = nc.dram_tensor("out_x", (1, 512, D), F32, kind="ExternalOutput").ap()
    build(nc, io, out, STOP)
    r = _run(nc, [arrays], core_ids=[0])
    return r.results[0]["out_x"]
```

```python
import numpy as np
import concourse.bass as bass
import concourse.mybir as mybir
from concourse.alu_op_type import AluOpType as ALU

F32 = mybir.dt.float32
F32R = mybir.dt.float32r
U32 = mybir.dt.uint32
ACT = mybir.ActivationFunctionType
AX = mybir.AxisListType

P = 128
D = 1024
KT = D // P
NLAT, NCTX = 4, 2
NTOK = NLAT + NCTX
NMAX = 512
EPS = 1e-6
LEVELS = 7
DFF = 2816
FT = DFF // P
LAT, CTX = list(range(NLAT)), list(range(NLAT, NTOK))

RING = 4
HALF = KT * NMAX // 2
SLOT = 2 * HALF
FEATS = KT * NTOK * P
ARENA = 13280


class Program:

    ENGINES = ("pe", "act", "dve", "pool", "sp")

    def __init__(self, nc, stack):
        self.nc = nc
        self.queue = {e: [] for e in self.ENGINES}
        self.sem = {e: stack.enter_context(nc.semaphore("done_" + e)) for e in self.ENGINES}
        self.count = {e: 0 for e in self.ENGINES}
        self.waited = {e: {} for e in self.ENGINES}
        self.stack = stack
        self.names = {}

    def last(self, engine):
        return (engine, self.count[engine])

    def put(self, engine, fn, after=(), count=True):
        need = {}
        todo = list(after)
        while todo:
            x = todo.pop()
            if x is None:
                continue
            if isinstance(x, list):
                todo.extend(x)
                continue
            if x[1] > 0:
                need[x[0]] = max(need.get(x[0], 0), x[1])
        seen = self.waited[engine]
        for name, value in need.items():
            if seen.get(name, 0) < value:
                seen[name] = value
                sem = self.sem[name] if name in self.sem else self.names[name]
                self.queue[engine].append(lambda e, s=sem, v=value: e.wait_ge(s, v))
        if count:
            self.count[engine] += 1
            self.queue[engine].append(lambda e, f=fn, s=self.sem[engine]: f(e).then_inc(s, 1))
            return (engine, self.count[engine])
        self.queue[engine].append(lambda e, f=fn: f(e))
        return None

    def dma(self, engine, stream, out, in_, after=()):
        if stream not in self.names:
            self.names[stream] = self.stack.enter_context(self.nc.semaphore(stream))
            self.count[stream] = 0
        self.put(engine, lambda e, s=self.names[stream]: e.dma_start(out, in_).then_inc(s, 16), after, count=False)
        self.count[stream] += 16
        return (stream, self.count[stream])

    def mm(self, out, lhsT, rhs, start=True, stop=True, after=(), count=False):
        return self.put("pe", lambda e: e.matmul(out, lhsT, rhs, start=start, stop=stop), after, count)

    def turn(self, out, in_, ident, after=(), count=False):
        return self.put("pe", lambda e: e.transpose(out, in_, ident), after, count)

    def act(self, out, in_, func, after=(), bias=0.0, scale=1.0, accum=None):
        kw = {} if accum is None else {"accum_out": accum}
        return self.put("act", lambda e: e.activation(out, in_, func, bias=bias, scale=scale, **kw),
                        [self.last("act"), list(after)])

    def tt(self, out, a, b, op, after=(), eng="dve"):
        return self.put(eng, lambda e: e.tensor_tensor(out, a, b, op), [self.last(eng), list(after)])

    def ts(self, out, a, s1, s2, op0, op1=None, after=(), eng="dve"):
        if op1 is None:
            return self.put(eng, lambda e: e.tensor_scalar(out, a, s1, None, op0), [self.last(eng), list(after)])
        return self.put(eng, lambda e: e.tensor_scalar(out, a, s1, s2, op0, op1), [self.last(eng), list(after)])

    def stt(self, out, a, s, b, op0, op1, after=()):
        return self.put("dve", lambda e: e.scalar_tensor_tensor(out, a, s, b, op0, op1),
                        [self.last("dve"), list(after)])

    def copy(self, out, a, after=(), eng="dve"):
        if eng == "act":
            return self.act(out, a, ACT.Copy, after)
        return self.put(eng, lambda e: e.tensor_copy(out, a), [self.last(eng), list(after)])

    def recip(self, out, a, after=()):
        return self.put("dve", lambda e: e.reciprocal(out, a), [self.last("dve"), list(after)])

    def reduce(self, out, a, op, after=(), negate=False):
        return self.put("dve", lambda e: e.tensor_reduce(out, a, AX.X, op, negate=negate),
                        [self.last("dve"), list(after)])

    def memset(self, out, value, after=(), eng="dve"):
        return self.put(eng, lambda e: e.memset(out, value), [self.last(eng), list(after)])


def grid(ap, a):
    return ap.rearrange("p (a b) -> p a b", a=a)


def over(ap, n):
    p, m = ap.shape
    return ap.unsqueeze(2).broadcast_to((p, m, n))


def rows_over(ap, n):
    p, m = ap.shape
    return ap.unsqueeze(1).broadcast_to((p, n, m))


def build(nc, io, out, stop=99):
    from contextlib import ExitStack
    stack = ExitStack()
    with stack:
        program(nc, stack, io, out, stop)


def program(nc, stack, io, out, stop):
    g = Program(nc, stack)
    mm, turn, act, tt, ts, stt, copy = g.mm, g.turn, g.act, g.tt, g.ts, g.stt, g.copy

    def sb(name, n):
        return stack.enter_context(nc.sbuf_tensor(name, [P, n], F32))

    def two_names(name, n):
        at = -(-nc.sbuf_base // 32) * 32
        plain = sb(name, n)
        assert nc.sbuf_base == at + 4 * n
        rounded = nc.alloc_sbuf_tensor_at(name + "_r", [P, n], F32R, offset=at)
        return plain, rounded

    X = grid(sb("x_lat", NLAT * D)[:, :], NLAT)
    HC_t = sb("x_ctx", NCTX * D)
    HC = grid(HC_t[:, :], NCTX)
    FEAT_t, FEAT_r = two_names("feat", 2 * FEATS)
    FH, FL = grid(FEAT_r[:, 0:FEATS], KT), grid(FEAT_r[:, FEATS:2 * FEATS], KT)
    WEI_t, WEI_r = two_names("weights", RING * SLOT)
    AR, AR_r = two_names("arena", ARENA)
    CONST = sb("const", 3 * P + LEVELS * P + (2 * (LEVELS - 1) + 1) * 64 + 2)
    PCOL = sb("param_cols", 3 * P + 96)
    MODC = sb("mod_cols", 96)
    SM_t = sb("small", 284)
    COND = sb("cond", 2 * KT * 32)
    ROW_t = sb("rows", 2 * NMAX)
    PS_t = stack.enter_context(nc.psum_tensor("psum", [P, 8 * NMAX], F32))
    row_readers = [[], []]
    n_rows = [0]

    ident, TRI_U, TRI_L = (CONST[:, i * P:(i + 1) * P] for i in range(3))
    LEVEL_U = [CONST[:, (3 + i) * P:(4 + i) * P] for i in range(LEVELS)]
    c0 = (3 + LEVELS) * P
    LEVEL_C = [[CONST[:, c0 + (d * (LEVELS - 1) + i) * 64:c0 + (d * (LEVELS - 1) + i + 1) * 64]
                for i in range(LEVELS - 1)] for d in range(2)]
    c0 += 2 * (LEVELS - 1) * 64
    IDENT_C = CONST[:, c0:c0 + 64]
    FOLD = CONST[:, c0 + 64:c0 + 66]

    def ar(off, n):
        assert off + n <= ARENA, (off, n)
        return AR[:, off:off + n]

    def resid(t):
        return X[:, t, :] if t < NLAT else HC[:, t - NLAT, :]

    free_banks = [(i, []) for i in range(8)]

    def bank():
        i, toks = free_banks.pop(0)
        return i, PS_t[:, i * NMAX:(i + 1) * NMAX], toks

    def free(i, *toks, n=1):
        for j in range(n):
            free_banks.append((i + j, list(toks)))

    flip = [0]

    def evac_engine():
        flip[0] ^= 1
        return "act" if flip[0] else "dve"

    plan = weight_plan(io)
    slot_readers = [[] for _ in range(RING)]
    taken = [0]
    next_slot = [0]
    ahead = []

    def start_chunk():
        name, index, k0, kt, n0, n, split = plan[len(started_chunks)]
        started_chunks.append(name)
        src = io[name][index] if index is not None else io[name]
        src = src[k0 * P:(k0 + kt) * P, n0:n0 + n].rearrange("(k p) n -> p k n", p=P)
        parts = []
        step = HALF // NMAX if split else kt
        for q0 in range(0, kt, step):
            q = min(step, kt - q0)
            s = next_slot[0] % RING
            next_slot[0] += 1
            size = q * n
            raw = WEI_t[:, s * SLOT:s * SLOT + size]
            tok = g.dma("sp", f"weights_{s}", raw.rearrange("p (k n) -> p k n", k=q), src[:, q0:q0 + q, :],
                        after=slot_readers[s])
            if not split:
                parts.append((s, q0, q, grid(raw, q), None, [tok]))
                continue
            hi = WEI_r[:, s * SLOT + HALF:s * SLOT + HALF + size]
            lo = WEI_r[:, s * SLOT:s * SLOT + size]
            th = act(hi, raw, ACT.Copy, after=[tok])
            tl = tt(lo, raw, hi.bitcast(F32), ALU.subtract, after=[th])
            parts.append((s, q0, q, grid(hi, q), grid(lo, q), [th, tl]))
        ahead.append(parts)

    started_chunks = []

    def take_weights(name, k0, kt, n0, n):
        assert plan[taken[0]][0] == name and plan[taken[0]][2:6] == (k0, kt, n0, n), (plan[taken[0]], name, k0, kt, n0, n)
        taken[0] += 1
        if not ahead:
            start_chunk()
        if len(started_chunks) < len(plan):
            start_chunk()
        parts = ahead.pop(0)
        where = {}
        for s, q0, q, hi, lo, toks in parts:
            for k in range(q):
                where[q0 + k] = (hi[:, k, :], lo[:, k, :] if lo is not None else None, toks)

        def release(tok):
            for p_ in parts:
                slot_readers[p_[0]] = [tok]

        return where, release

    def product(ps, terms, first, last, after=()):
        for i, ((lh, ll), (rh, rl), toks) in enumerate(terms):
            a, z = first and i == 0, last and i == len(terms) - 1
            wait = [toks, after if i == 0 else None]
            if ll is None:
                tok = mm(ps, lh, rh, a, z, after=wait, count=i == len(terms) - 1)
            else:
                mm(ps, lh, rh, a, False, after=wait)
                mm(ps, lh, rl, False, False)
                tok = mm(ps, ll, rh, False, z, count=i == len(terms) - 1)
        return tok

    def linear_tok(src, nk, name, c0, ncols, tiles, done, ready, k0=0):
        for n0 in range(0, ncols, NMAX):
            n = min(NMAX, ncols - n0)
            where, release = take_weights(name, k0, nk, c0 + n0, n)
            for t in tiles:
                b, ps, bt = bank()
                tok = product(ps[:, 0:n], [(src(k, t), where[k][0:2], where[k][2]) for k in range(nk)], True, True,
                              after=[ready, bt])
                free(b, *done(t, n0, n, ps[:, 0:n], tok))
            release(tok)

    def linear_feat(name, c0w, ncols, ranges, done, ready):
        for n0 in range(0, ncols, NMAX):
            n = min(NMAX, ncols - n0)
            where, release = take_weights(name, 0, KT, c0w + n0, n)
            for m0 in range(0, n, P):
                m = min(P, n - m0)
                for c0, c in ranges:
                    b, ps, bt = bank()
                    tok = product(ps[0:m, 0:c], [((where[k][0][:, m0:m0 + m], where[k][1][:, m0:m0 + m]),
                                                  feat_cols(k, c0, c), where[k][2]) for k in range(KT)], True, True,
                                  after=[ready, bt])
                    free(b, *done((n0 + m0) // P, c0, c, ps[0:m, 0:c], tok))
            release(tok)

    feat_tile = lambda k, t: (FH[:, k, t * P:(t + 1) * P], FL[:, k, t * P:(t + 1) * P])
    feat_cols = lambda k, c0, c: (FH[:, k, c0:c0 + c], FL[:, k, c0:c0 + c])

    def split_feat(evac, hi, lo, shape):
        i = n_rows[0] % 2
        n_rows[0] += 1
        n = shape[0] * shape[1]
        v = ROW_t[:, i * NMAX:i * NMAX + n]
        tv = evac(v, row_readers[i])
        v3 = grid(v, shape[0]) if shape[0] > 1 else v
        copy(hi, v3, after=[tv])
        tok = tt(lo, v3, hi.bitcast(F32), ALU.subtract)
        row_readers[i] = [tok]
        return tv, tok

    t_const = g.dma("sp", "const_in", CONST[:, :], io["k_const"][:, :])
    ctx_in = []

    col_of = {}
    prow = grid(ar(0, 4 * P), 4)

    def as_rows(ap, k):
        return ap.rearrange(k, b=P) if "b" in k else ap

    groups = [
        [("norm_pre_g", "l (a b) -> (l a) b", 32), ("norm_post_g", "l (a b) -> (l a) b", 32),
         ("g_pre_mix_2", "l (a b) -> (l a) b", 16), ("g_post_mix_2", "l (a b) -> (l a) b", 16),
         ("g_pre_ffn_2", "l (a b) -> (l a) b", 16), ("g_post_ffn_2", "l (a b) -> (l a) b", 16)],
        [("c", "l (a b) -> (l a) b", 8), ("c_2", "l (a b) -> (l a) b", 8), ("c_ctx_2", "(a b) -> a b", 8),
         ("gla_b_a", "l (a b) -> (l a) b", 8), ("gdn_conv_2", "l t (a b) -> (l t a) b", 60),
         ("mla_q_norm_2", "l (a b) -> (l a) b", 2), ("mla_kv_norm_2", "l (a b) -> (l a) b", 1),
         ("sgu_b_s", "l a b -> (l a) b", 4)],
        [("b_mod", "l (a b) -> (l a) b", 96)],
        [("b_mod_2", "l (a b) -> (l a) b", 96)],
    ]
    t_pc = []
    for q, group in sorted(enumerate(groups), key=lambda x: x[0] != 1):
        r = 0
        for name, how, n in group:
            t_row = g.dma("act", f"params_{q}", prow[r:r + n, q, :], as_rows(io[name], how))
            col_of[name] = (q, r)
            r += n
        b, ps, bt = bank()
        tok = turn(ps[:, 0:r], prow[0:r, q, :], ident[0:r, 0:r], after=[t_row, t_const, bt], count=True)
        t_pc.append(copy(PCOL[:, q * P:q * P + r], ps[:, 0:r], after=[tok]))
        free(b, t_pc[-1])

    def pcol(name, i, n=1):
        q, r = col_of[name]
        return PCOL[:, q * P + r + i:q * P + r + i + n]

    t_x = g.dma("act", "x_in", X, io["x"].rearrange("a (t p) d -> p (a t) d", p=P))
    small_used = [0]

    def small(n):
        a = small_used[0]
        small_used[0] += n
        assert small_used[0] <= 284, small_used
        return SM_t[:, a:a + n]

    eps_col = small(1)
    one_col = small(1)
    g.memset(eps_col, EPS)
    g.memset(one_col, 1.0)
    cond1, cond2 = (COND[:, i * 256:(i + 1) * 256].rearrange("p (k v) -> p k v", v=32) for i in range(2))
    tz = g.memset(COND[:, :], 0.0)
    act(cond1[:, :, 0], pcol("c", 0, 8), ACT.Silu, after=[t_pc, tz])
    act(cond2[:, :, 0], pcol("c_2", 0, 8), ACT.Silu)
    t_cond = act(cond2[:, :, 1], pcol("c_ctx_2", 0, 8), ACT.Silu)

    def modulation(name, index, bias_name, bias_at, cond, nv, ncols):
        toks = []
        mod_free = g.last("dve")
        for n0 in range(0, ncols, NMAX):
            where, release = take_weights(name, 0, KT, n0, NMAX)
            b, ps, bt = bank()
            for k in range(KT):
                j = k % 4
                tok = mm(ps[32 * j:32 * j + 32, :], cond[:, k, :], where[k][0], k < 4, k >= 4,
                         after=[where[k][2], bt, t_cond] if k == 0 else (), count=k == KT - 1)
            release(tok)
            i = n_rows[0] % 2
            n_rows[0] += 1
            row = ROW_t[:, i * NMAX:(i + 1) * NMAX]
            tr = copy(row, ps, after=[tok, row_readers[i]], eng="act")
            free(b, tr)
            b, ps, bt = bank()
            for m in range(4):
                tok = mm(ps[:, m * nv:(m + 1) * nv], row[:, m * P:(m + 1) * P], FOLD[:, 0:nv],
                         after=[tr, bt, t_const], count=m == 3)
            row_readers[i] = [tok]
            m0 = n0 // P
            tc = tt(MODC[:, m0 * nv:(m0 + 4) * nv].rearrange("p (m v) -> p m v", v=nv),
                    ps[:, 0:4 * nv].rearrange("p (m v) -> p m v", v=nv),
                    over(pcol(bias_name, bias_at + m0, 4), nv), ALU.add, after=[tok, mod_free])
            free(b, tc)
            toks = [tc]
        return toks

    def modc(part, v, nv):
        return MODC[:, 0:48 * nv].rearrange("p (m v) -> p m v", v=nv)[:, part * KT:(part + 1) * KT, v] if nv > 1 \
            else MODC[:, part * KT:(part + 1) * KT]

    SSQ = small(12)
    RSTD = small(12)
    PRE_A = small(16)
    PRE_B = small(16)
    GATE = small(16)
    junk_t = sb("junk", NMAX)

    def rstd_of(out, ss, n, after=()):
        a = act(out, ss, ACT.Sqrt, bias=eps_col[0:out.shape[0], :], scale=1.0 / n, after=after)
        return g.recip(out, out, after=[a])

    def prenorm(tiles, xn_off, g_name, g_at, parts, nv, ready):
        shift, scale = parts
        gcol = pcol(g_name, g_at, KT)
        for v, some in ((0, [t for t in tiles if t < NLAT]), (1, [t for t in tiles if t >= NLAT])):
            if some:
                stt(PRE_A[:, v * 8:v * 8 + 8], modc(scale, v, nv), 1.0, gcol, ALU.add, ALU.mult, after=ready)
                copy(PRE_B[:, v * 8:v * 8 + 8], modc(shift, v, nv))
        xn = grid(ar(xn_off, NTOK * D), NTOK)
        for t in tiles:
            tq = act(xn[:, t, :], resid(t), ACT.Square, accum=SSQ[:, t:t + 1], after=[g.last("dve"), t_x, ctx_in])
        t0, t1 = tiles[0], tiles[-1] + 1
        tr = rstd_of(RSTD[:, t0:t1], SSQ[:, t0:t1], D, after=[tq])
        txn = {}
        for t in tiles:
            if t % 2:
                txn[t] = act(xn[:, t, :], resid(t), ACT.Copy, scale=RSTD[:, t:t + 1], after=[tr])
            else:
                txn[t] = ts(xn[:, t, :], resid(t), RSTD[:, t:t + 1], None, ALU.mult, after=[tr])
        toks = []
        for v, some in ((0, [t for t in tiles if t < NLAT]), (1, [t for t in tiles if t >= NLAT])):
            for k in range(KT if some else 0):
                b, ps, bt = bank()
                for i, t in enumerate(some):
                    tok = turn(ps[:, i * P:(i + 1) * P], xn[:, t, k * P:(k + 1) * P], ident, after=[bt, txn[t]],
                               count=i == len(some) - 1)
                n = len(some) * P
                a, c = PRE_A[:, v * 8 + k:v * 8 + k + 1], PRE_B[:, v * 8 + k:v * 8 + k + 1]
                t0_ = some[0] * P

                def evac(dst, wait, ps=ps, n=n, a=a, c=c, tok=tok):
                    return act(dst, ps[:, 0:n], ACT.Identity, scale=a, bias=c, after=[tok, tr, wait])

                tv, te = split_feat(evac, FH[:, k, t0_:t0_ + n], FL[:, k, t0_:t0_ + n], (1, n))
                free(b, tv)
        return [g.last("act"), g.last("dve")]

    def post_begin(v, name, at, gate_part, nv, gb_off, after):
        gc = GATE[:, v * 8:v * 8 + 8]
        tg = tt(gc, modc(gate_part, v, nv), pcol(name, at, KT), ALU.mult, after=after)
        for h in range(2):
            b, ps, bt = bank()
            for k in range(4):
                tok = mm(ps[:, k * P:(k + 1) * P], gc[:, h * 4 + k:h * 4 + k + 1].broadcast_to((P, P)), ident,
                         after=[tg, bt], count=k == 3)
            te = copy(ar(gb_off + h * NMAX, NMAX), ps, after=[tok, after], eng="act")
            free(b, te)
        return te

    def keep_y(Y):
        def done(t, n0, n, ps, tok):
            h = n0 // NMAX
            c = copy(Y[:, t, n0:n0 + n], ps, after=[tok])
            act(junk_t[:, 0:n], Y[:, t, n0:n0 + n], ACT.Square, accum=SSQ[:, 2 * t + h:2 * t + h + 1], after=[c])
            return (c,)
        return done

    def post(tiles, Y, gb_offs):
        t0, t1 = tiles[0], tiles[-1] + 1
        pairs = SSQ[:, 2 * t0:2 * t1].rearrange("p (t h) -> p t h", h=2)
        a = tt(RSTD[:, t0:t1], pairs[:, :, 0], pairs[:, :, 1], ALU.add, after=[g.last("act")])
        rstd_of(RSTD[:, t0:t1], RSTD[:, t0:t1], D, after=[a])
        for t in tiles:
            gb = ar(gb_offs[0 if t < NLAT else 1], D)
            a = stt(Y[:, t, :], Y[:, t, :], RSTD[:, t:t + 1], gb, ALU.mult, ALU.mult, after=[g.last("act")])
            tok = tt(resid(t), resid(t), Y[:, t, :], ALU.add, after=[t_x, ctx_in])
        return tok

    def to_feat(y, tiles, after):
        toks = []
        for t in tiles:
            for h in range(2):
                b, ps, bt = bank()
                for k in range(4):
                    kk = h * 4 + k
                    tok = turn(ps[:, k * P:(k + 1) * P], y(t, kk), ident, after=[after, bt], count=k == 3)
                tv, te = split_feat(lambda dst, wait, ps=ps, tok=tok: copy(dst, ps, after=[tok, wait], eng="act"),
                                    FH[:, h * 4:h * 4 + 4, t * P:(t + 1) * P],
                                    FL[:, h * 4:h * 4 + 4, t * P:(t + 1) * P], (4, P))
                free(b, tv)
                toks.append(te)
        return toks

    def first_layer_end(i, y, name, Y, gb_off, tiles=LAT):
        tf = to_feat(y, tiles, [g.last("act"), g.last("dve")])
        tg = post_begin(0, "norm_post_g", i * KT, 2, 1, gb_off, [g.last("dve"), g.last("pe")])
        linear_tok(feat_tile, KT, name, 0, D, tiles, keep_y(Y), [tf])

    def head_rms(ps, nh, d, out, sq, ss, tok):
        a = act(sq, ps, ACT.Square, after=[tok])
        g.reduce(ss, grid(sq, nh), ALU.add, after=[a])
        r = rstd_of(ss, ss, d, after=[g.last("dve")])
        c = tt(grid(out, nh), grid(ps, nh), over(ss, d), ALU.mult, after=[r])
        return a, c

    def attention(units, bufs, out_t):
        PR, PTR, S = bufs[0:3], bufs[3:5], bufs[5:]
        s_readers, pr_written = [None, None], [None, None, None]
        NEGM, SUM = att_cols[:, 0:3], att_cols[:, 3:9]
        pr_readers, pt_readers = [[], [], []], [[], []]
        toks_of = dict(free_banks)
        assert len(toks_of) == 8 and len(units) % 2 == 0
        pair_free = [toks_of[2 * i] + toks_of[2 * i + 1] for i in range(3)]
        one_free = [toks_of[6], toks_of[7]]
        sum_readers, out_readers = [None] * 6, [None, None]
        state = {}

        def pair(i):
            return PS_t[:, 2 * i * NMAX:(2 * i + 2) * NMAX]

        def stage_scores(n):
            for j in range(len(units[n]["scores"])):
                for m in (n, n + 1):
                    u = units[m]
                    lt, rh, n0, w, st, sp_ = u["scores"][j]
                    state[m] = mm(pair(m % 2)[:, n0:n0 + w], lt, rh, st, sp_, after=[pair_free[m % 2], u["ready"]],
                                  count=j == len(u["scores"]) - 1)

        def stage_softmax(n):
            u, i, tok = units[n], n % 3, state[n]
            nk = u["nk"]
            src = pair(n % 2)[:, 0:nk]
            if u["bias"]:
                j = n % len(S)
                u["bias"](src, S[j][:, 0:nk], [tok, s_readers[j]])
                src = S[j][:, 0:nk]
            tm = g.reduce(NEGM[:, i:i + 1], src, ALU.max, negate=True, after=[tok, pr_written[i]])
            te = act(PR[i][:, 0:nk], src, ACT.Exp, bias=NEGM[:, i:i + 1], accum=SUM[:, n % 6:n % 6 + 1],
                     after=[tm, pr_readers[i], sum_readers[n % 6], tok])
            pair_free[n % 2] = [tm, te]
            pr_written[i] = te
            if u["bias"]:
                s_readers[j] = te
            state[n] = te

        def stage_turn(n):
            u, i = units[n], n % 3
            nk = u["nk"]
            ps = pair(2)
            for j in range(nk // P):
                tok = turn(ps[:, j * P:(j + 1) * P], PR[i][:, j * P:(j + 1) * P], ident,
                           after=[pair_free[2], state[n]], count=j == nk // P - 1)
            pr_readers[i] = [tok]
            te = copy(PTR[n % 2][:, 0:nk], ps[:, 0:nk], after=[tok, pt_readers[n % 2]],
                      eng="act" if u["bias"] or n % 2 else "dve")
            pair_free[2] = [te]
            tr = g.recip(SUM[:, n % 6:n % 6 + 1], SUM[:, n % 6:n % 6 + 1], after=[state[n]])
            state[n] = [te, tr]

        def stage_values(n):
            u, k = units[n], n // 2 % 2
            half = slice(64 * (n % 2), 64 * (n % 2) + 64)
            ps = PS_t[:, (6 + k) * NMAX:(7 + k) * NMAX]
            for j, v in enumerate(u["values"]):
                tok = mm(ps[half, 0:P], v, PTR[n % 2][:, j * P:(j + 1) * P], j == 0, j == len(u["values"]) - 1,
                         after=[one_free[k], state[n], u["ready"]], count=j == len(u["values"]) - 1)
            pt_readers[n % 2] = [tok]
            if n % 2:
                state[n] = [copy(out_t[k], ps[:, 0:P], after=[tok, out_readers[k]], eng="act"), state[n]]

        def stage_output(n):
            k = n // 2 % 2
            ps = PS_t[:, (6 + k) * NMAX + P:(6 + k) * NMAX + 2 * P]
            tok = turn(ps, out_t[k], ident, after=[state[n + 1]], count=True)
            out_readers[k] = [tok]
            for m in (n, n + 1):
                one_free[k] = [units[m]["done"](ps[:, 64 * (m % 2):64 * (m % 2) + 64], SUM[:, m % 6:m % 6 + 1],
                                                [tok, state[m]])]
                sum_readers[m % 6] = one_free[k]

        last = len(units)
        for n in range(0, last + 4, 2):
            if 2 <= n < last + 2:
                stage_turn(n - 2)
            if n < last:
                stage_scores(n)
            if 2 <= n < last + 2:
                stage_turn(n - 1)
            if n < last:
                stage_softmax(n)
                stage_softmax(n + 1)
            if n >= 4:
                stage_output(n - 4)
            if 2 <= n < last + 2:
                stage_values(n - 2)
                stage_values(n - 1)
        free_banks[:] = [(2 * i + j, list(pair_free[i])) for i in range(3) for j in range(2)] + \
            [(6 + i, list(one_free[i])) for i in range(2)]

    att_cols = small(9)

    def gla(i, j, ready):
        H, DK, DV = 4, 128, 256
        q, k = grid(ar(0, 2048), H), grid(ar(2048, 2048), H)
        v, z = grid(ar(4096, 4096), NLAT), grid(ar(8192, 4096), NLAT)
        b_ = HC_t[:, :]
        aT = ar(12288, 512)
        ff = lambda off, n: FEAT_t[:, off:off + n]
        AT, QK0, QK1, e_, qe = (ff(n * 2048, 2048) for n in range(5))
        S_ = grid(ff(10240, 1024), H)
        gh = ff(11264, 1024)
        reset = aT
        ss, last_decay = junk_t[:, 256:272], junk_t[:, 272:288]
        wa2 = ROW_t[:, 0:512]
        t_par = g.dma("pool", "layer_params", wa2[0:16, :], io["gla_w_a2"][j], after=ready)
        lat = [(0, NLAT * P)]

        def keep_a(m, c0, c, ps, tok):
            return (copy(aT[0:16, c0:c0 + c], ps, after=[tok]),)

        linear_feat("gla_w_in", 3072, 16, lat, keep_a, ready)
        t_aT = g.last("dve")

        for h in range(H):
            b, ps, bt = bank()
            tok = mm(ps, wa2[0:16, h * DK:(h + 1) * DK], aT[0:16, :], after=[bt, t_aT, t_par], count=True)
            xs = b_[:, h * 512:(h + 1) * 512]
            tx = ts(xs, ps, pcol("gla_b_a", j * 4 + h), None, ALU.add, after=[tok])
            free(b, tx)
        t_wa = [tok]

        def keep_qk(m, c0, c, ps, tok):
            if m < 4:
                return (act(q[:, m, c0:c0 + c], ps, ACT.Copy, scale=DK ** -0.5, after=[tok]),)
            return (copy(k[:, m - 4, c0:c0 + c], ps, after=[tok]),)

        linear_feat("gla_w_in", 0, 1024, lat, keep_qk, ready)
        t_qk = [g.last("act"), g.last("dve")]

        def keep_vz(t, n0, n, ps, tok):
            if n0 < 1024:
                return (copy(v[:, t, n0:n0 + n], ps, after=[tok], eng=evac_engine()),)
            return (act(z[:, t, n0 - 1024:n0 - 1024 + n], ps, ACT.Silu, after=[tok]),)

        linear_tok(feat_tile, KT, "gla_w_in", 1024, 2048, LAT, keep_vz, ready)
        t_in = [g.last("pe"), g.last("act"), g.last("dve")]
        g.dma("pool", "layer_params", gh, io["gla_g_head"][j].rearrange("h d -> (h d)").partition_broadcast(P),
              after=t_in)
        t_par = g.dma("pool", "layer_params", reset, io["k_reset"][:, :], after=t_in)
        act(e_, b_, ACT.Abs, after=t_in)
        act(e_, e_, ACT.Exp, scale=-1.0)
        tl = act(e_, e_, ACT.Ln, bias=one_col)
        stt(b_, b_, 0.0, e_, ALU.min, ALU.subtract, after=[tl])
        for h in range(H):
            xs = b_[:, h * 512:(h + 1) * 512]
            tb = g.put("dve", lambda e, xs=xs: e.tensor_tensor_scan(xs, reset, xs, 0.0, ALU.mult, ALU.add),
                       [g.last("dve"), t_par])
        act(qe, b_, ACT.Exp, scale=1.0 / 16, after=[tb])
        for t in LAT:
            tt(z[:, t, :], z[:, t, :], gh, ALU.mult, after=[t_par, t_in], eng="pool")

        qf, kf = ar(0, 2048), ar(2048, 2048)
        ATg = AT.rearrange("p (n j) -> p n j", j=P)
        g.memset(AT, 0.0, after=[t_in])
        readers = [[], []]
        for lv in range(-1, LEVELS):
            if lv < 0:
                lhs, rhs, tq, mask = kf, qf, t_qk, ident
            else:
                s = 1 << lv
                QK = (QK0, QK1)[lv % 2]
                e4, b4, q4, k4, o4 = (x.rearrange("p (n h s) -> p n h s", h=2, s=s) for x in (e_, b_, qf, kf, QK))
                mid = b4[:, :, 0, s - 1:s].broadcast_to((P, 2048 // (2 * s), s))
                tt(e4[:, :, 0, :], mid, b4[:, :, 0, :], ALU.subtract, after=[g.last("act"), t_in])
                td = tt(e4[:, :, 1, :], b4[:, :, 1, :], mid, ALU.subtract)
                te = act(e_, e_, ACT.Exp, scale=1.0 / 16, after=[td])
                tt(o4[:, :, 0, :], k4[:, :, 0, :], e4[:, :, 0, :], ALU.mult, after=[te, readers[lv % 2]])
                tq = tt(o4[:, :, 1, :], q4[:, :, 1, :], e4[:, :, 1, :], ALU.mult)
                lhs = rhs = QK
                mask = LEVEL_U[lv]
            for h in range(H):
                b, ps, bt = bank()
                for c in range(NLAT):
                    at = slice((h * NLAT + c) * P, (h * NLAT + c + 1) * P)
                    tok = mm(ps[:, c * P:(c + 1) * P], lhs[:, at], rhs[:, at], after=[bt, tq], count=c == NLAT - 1)
                tm = g.put("dve", lambda e, h=h, ps=ps, mask=mask: e.copy_predicated(
                    ATg[:, h * NLAT:(h + 1) * NLAT, :], rows_over(mask.bitcast(U32), NLAT), grid(ps, NLAT)),
                    [g.last("dve"), tok])
                free(b, tm)
            readers[lv % 2] = [tok]
        t_at = tm

        blast = b_.rearrange("p (n t) -> p n t", t=P)
        tt(e_.rearrange("p (n t) -> p n t", t=P), blast[:, :, P - 1:P].broadcast_to((P, 16, P)), blast, ALU.subtract,
           after=[g.last("act")])
        te = act(e_, e_, ACT.Exp, scale=1.0 / 16, after=[g.last("dve")])
        tk = tt(e_, e_, kf, ALU.mult, after=[te])
        tc = copy(last_decay, qe.rearrange("p (n t) -> p n t", t=P)[:, :, P - 1])
        tqe = tt(qe, qe, qf, ALU.mult)
        ktok = QK0
        for n in range(4):
            b, ps, bt = bank()
            for m in range(4):
                tok = turn(ps[:, m * P:(m + 1) * P], e_[:, (4 * n + m) * P:(4 * n + m + 1) * P], ident,
                           after=[bt, tk], count=m == 3)
            t_kt = copy(ktok[:, n * 512:(n + 1) * 512], ps, after=[tok, readers], eng="act")
            free(b, t_kt)

        t_S = None
        t_pool = g.last("pool")
        for c in range(NLAT):
            t_s2 = []
            for h in range(H):
                n = h * NLAT + c
                at = slice(n * P, (n + 1) * P)
                vh = v[:, c, h * DV:(h + 1) * DV]
                b, ps, bt = bank()
                if c:
                    mm(ps[:, 0:DV], qe[:, at], S_[:, h, :], True, False, after=[bt, t_S, tqe])
                tok = mm(ps[:, 0:DV], AT[:, at], vh, c == 0, True, after=[bt, t_at], count=True)
                a = act(junk_t[:, 0:DV], ps[:, 0:DV], ACT.Square, accum=ss[:, n:n + 1], after=[tok])
                r = rstd_of(ss[:, n:n + 1], ss[:, n:n + 1], DV, after=[a])
                zh = z[:, c, h * DV:(h + 1) * DV]
                o = stt(zh, ps[:, 0:DV], ss[:, n:n + 1], zh, ALU.mult, ALU.mult, after=[r, t_pool])
                free(b, o)
                if c < NLAT - 1:
                    b, ps, bt = bank()
                    tok = mm(ps[:, 0:DV], ktok[:, at], vh, after=[bt, t_kt], count=True)
                    if c == 0:
                        t_s2 = copy(S_[:, h, :], ps[:, 0:DV], after=[tok])
                    else:
                        t_s2 = stt(S_[:, h, :], S_[:, h, :], last_decay[:, n:n + 1], ps[:, 0:DV], ALU.mult, ALU.add,
                                   after=[tok])
                    free(b, t_s2)
            t_S = t_s2
        first_layer_end(i, lambda t, k: z[:, t, k * P:(k + 1) * P], "gla_w_out", v, 0)
        return v, 0

    def sgu(i, ready):
        u, v, z = (grid(ar(n * 4096, 4096), NLAT) for n in range(3))
        lng, lnb = HC_t[:, 0:1024], HC_t[:, 1024:2048]
        ws, wsT = grid(ROW_t[:, 0:512], 4), grid(ar(12288, 512), 4)
        st, mv = ar(12800, 12), ar(12812, 8)
        t_par = g.dma("pool", "layer_params", lng, io["sgu_ln_g"][0].partition_broadcast(P), after=ready)
        t_par = g.dma("pool", "layer_params", lnb, io["sgu_ln_b"][0].partition_broadcast(P), after=ready)
        t_par = g.dma("pool", "layer_params", ws, io["sgu_w_s"][0].rearrange("g t s -> t g s"), after=ready)
        b, ps, bt = bank()
        for n in range(4):
            tok = turn(ps[:, n * P:(n + 1) * P], ws[:, n, :], ident, after=[bt, t_par], count=n == 3)
        t_ws = tt(wsT, grid(ps, 4), rows_over(TRI_U, 4), ALU.mult, after=[tok])
        free(b, t_ws)

        def keep(t, n0, n, ps, tok):
            dst = (u, v, z)[n0 // D][:, t, n0 % D:n0 % D + n]
            return (act(dst, ps, ACT.Silu if n0 >= 2 * D else ACT.Gelu_apprx_tanh, after=[tok]),)

        linear_tok(feat_tile, KT, "sgu_w_in", D, D, LAT, lambda t, n0, n, ps, tok: keep(t, n0 + D, n, ps, tok), ready)
        tv = g.last("act")
        for t in LAT:
            for h in range(2):
                g.put("dve", lambda e, t=t, h=h: e.bn_stats(st[:, 6 * h:6 * h + 6], v[:, t, h * 512:(h + 1) * 512]),
                      [g.last("dve"), tv])
            g.put("dve", lambda e: e.bn_aggr(mv[:, 0:2], st[:, 0:12].rearrange("p (a b) -> p a b", a=2)),
                  [g.last("dve")])
            rstd_of(mv[:, 2:3], mv[:, 1:2], 1, after=[g.last("dve")])
            ts(v[:, t, :], v[:, t, :], mv[:, 0:1], mv[:, 2:3], ALU.subtract, ALU.mult)
            tt(v[:, t, :], v[:, t, :], lng, ALU.mult, after=[t_par])
            tln = tt(v[:, t, :], v[:, t, :], lnb, ALU.add)
        linear_tok(feat_tile, KT, "sgu_w_in", 0, D, LAT, keep, ready)
        linear_tok(feat_tile, KT, "sgu_w_in", 2 * D, D, LAT,
                   lambda t, n0, n, ps, tok: keep(t, n0 + 2 * D, n, ps, tok), ready)
        tz = g.last("act")
        for t in LAT:
            tuz = tt(z[:, t, :], z[:, t, :], u[:, t, :], ALU.mult, after=[tz], eng="pool")
            for h in range(2):
                b, ps, bt = bank()
                for n in range(2):
                    gr = 2 * h + n
                    tok = mm(ps[:, n * 256:(n + 1) * 256], wsT[:, gr, :], v[:, t, gr * 256:(gr + 1) * 256],
                             after=[bt, tln, t_ws], count=n == 1)
                for n in range(2):
                    gr = 2 * h + n
                    zz = z[:, t, gr * 256:(gr + 1) * 256]
                    o = stt(zz, ps[:, n * 256:(n + 1) * 256], pcol("sgu_b_s", gr), zz, ALU.add, ALU.mult,
                            after=[tok, tuz])
                free(b, o)
        first_layer_end(i, lambda t, k: z[:, t, k * P:(k + 1) * P], "sgu_w_out", v, 0)
        return v, 0

    def fox(i, ready):
        H, DH = 16, 64
        qT, kT = grid(ar(0, 4096), 8), grid(ar(4096, 4096), 8)
        v = grid(ar(8192, 4096), NLAT)
        O = [qT[:, :, t * P:(t + 1) * P] for t in LAT]
        F, negF = ROW_t[:, 0:512], ROW_t[:, 512:1024]
        neg, Ftok = ar(12288, 128), grid(ar(12416, 64), NLAT)
        ss = ar(12480, 8)
        gq, gk, bf, gqs = (ar(12488 + n, 1) for n in range(4))
        qn, sq = [HC_t[:, 0:512], HC_t[:, 512:1024]], HC_t[:, 1024:1536]
        zs = [HC_t[:, 0:512], HC_t[:, 512:1024]]
        att = [HC_t[:, n * 512:(n + 1) * 512] for n in range(4)] + [F, junk_t[:, :]]
        att_out = [ar(13024 + n * P, P) for n in range(2)]
        NHL, PICK = AR_r[:, 12496:13008], AR_r[:, 13008:13024]
        for n in range(2):
            g.dma("pool", "layer_params", gq[64 * n:64 * n + 64, :], io["fox_g_q"].rearrange("a d -> d a"), after=ready)
            g.dma("pool", "layer_params", gk[64 * n:64 * n + 64, :], io["fox_g_k"].rearrange("a d -> d a"), after=ready)
        g.dma("pool", "layer_params", bf[0:16, :], io["fox_b_f"].rearrange("a d -> d a"), after=ready)
        t_par = g.dma("pool", "layer_params", neg, io["k_neg"][:, :], after=ready)
        t_gq = ts(gqs, gq, DH ** -0.5, None, ALU.mult, after=[t_par])
        def keep_f(m, c0, c, ps, tok):
            return (ts(F[0:16, c0:c0 + c], ps, bf[0:16, :], None, ALU.add, after=[tok, t_par]),)

        linear_feat("fox_w_in", 4096, 16, [(0, 512)], keep_f, ready)
        F_, N_ = F[0:16, :], negF[0:16, :]
        act(N_, F_, ACT.Abs, after=[g.last("dve")])
        act(N_, N_, ACT.Exp, scale=-1.0)
        tl = act(N_, N_, ACT.Ln, bias=one_col[0:16, :])
        stt(F_, F_, 0.0, N_, ALU.min, ALU.subtract, after=[tl])
        g.memset(N_, 1.0)
        g.put("dve", lambda e: e.tensor_tensor_scan(F_, N_, F_, 0.0, ALU.mult, ALU.add), [g.last("dve")])
        tF = ts(N_, F_, -1.0, None, ALU.mult)
        g.memset(ar(12496, 512), 0.0, after=ready)
        copy(NHL, ar(12496, 512))
        for r0 in (0, 64):
            copy(NHL[r0:r0 + 16, :], N_)
            tt(NHL[r0 + 32:r0 + 48, :], N_, NHL[0:16, :].bitcast(F32), ALU.subtract)
            tt(PICK[r0:r0 + 64, :], ident[r0:r0 + 64, r0:r0 + 16], ident[r0:r0 + 64, r0 + 32:r0 + 48], ALU.add)
        b, ps, bt = bank()
        for t in LAT:
            tok = turn(ps[:, t * 16:(t + 1) * 16], F_[:, t * P:(t + 1) * P], ident[0:16, 0:16], after=[bt, tF],
                       count=t == NLAT - 1)
        tFt = copy(Ftok, ps[:, 0:64].rearrange("p (t h) -> p t h", h=16), after=[tok])
        free(b, tFt)
        rd = [[], []]
        cnt = [0]

        def keep(t, n0, n, ps, tok):
            if n0 >= 2048:
                return (copy(v[:, t, n0 - 2048:n0 - 2048 + n], ps, after=[tok], eng=evac_engine()),)
            r = cnt[0] % 2
            cnt[0] += 1
            a, c = head_rms(ps, 8, DH, qn[r], sq, ss, [tok, rd[r], g.last("dve")])
            pending.append((t, n0, r, c))
            if len(pending) > 1:
                turn_q(*pending.pop(0))
            return a, c

        pending = []

        def turn_q(t, n0, r, c):
            b, ps, bt = bank()
            for m in range(4):
                tk = turn(ps[:, m * P:(m + 1) * P], qn[r][:, m * P:(m + 1) * P], ident, after=[bt, c], count=m == 3)
            rd[r] = [tk]
            dst, gcol = (qT, gqs) if n0 < D else (kT, gk)
            p0 = (n0 % D) // P
            te = act(dst[:, p0:p0 + 4, t * P:(t + 1) * P], grid(ps, 4), ACT.Copy, scale=gcol, after=[tk, t_par, t_gq])
            free(b, te)

        linear_tok(feat_tile, KT, "fox_w_in", 0, 3072, LAT, keep, ready)
        while pending:
            turn_q(*pending.pop(0))
        t_in = [g.last("act"), g.last("dve"), g.last("pe")]
        units = []
        for t in LAT:
            for h in range(H):
                base, pr = 64 * (h % 2), h // 2
                nk = (t + 1) * P

                def bias(src, dst, tok, t=t, h=h, nk=nk):
                    if t:
                        ts(dst[:, 0:t * P], src[:, 0:t * P], Ftok[:, t, h:h + 1], None, ALU.add,
                           after=[tok])
                    return stt(dst[:, t * P:nk], src[:, t * P:nk], Ftok[:, t, h:h + 1], neg, ALU.add, ALU.add,
                               after=[tok, t_par])

                def done(ps, rinv, toks, t=t, h=h):
                    return ts(O[t][:, h // 2, 64 * (h % 2):64 * (h % 2) + 64], ps, rinv, None, ALU.mult, after=toks)

                units.append(dict(
                    nk=nk, ready=t_in, bias=bias, done=done,
                    scores=[(qT[base:base + 64, pr, t * P:(t + 1) * P], kT[base:base + 64, pr, 0:nk], 0, nk, True, False),
                            (PICK[base:base + 64, h:h + 1].broadcast_to((64, P)), NHL[base:base + 64, 0:nk], 0, nk, False, True)],
                    values=[v[:, s, h * DH:(h + 1) * DH] for s in range(t + 1)]))
        attention(units, att, att_out)
        z_readers = [[], []]
        t_att = [g.last("act"), g.last("dve"), g.last("pe")]

        def gate_o(t, n0, n, ps, tok):
            a = act(zs[t % 2], ps, ACT.Silu, after=[tok, z_readers[t % 2], t_att])
            o = O[t][:, n0 // P:n0 // P + 4, :]
            z_readers[t % 2] = [tt(o, o, grid(zs[t % 2], 4), ALU.mult, after=[a])]
            return (a,)

        linear_tok(feat_tile, KT, "fox_w_in", 3072, 1024, LAT, gate_o, ready)
        first_layer_end(i, lambda t, k: O[t][:, k, :], "fox_w_out", v, 4096)
        return v, 4096

    def ffn(tiles, ready):
        T = len(tiles) * P
        Y = grid(ar(0, NTOK * D), NTOK)
        h0 = NTOK * D
        G = grid(ar(h0, 4 * T), 4)
        HH = grid(AR_r[:, h0:h0 + 4 * T], 4)
        HL = grid(AR_r[:, h0 + 4 * T:h0 + 8 * T], 4)
        ranges = [(0, 512), (512, 256)] if T > 512 else [(0, 512)]

        def keep_gate(m, c0, c, ps, tok):
            return (act(G[:, m, c0:c0 + c], ps, ACT.Silu, after=[tok]),)

        def keep_hidden(m, c0, c, ps, tok):
            tv, te = split_feat(lambda dst, wait: tt(dst, G[:, m, c0:c0 + c], ps, ALU.mult,
                                                     after=[tok, wait, g.last("act")]),
                                HH[:, m, c0:c0 + c], HL[:, m, c0:c0 + c], (1, c))
            return (tv,)

        def add_y(t, n0, n, ps, tok):
            y = Y[:, t, n0:n0 + n]
            c = copy(y, ps, after=[tok]) if f0 == 0 else tt(y, y, ps, ALU.add, after=[tok])
            if f0 + NMAX >= DFF:
                h = n0 // NMAX
                act(junk_t[:, 0:n], y, ACT.Square, accum=SSQ[:, 2 * t + h:2 * t + h + 1], after=[c])
            return (c,)

        for f0 in range(0, DFF, NMAX):
            nf = min(NMAX, DFF - f0)
            linear_feat("w_ffn_gate_2", f0, nf, ranges, keep_gate, ready)
            linear_feat("w_ffn_up_2", f0, nf, ranges, keep_hidden, ready)
            linear_tok(lambda k, t: (HH[:, k, t * P:(t + 1) * P], HL[:, k, t * P:(t + 1) * P]), nf // P,
                       "w_ffn_down_2", 0, D, tiles, add_y, [g.last("dve")], k0=f0 // P)
        return Y

    def rope(x1, x2, o1, o2, cs, sn, t1, t2, after):
        nh, h = x1.shape[1], x1.shape[2]
        c, s = rows_over(cs, nh), rows_over(sn, nh)
        tt(t1, x2, s, ALU.mult, after=after)
        tt(t2, x1, s, ALU.mult)
        tt(o1, x1, c, ALU.mult)
        tt(o1, o1, t1, ALU.subtract)
        tt(o2, x2, c, ALU.mult)
        return tt(o2, o2, t2, ALU.add)

    def even(ready):
        QT, KTT = grid(ar(0, 3072), 4), grid(ar(3072, 3072), 4)
        vtok = grid(ar(6144, 3072), NTOK)
        c0_ = 9216
        PADW = 776
        raw = [ar(c0_ + n * PADW, PADW) for n in range(2)]
        acc, sqb = ar(c0_ + 2 * PADW, 768), ar(c0_ + 2 * PADW + 768, 768)
        onescol = ar(c0_ + 2 * PADW + 1536, P)
        g.memset(onescol, 0.0, after=ready)
        g.memset(onescol[0:64, 0:64], 1.0)
        t_ones = g.memset(onescol[64:128, 64:128], 1.0)
        t_rz = [g.memset(raw[n], 0.0) for n in range(2)]
        GA, BETA = grid(small(96), NTOK), grid(small(96), NTOK)
        dtb, nega = ar(c0_ + 3216, 16), ar(c0_ + 3232, 16)
        abt = grid(ar(c0_ + 3248, NTOK * 16), NTOK)
        g.dma("pool", "layer_params", dtb, io["gdn_dt_bias_2"][0].rearrange("a b -> (a b)").partition_broadcast(P),
              after=ready)
        t_par = g.dma("pool", "layer_params", nega, io["gdn_a_log_2"][0].rearrange("a b -> (a b)")
                      .partition_broadcast(P), after=ready)
        act(nega, nega, ACT.Exp, after=[t_par])
        gate_dram = nc.dram_tensor("gate_spill", [P, NTOK, 512], F32, kind="Internal")
        down_dram = nc.dram_tensor("down_spill", [P, NTOK, 416], F32, kind="Internal")
        gate_sb = [raw[0][:, 0:512], raw[1][:, 0:512]]

        def keep_ab(t, n0, n, ps, tok):
            a = tt(GA[:, t, :], ps[:, 0:16], dtb, ALU.add, after=[tok, t_par])
            c = act(BETA[:, t, :], ps[:, 16:32], ACT.Sigmoid, after=[tok, a])
            return a, c

        linear_tok(feat_tile, KT, "w_in_even_2", 2048, 32, range(NTOK), keep_ab, ready)
        act(abt, GA, ACT.Abs, after=[g.last("dve")])
        act(abt, abt, ACT.Exp, scale=-1.0)
        tl = act(abt, abt, ACT.Ln, bias=one_col)
        stt(GA, GA, 0.0, abt, ALU.max, ALU.add, after=[tl])
        stt(GA, GA, -1.0, rows_over(nega, NTOK), ALU.mult, ALU.mult)
        gate_readers = [[], []]

        def keep_gate(t, n0, n, ps, tok):
            a = act(gate_sb[t % 2], ps, ACT.Silu, after=[tok, gate_readers[t % 2], t_rz])
            gate_readers[t % 2] = [g.dma("act", f"gate_out_{t % 2}", gate_dram[:, t, :], gate_sb[t % 2], after=[a])]
            return (a,)

        def keep_down(t, n0, n, ps, tok):
            a = copy(gate_sb[t % 2][:, 0:416], ps, after=[tok, gate_readers[t % 2], t_rz], eng="act")
            gate_readers[t % 2] = [g.dma("act", f"gate_out_{t % 2}", down_dram[:, t, :], gate_sb[t % 2][:, 0:416],
                                         after=[a])]
            return (a,)

        linear_tok(feat_tile, KT, "w_in_even_2", 1536, 512, range(NTOK), keep_gate, ready)
        linear_tok(feat_tile, KT, "w_in_even_2", 2080, 416, range(NTOK), keep_down, ready)
        t_down_out = [list(x) for x in gate_readers]
        for n in range(2):
            g.memset(raw[n], 0.0, after=[gate_readers[n]])
        t_rz = g.last("dve")
        raw_readers = [[], []]
        spans = [(2, 0, 512), (518, 512, 256)]
        tail = []

        def conv_tail(m, ta):
            if m < 8:
                a = act(sqb, acc, ACT.Square, after=[ta, g.last("dve")])
                for c0, c in ((0, 512), (512, 256)):
                    b, ps, bt = bank()
                    tok = mm(ps[:, 0:c], onescol, sqb[:, c0:c0 + c], after=[bt, a, t_ones], count=True)
                    te = act(sqb[:, c0:c0 + c], ps[:, 0:c], ACT.Sqrt, bias=eps_col, after=[tok])
                    free(b, te)
                g.recip(sqb, sqb, after=[te])
                if m < 4:
                    return stt(QT[:, m, :], acc, 0.125, sqb, ALU.mult, ALU.mult)
                return tt(KTT[:, m - 4, :], acc, sqb, ALU.mult)
            return to_tokens(acc, ta, vtok, m - 8)

        def to_tokens(src, td, dst, m):
            for ts0, nt in ((0, 4), (4, 2)):
                b, ps, bt = bank()
                for t in range(nt):
                    tok = turn(ps[:, t * P:(t + 1) * P], src[:, (ts0 + t) * P:(ts0 + t + 1) * P], ident,
                               after=[bt, td], count=t == nt - 1)
                te = copy(dst[:, ts0:ts0 + nt, m * P:(m + 1) * P],
                          grid(ps[:, 0:nt * P], nt), after=[tok], eng="act")
                free(b, te)
            return te

        def keep_conv(m, c0, c, ps, tok):
            r = m % 2
            off = 2 if c0 == 0 else 518
            a = copy(raw[r][:, off:off + c], ps, after=[tok, raw_readers[r], t_rz], eng="act")
            if c0:
                for o, d0, n in spans:
                    for j in range(5):
                        src = raw[r][:, o - 2 + j:o - 2 + j + n]
                        wj = pcol("gdn_conv_2", j * 12 + m)
                        if j == 0:
                            ts(acc[:, d0:d0 + n], src, wj, None, ALU.mult, after=[a, g.last("pe"), g.last("act")])
                        else:
                            stt(acc[:, d0:d0 + n], src, wj, acc[:, d0:d0 + n], ALU.mult, ALU.add)
                raw_readers[r] = [g.last("dve")]
                ta = act(acc, acc, ACT.Silu, after=[g.last("dve")])
                conv_tail(m, ta)
            return (a,)

        linear_feat("w_in_even_2", 0, 1536, [(0, 512), (512, 256)], keep_conv, ready)
        t_conv = [g.last("act"), g.last("dve"), g.last("pe")]

        GC, EG, KD, BEG, GL = (grid(ar(c0_ + n * 96, 96), NTOK) for n in range(5))
        r0 = c0_ + 480
        ones = ROW_t[:, 0:P]
        u_, wT, kd, vb, kb = (ar(r0 + n * 512, 512) for n in (0, 1, 3, 4, 5))
        qd2 = [ar(r0 + 1024, 512), junk_t[:, :]]
        S2 = [ar(r0 + 3072 + n * 256, 256) for n in range(2)]
        Gh = small(4)
        ktok, OG = grid(FEAT_t[:, 6144:9216], NTOK), grid(FEAT_t[:, 9216:12288], NTOK)
        DIF, DD0, DD1, DU, XC2, VM = (FEAT_t[:, n * 1024:(n + 1) * 1024] for n in range(6))
        DD = [DD0, DD1]
        Cc = [DIF[:, 0:512], DIF[:, 512:1024]]
        XC, XTC, VC, MC = XC2[:, 0:512], XC2[:, 512:1024], VM[:, 0:512], VM[:, 512:1024]
        XT = ROW_t[:, :]
        h8 = lambda ap: ap.rearrange("p (h n) -> p h n", h=8)
        g.memset(ones, 1.0, after=t_conv)
        for m in range(4):
            to_tokens(KTT[:, m, :], t_conv, ktok, m)
        b, ps, bt = bank()
        for t in range(NTOK):
            for d in range(2):
                tok = mm(ps[:, t * 16 + d * 8:t * 16 + d * 8 + 8], (TRI_U, TRI_L)[d], GA[:, t, d * 8:d * 8 + 8],
                         after=[bt, t_conv])
        tok = mm(ps[:, 96:192], ones, GA.rearrange("p t d -> p (t d)"), after=[g.last("dve")], count=True)
        f = lambda x: x.rearrange("p t d -> p (t d)")
        copy(f(GC), ps[:, 0:96], after=[tok])
        a = tt(f(KD), ps[:, 96:192], f(GC), ALU.subtract)
        act(f(EG), f(GC), ACT.Exp, after=[a])
        act(f(KD), f(KD), ACT.Exp)
        te = act(f(GL), ps[:, 96:192], ACT.Exp)
        free(b, te, a)
        tb = tt(f(BEG), f(BETA), f(EG), ALU.mult, after=[te])
        started = [False, False]
        step_done = [None]
        c_read, m_read = [None], [None]
        order = [(d, t) for pair in zip([4, 5, 0, 1, 2, 3], [5, 4, 3, 2, 1, 0]) for d, t in enumerate(pair)]
        seen = set()
        lo_, hi_ = slice(0, 64), slice(64, 128)
        c8 = lambda ap: ap.rearrange("p (h n) -> p h n", h=8)

        def prepare(n):
            d, t = order[n]
            DDn, qdn = DD[n % 2], qd2[n % 2]
            tri = (TRI_U, TRI_L)[d]
            tile = slice(t * P, (t + 1) * P)
            for hb in range(2):
                b, ps, bt = bank()
                for h in range(4):
                    hh = hb * 4 + h
                    tok = mm(ps[:, h * P:(h + 1) * P],
                             GA[:, t, d * 8 + hh:d * 8 + hh + 1].broadcast_to((P, P)), tri,
                             after=[bt], count=h == 3)
                half = slice(hb * 512, (hb + 1) * 512)
                a = tt(grid(DIF[:, half], 4), grid(ps, 4), over(GC[:, t, d * 8 + hb * 4:d * 8 + hb * 4 + 4], P),
                       ALU.subtract, after=[tok, c_read])
                for par in range(2):
                    rows = slice(64 * par, 64 * par + 64)
                    src = grid(ps, 4)[rows, par::2, :]
                    c = act(grid(qdn, 4)[rows, hb * 2:hb * 2 + 2, :], src, ACT.Exp, after=[tok, a])
                free(b, a, c)
                yield
            ts(DDn, DIF, 0.0, None, ALU.min)
            a = ts(DU, DIF, 0.0, None, ALU.max, after=[m_read])
            yield
            act(DDn, DDn, ACT.Exp, after=[a])
            td = act(DU, DU, ACT.Exp, scale=-1.0)
            tt(grid(qdn, 4), grid(qdn, 4), QT[:, :, tile], ALU.mult, after=[c])
            yield
            for which in range(2):
                two = [bank(), bank()]
                toks = [None, None]
                for h in range(4):
                    for par, (b, ps, bt) in enumerate(two):
                        rows = slice(64 * par, 64 * par + 64)
                        kk = KTT[rows, h, tile]
                        toks[par] = mm(ps[:, h * P:(h + 1) * P], kk, (kk, QT[rows, h, tile])[which],
                                       after=[bt, t_conv], count=h == 3)
                for par, (b, ps, bt) in enumerate(two):
                    mine = lambda ap: h8(ap)[:, par::2, :]
                    if which == 0:
                        tt(mine(DU), mine(DU), grid(ps, 4), ALU.mult, after=[toks[1], td])
                        a = tt(mine(DU), mine(DU), over(BETA[:, t, d * 8 + par:d * 8 + 8:2], P), ALU.mult)
                    else:
                        tt(mine(DDn), mine(DDn), grid(ps, 4), ALU.mult, after=[toks[1], td])
                        a = tt(mine(DDn), mine(DDn), rows_over(tri, 4), ALU.mult)
                    free(b, a)
                    yield
                if which == 0:
                    copy(c8(MC)[lo_], h8(DU)[lo_, :, lo_], after=[a], eng="pool")
                    tM[0] = copy(c8(MC)[hi_], h8(DU)[hi_, :, hi_], eng="pool")
            yield

        def blocks(out, lhsT, rhs, heads, after):
            for h in heads:
                for rows in (lo_, hi_):
                    tok = mm(out[rows, (h - heads[0]) * 64:(h - heads[0] + 1) * 64], lhsT[rows, h, :],
                             rhs[rows] if len(rhs.shape) == 2 else rhs[rows, h, :],
                             after=after, count=h == heads[-1] and rows is hi_)
            return tok

        def solve(n):
            d, t = order[n]
            lv = LEVEL_C[d]
            stt(c8(Cc[0]), c8(MC), -1.0, rows_over(lv[0], 8), ALU.mult, ALU.mult, after=[tM[0]])
            tx = tt(c8(XC), c8(Cc[0]), rows_over(IDENT_C, 8), ALU.add)
            b, ps, bt = bank()
            tok = blocks(ps, c8(XC), IDENT_C, range(8), [bt, tx])
            tx = copy(XTC, ps, after=[tok])
            free(b, tx)
            txs = [tx, tx]
            readers = [[tx], [None]]
            for level in range(1, LEVELS - 1):
                C = Cc[level % 2]
                tc = tt(c8(C), c8(MC), rows_over(lv[level], 8), ALU.mult, after=[readers[level % 2], g.last("dve")]
                        if level == 1 else [readers[level % 2]], eng="pool")
                tv = []
                for hb in range(2):
                    b, ps, bt = bank()
                    tok = blocks(ps, c8(C), c8(XTC), range(4 * hb, 4 * hb + 4), [bt, tc, txs[hb]])
                    tv.append(copy(VC[:, hb * 256:(hb + 1) * 256], ps[:, 0:256], after=[tok], eng="act"))
                    free(b, tv[-1])
                readers[level % 2] = [tok]
                for hb in range(2):
                    zz = []
                    for l_, r_, dst in ((XC, VC, XTC), (VC, XC, XC)):
                        b, ps, bt = bank()
                        tok = blocks(ps, c8(l_), c8(r_), range(4 * hb, 4 * hb + 4), [bt, tv[hb]])
                        zz.append((b, ps, tok, dst))
                    half = slice(hb * 256, (hb + 1) * 256)
                    for b, ps, tok, dst in zz:
                        txs[hb] = tt(dst[:, half], dst[:, half], ps[:, 0:256], ALU.subtract, after=[tok])
                        free(b, txs[hb])
            c_read[0] = g.last("pe")
            near, far = (lo_, hi_) if d == 0 else (hi_, lo_)
            full = h8(XT)
            copy(full[lo_, :, lo_], c8(XTC)[lo_], after=[txs, step_done], eng="pool")
            copy(full[hi_, :, hi_], c8(XTC)[hi_], eng="pool")
            tf_ = g.memset(full[far, :, near], 0.0, eng="pool")
            b, ps, bt = bank()
            for h in range(8):
                tok = mm(ps[near, h * 64:(h + 1) * 64], h8(DU)[far, h, near], c8(XTC)[far, h, :],
                         after=[bt, txs], count=h == 7)
            m_read[0] = tok
            tv = copy(VC[near], ps[near, :], after=[tok], eng="act")
            free(b, tv)
            b, ps, bt = bank()
            for h in range(8):
                tok = mm(ps[near, h * 64:(h + 1) * 64], c8(XC)[near, h, :], c8(VC)[near, h, :], after=[bt, tv],
                         count=h == 7)
            tz_ = ts(full[near, :, far], c8(ps)[near], -1.0, None, ALU.mult, after=[tok, step_done])
            free(b, tz_)
            return [tz_, tf_]

        def step(n, solved):
            d, t = order[n]
            DDn, qdn = DD[n % 2], qd2[n % 2]
            gs = slice(d * 8, d * 8 + 8)
            v3, k3 = grid(vtok[:, t, :], 8), grid(ktok[:, t, :], 8)
            tt(grid(vb, 8), v3, over(BETA[:, t, gs], 64), ALU.mult, after=[step_done])
            tt(grid(kb, 8), k3, over(BEG[:, t, gs], 64), ALU.mult, after=[tb])
            tk = tt(grid(kd, 8), k3, over(KD[:, t, gs], 64), ALU.mult)
            b, ps, bt = bank()
            for h in range(8):
                at = slice(h * P, (h + 1) * P)
                tok = mm(ps[:, h * 64:(h + 1) * 64], XT[:, at], vb[:, h * 64:(h + 1) * 64], after=[bt, tk, solved],
                         count=h == 7)
            tu = copy(u_, ps, after=[tok, step_done], eng="act")
            free(b, tu)
            b, ps, bt = bank()
            for h in range(8):
                at = slice(h * P, (h + 1) * P)
                tok = mm(ps[64 * (h % 2):64 * (h % 2) + 64, (h // 2) * P:(h // 2 + 1) * P], kb[:, h * 64:(h + 1) * 64],
                         XT[:, at], after=[bt], count=h == 7)
            tw = copy(wT, ps, after=[tok], eng="act")
            free(b, tw)
            yield
            S = S2[d]
            rows = lambda h: slice(64 * (h % 2), 64 * (h % 2) + 64)
            tn = tu
            if started[d]:
                two = [bank(), bank()]
                for m in range(4):
                    for par, (b, ps, bt) in enumerate(two):
                        tok = mm(ps[:, m * 64:(m + 1) * 64], wT[rows(par), m * P:(m + 1) * P],
                                 S[rows(par), m * 64:(m + 1) * 64], after=[bt, tw], count=m == 3)
                for par, (b, ps, bt) in enumerate(two):
                    mine = grid(u_, 8)[:, par::2, :]
                    tn = tt(mine, mine, grid(ps[:, 0:256], 4), ALU.subtract, after=[tok, tu])
                    free(b, tn)
                yield
            for par in range(2):
                b, ps, bt = bank()
                for m in range(4):
                    h = 2 * m + par
                    if started[d]:
                        mm(ps[:, m * 64:(m + 1) * 64], qdn[rows(h), m * P:(m + 1) * P],
                           S[rows(h), m * 64:(m + 1) * 64], True, False, after=[bt, tn])
                    tok = mm(ps[:, m * 64:(m + 1) * 64], DDn[:, h * P:(h + 1) * P], u_[:, h * 64:(h + 1) * 64],
                             not started[d], True, after=[bt, tn, tk], count=m == 3)
                dst, src = grid(OG[:, t, :], 8)[:, par::2, :], grid(ps[:, 0:256], 4)
                if t in seen:
                    a = tt(dst, dst, src, ALU.add, after=[tok])
                else:
                    a = copy(dst, src, after=[tok])
                free(b, a)
                yield
            seen.add(t)
            b, ps, bt = bank()
            for h in range(8):
                tok = mm(ps[rows(h), (h // 2) * 64:(h // 2 + 1) * 64], kd[:, h * 64:(h + 1) * 64],
                         u_[:, h * 64:(h + 1) * 64], after=[bt, tn], count=h == 7)
            if started[d]:
                for par in range(2):
                    copy(Gh[64 * par:64 * par + 64, 0:4], GL[64 * par:64 * par + 64, t, d * 8 + par:d * 8 + 8:2])
                tt(grid(S, 4), grid(S, 4), over(Gh[:, 0:4], 64), ALU.mult, after=[tok])
                a = tt(S, S, ps[:, 0:256], ALU.add)
            else:
                a = copy(S, ps[:, 0:256], after=[tok])
            free(b, a)
            started[d] = True
            step_done[0] = [a, tok, tu, tw]

        def side_by_side(*runs):
            runs = list(runs)
            while runs:
                for x in list(runs):
                    if next(x, self_end) is self_end:
                        runs.remove(x)

        self_end = object()
        tM = [None]
        side_by_side(prepare(0))
        for n in range(len(order)):
            solved = solve(n)
            side_by_side(step(n, solved), *([prepare(n + 1)] if n + 1 < len(order) else []))
        step_done = [step_done[0], g.last("act"), g.last("dve")]
        O = grid(ar(0, NTOK * D), NTOK)
        GB = grid(ar(6144, 3072), NTOK)
        onb = ar(9216, 64)
        sq, ssg = ar(9280, 512), ar(9792, 8)
        down = grid(ar(9904, NTOK * 416), NTOK)
        t_dn = g.dma("pool", "down_in", down, down_dram[:, :, :], after=[step_done, t_down_out])
        g.dma("pool", "layer_params", onb, io["gdn_out_norm_2"][0].partition_broadcast(P), after=[step_done])
        t_par = g.dma("pool", "layer_params", GB, gate_dram[:, :, :], after=[step_done, t_down_out])
        for t in range(NTOK):
            o_ = O[:, t, 0:512]
            head_rms(OG[:, t, :], 8, 64, o_, sq, ssg, [g.last("dve"), step_done])
            tt(grid(o_, 8), grid(o_, 8), rows_over(onb, 8), ALU.mult, after=[t_par])
            tt(o_, o_, GB[:, t, :], ALU.mult)
        t_gdn = [g.last("act"), g.last("dve"), g.last("pe")]
        H, NOPE, ROPE, DQK = 8, 64, 32, 96
        o0 = NTOK * D
        qd, kvd = down[:, :, 0:256], down[:, :, 256:416]
        qnT, kvT = grid(ar(6144, 1536), 2), ar(7680, 768)
        cs, sn = grid(ar(8448, 64), NLAT), grid(ar(8512, 64), NLAT)
        ss = ar(8576, 16)
        t1, t2 = (ar(8592 + 64 * n, 64).rearrange("p (h d) -> p h d", d=16) for n in range(2))
        kpe = grid(ar(8720, NTOK * 32), NTOK)
        qk_tok = [ar(8912 + n * 384, 384) for n in range(2)]
        qT, kT = grid(FEAT_t[:, 0:3072], 4), grid(FEAT_t[:, 3072:6144], 4)
        vt = grid(FEAT_t[:, 6144:7680], NTOK)
        att = [FEAT_t[:, 7680 + n * 768:8448 + n * 768] for n in range(5)]
        att_out = [FEAT_t[:, 11520 + n * P:11520 + (n + 1) * P] for n in range(2)]
        g.dma("pool", "layer_params", cs, io["k_cos_mla"][:, :, :], after=t_gdn)
        t_par = g.dma("pool", "layer_params", sn, io["k_sin_mla"][:, :, :], after=t_gdn)
        for t in range(NTOK):
            act(junk_t[:, 0:256], qd[:, t, :], ACT.Square, accum=ss[:, t:t + 1], after=[t_gdn, t_dn])
            a = act(junk_t[:, 0:128], kvd[:, t, 0:128], ACT.Square, accum=ss[:, 8 + t:9 + t])
        rstd_of(ss[:, 0:6], ss[:, 0:6], 256, after=[a])
        r = rstd_of(ss[:, 8:14], ss[:, 8:14], 128)
        for t in range(NTOK):
            ts(qd[:, t, :], qd[:, t, :], ss[:, t:t + 1], None, ALU.mult, after=[r, t_dn])
            ts(kvd[:, t, 0:128], kvd[:, t, 0:128], ss[:, 8 + t:9 + t], None, ALU.mult)
            if t < NLAT:
                a1, a2 = kvd[:, t, 128:144].unsqueeze(1), kvd[:, t, 144:160].unsqueeze(1)
                tn = rope(a1, a2, kpe[:, t, 0:16].unsqueeze(1), kpe[:, t, 16:32].unsqueeze(1), cs[:, t, :],
                          sn[:, t, :], t1[:, 0:1, :], t2[:, 0:1, :], [t_par])
            else:
                tn = copy(kpe[:, t, :], kvd[:, t, 128:160])
            b, ps, bt = bank()
            turn(ps[:, 0:P], qd[:, t, 0:P], ident, after=[bt, tn])
            turn(ps[:, P:2 * P], qd[:, t, P:2 * P], ident)
            tok = turn(ps[:, 2 * P:3 * P], kvd[:, t, 0:P], ident, count=True)
            for m in range(2):
                act(qnT[:, m, t * P:(t + 1) * P], ps[:, m * P:(m + 1) * P], ACT.Copy, scale=pcol("mla_q_norm_2", m),
                    after=[tok])
            te = act(kvT[:, t * P:(t + 1) * P], ps[:, 2 * P:3 * P], ACT.Copy, scale=pcol("mla_kv_norm_2", 0))
            free(b, te)
        t_down = [te]
        for grp in range(2):
            rd = [[], []]

            def up_q(t, n0, n, ps, tok):
                r = t % 2
                qk = qk_tok[r].rearrange("p (h d) -> p h d", d=DQK)
                psv = ps.rearrange("p (h d) -> p h d", d=DQK)
                if t < NLAT:
                    a = act(qk, psv, ACT.Copy, scale=DQK ** -0.5, after=[tok, rd[r], g.last("dve")])
                    x1, x2 = qk[:, :, 64:80], qk[:, :, 80:96]
                    tt(t1, x2, rows_over(sn[:, t, :], 4), ALU.mult, after=[a, t_par])
                    tt(t2, x1, rows_over(sn[:, t, :], 4), ALU.mult)
                    tt(x1, x1, rows_over(cs[:, t, :], 4), ALU.mult)
                    tt(x1, x1, t1, ALU.subtract)
                    tt(x2, x2, rows_over(cs[:, t, :], 4), ALU.mult)
                    c = tt(x2, x2, t2, ALU.add)
                else:
                    a = c = act(qk, psv, ACT.Copy, scale=DQK ** -0.5, after=[tok, rd[r], g.last("dve")])
                b, p2, bt = bank()
                for h in range(4):
                    tk = turn(p2[0:DQK, h * P:(h + 1) * P], qk[:, h, :], ident, after=[bt, c], count=h == 3)
                rd[r] = [tk]
                te = copy(qT[0:DQK, :, t * P:(t + 1) * P], grid(p2[0:DQK, :], 4), after=[tk, g.last("pe")], eng="act")
                free(b, te)
                return (a,)

            def up_kv(t, n0, n, ps, tok):
                r = t % 2
                psv = ps.rearrange("p (h d) -> p h d", d=128)
                qk = qk_tok[r].rearrange("p (h d) -> p h d", d=DQK)
                a1 = copy(qk[:, :, 0:64], psv[:, :, 0:64], after=[tok, rd[r], g.last("act")])
                c = copy(qk[:, :, 64:96], rows_over(kpe[:, t, :], 4))
                a2 = copy(vt[:, t, :].rearrange("p (h d) -> p h d", d=64), psv[:, :, 64:128], after=[tok, a1], eng="act")
                b, p2, bt = bank()
                for h in range(4):
                    tk = turn(p2[0:DQK, h * P:(h + 1) * P], qk[:, h, :], ident, after=[bt, c], count=h == 3)
                rd[r] = [tk]
                te = copy(kT[0:DQK, :, t * P:(t + 1) * P], grid(p2[0:DQK, :], 4), after=[tk], eng="dve")
                free(b, te)
                return a1, a2

            src_q = lambda k, t: (qnT[:, k, t * P:(t + 1) * P], None)
            src_k = lambda k, t: (kvT[:, t * P:(t + 1) * P], None)
            prev = [t_down, t_gdn, g.last("pe"), g.last("act"), g.last("dve")]
            g.put("act", lambda e: e.activation(ss[:, 14:15], one_col, ACT.Copy), prev)
            g.put("dve", lambda e: e.tensor_copy(ss[:, 15:16], one_col), prev)
            linear_tok(src_q, 2, "mla_w_q_up_2", grp * 384, 384, range(NTOK), up_q, prev)
            rd = [list(rd[0]), list(rd[1])]
            linear_tok(src_k, 1, "mla_w_kv_up_2", grp * 512, 512, range(NTOK), up_kv, prev)
            t_up = [g.last("act"), g.last("dve"), g.last("pe")]
            units = []
            for t in range(NTOK):
                for h in range(4):
                    hh = grp * 4 + h

                    def done(ps, rinv, toks, t=t, hh=hh):
                        return ts(O[:, t, 512 + hh * 64:512 + hh * 64 + 64], ps, rinv, None, ALU.mult, after=toks)

                    q_ = qT[0:DQK, h, t * P:(t + 1) * P]
                    if t < NLAT:
                        sc = [(q_, kT[0:DQK, h, 0:512], 0, 512, True, True),
                              (q_, kT[0:DQK, h, 512:768], 512, 256, True, True)]
                        keys = range(NTOK)
                    else:
                        sc = [(q_, kT[0:DQK, h, 512:768], 0, 256, True, True)]
                        keys = CTX
                    units.append(dict(nk=len(keys) * P, ready=t_up, bias=None, done=done, scores=sc,
                                      values=[vt[:, s, h * 64:(h + 1) * 64] for s in keys]))
            attention(units, att, att_out)
        return O

    def odd(ready):
        DH = 64
        naq, nak = grid(ar(0, 2048), 4), grid(ar(2048, 3072), 4)
        nav = grid(ar(5120, 3072), NTOK)
        gq, gk = grid(ar(8192, 2048), 4), grid(ar(10240, 1536), 2)
        gv = grid(ar(11776, 768), NTOK)
        cs, sn = grid(ar(12544, 128), NLAT), grid(ar(12672, 128), NLAT)
        qg, kg, nam = (ar(12800 + 64 * n, 64) for n in range(3))
        kt_, ss = ar(12992, 128), ar(13120, 8)
        qn, sq = [HC_t[:, 0:512], HC_t[:, 512:1024]], HC_t[:, 1024:1536]
        kn = [HC_t[:, 1536:1792], HC_t[:, 1792:2048]]
        t1, t2 = (junk_t[:, n * 256:(n + 1) * 256].rearrange("p (h d) -> p h d", d=32) for n in range(2))
        att = [FEAT_t[:, n * 768:(n + 1) * 768] for n in range(7)]
        att_out = [FEAT_t[:, 8960 + n * P:8960 + (n + 1) * P] for n in range(2)]
        TB = FEAT_t[:, 5376:5376 + 3584]
        ON, OD = ([x[:, :, t * P:(t + 1) * P] for t in LAT] for x in (naq, gq))
        g.dma("pool", "layer_params", cs, io["k_cos_gqa"][:, :, :], after=ready)
        g.dma("pool", "layer_params", sn, io["k_sin_gqa"][:, :, :], after=ready)
        g.dma("pool", "layer_params", nam, io["k_window"][:, :], after=ready)
        g.dma("pool", "layer_params", qg, io["gqa_q_norm_2"][0].partition_broadcast(P), after=ready)
        t_par = g.dma("pool", "layer_params", kg, io["gqa_k_norm_2"][0].partition_broadcast(P), after=ready)
        W = 127
        rp = ROW_t[:, 0:W]
        tz = g.memset(rp[0:120, :], 0.0, after=ready)
        t_rp = g.dma("pool", "rpb_in", rp[0:120, 48:79], io["na_rpb_2"][0].rearrange("h r c -> (h r) c"), after=[tz])
        skew = nc.dram_tensor("rpb_rows", [8 * 15, 64, W], F32, kind="Internal")
        t_sk = g.dma("pool", "rpb_out", skew[:, :, :], rp[0:120, :].unsqueeze(1).broadcast_to((120, 64, W)),
                     after=[t_rp])

        def read_bias(grp, after):
            for par in range(2):
                for h in range(4):
                    src = bass.AP(tensor=skew.ap().tensor if hasattr(skew, "ap") else skew,
                                  offset=((grp * 4 + h) * 15 + 1 - par) * 64 * W + 63,
                                  ap=[[W - 1, 64], [64 * W, 14], [1, 64]])
                    dst = TB[64 * par:64 * par + 64, h * 896:(h + 1) * 896].rearrange("p (r c) -> p r c", r=14)
                    tok = g.dma("pool", "bias_in", dst, src, after=[t_sk, after])
            tv = TB.rearrange("p (n c) -> p n c", c=64)
            return tt(tv, tv, rows_over(nam, 56), ALU.add, after=[tok, t_par])

        def keep_feat(dst, scale):
            def done(m, c0, c, ps, tok):
                if scale != 1.0:
                    return (act(dst[:, m, c0:c0 + c], ps, ACT.Copy, scale=scale, after=[tok]),)
                return (copy(dst[:, m, c0:c0 + c], ps, after=[tok], eng=evac_engine()),)
            return done

        all_ = [(0, 512), (512, 256)]
        linear_feat("w_in_odd_2", 0, 512, [(0, 512)], keep_feat(naq, DH ** -0.5), ready)
        linear_feat("w_in_odd_2", 512, 512, all_, keep_feat(nak, 1.0), ready)
        linear_tok(feat_tile, KT, "w_in_odd_2", 1024, 512, range(NTOK),
                   lambda t, n0, n, ps, tok: (copy(nav[:, t, :], ps, after=[tok], eng=evac_engine()),), ready)
        rd = [[], []]
        pending = []

        def rot(x, nh, t, c):
            a1, a2 = x[:, :, 0:32], x[:, :, 32:64]
            tt(t1[:, 0:nh, :], a2, rows_over(sn[:, t, :], nh), ALU.mult, after=[c, t_par])
            tt(t2[:, 0:nh, :], a1, rows_over(sn[:, t, :], nh), ALU.mult)
            tt(a1, a1, rows_over(cs[:, t, :], nh), ALU.mult)
            tt(a1, a1, t1[:, 0:nh, :], ALU.subtract)
            tt(a2, a2, rows_over(cs[:, t, :], nh), ALU.mult)
            return tt(a2, a2, t2[:, 0:nh, :], ALU.add)

        def turn_q(t, r, c):
            b, ps, bt = bank()
            for m in range(4):
                tk = turn(ps[:, m * P:(m + 1) * P], qn[r][:, m * P:(m + 1) * P], ident, after=[bt, c], count=m == 3)
            rd[r] = [tk]
            te = act(gq[:, :, t * P:(t + 1) * P], grid(ps, 4), ACT.Copy, scale=DH ** -0.5, after=[tk])
            free(b, te)

        def keep_gq(t, n0, n, ps, tok):
            r = t % 2
            a, c = head_rms(ps, 8, DH, qn[r], sq, ss, [tok, rd[r], g.last("dve")])
            x = grid(qn[r], 8)
            tt(x, x, rows_over(qg, 8), ALU.mult, after=[t_par])
            pending.append((t, r, rot(x, 8, t, c)))
            if len(pending) > 1:
                turn_q(*pending.pop(0))
            return a, c

        linear_tok(feat_tile, KT, "w_in_odd_2", 1536, 512, LAT, keep_gq, ready)
        while pending:
            turn_q(*pending.pop(0))
        rk = [[], []]

        def turn_k(t, r, c):
            b, ps, bt = bank()
            for m in range(2):
                tk = turn(ps[:, m * P:(m + 1) * P], kn[r][:, m * P:(m + 1) * P], ident, after=[bt, c], count=m == 1)
            rk[r] = [tk]
            te = copy(gk[:, :, t * P:(t + 1) * P], grid(ps[:, 0:256], 2), after=[tk], eng="act")
            free(b, te)

        def keep_gkv(t, n0, n, ps, tok):
            r = t % 2
            a2 = copy(gv[:, t, :], ps[:, 128:256], after=[tok], eng="act")
            a, c = head_rms(ps[:, 0:128], 2, DH, kt_, sq[:, 0:128], ss[:, 0:2], [tok, g.last("dve")])
            x = grid(kt_, 2)
            c = tt(x, x, rows_over(kg, 2), ALU.mult, after=[t_par])
            if t < NLAT:
                c = rot(x, 2, t, c)
            k4 = kn[r].rearrange("p (h c d) -> p h c d", h=2, c=2)
            copy(k4[:, :, 0, :], x, after=[rk[r]])
            c = copy(k4[:, :, 1, :], x)
            pending.append((t, r, c))
            if len(pending) > 1:
                turn_k(*pending.pop(0))
            return a, a2, c

        linear_tok(feat_tile, KT, "w_in_odd_2", 2048, 256, range(NTOK), keep_gkv, ready)
        while pending:
            turn_k(*pending.pop(0))
        t_in = [g.last("act"), g.last("dve"), g.last("pe"), t_sk]
        row_readers[0].append(t_sk)
        t_b0 = read_bias(0, t_in)
        units = []
        for t in LAT:
            for hh in range(8):
                rows = slice(64 * (hh % 2), 64 * (hh % 2) + 64)
                kv = hh // 4

                def done(ps, rinv, toks, t=t, hh=hh):
                    return ts(OD[t][:, hh // 2, 64 * (hh % 2):64 * (hh % 2) + 64], ps, rinv, None, ALU.mult, after=toks)

                q_ = gq[rows, hh // 2, t * P:(t + 1) * P]
                units.append(dict(nk=768, ready=t_in, bias=None, done=done,
                                  scores=[(q_, gk[rows, kv, 0:512], 0, 512, True, True),
                                          (q_, gk[rows, kv, 512:768], 512, 256, True, True)],
                                  values=[gv[:, s, kv * 64:(kv + 1) * 64] for s in range(NTOK)]))
        attention(units, att, att_out)
        for grp in range(2):
            t_b = t_b0 if grp == 0 else read_bias(1, t_in)
            units = []
            for t in LAT:
                for h in range(4):
                    hh = grp * 4 + h
                    rows = slice(64 * (hh % 2), 64 * (hh % 2) + 64)

                    def bias(src, dst, tok, t=t, h=h):
                        a0 = h * 896 + (7 - 2 * t - 1) * 64
                        tt(dst[:, 0:512], src[:, 0:512], TB[:, a0:a0 + 512], ALU.add, after=[tok])
                        return copy(dst[:, 512:768], src[:, 512:768], after=[tok], eng="dve")

                    def done(ps, rinv, toks, t=t, hh=hh):
                        return ts(ON[t][:, hh // 2, 64 * (hh % 2):64 * (hh % 2) + 64], ps, rinv, None, ALU.mult, after=toks)

                    q_ = naq[rows, hh // 2, t * P:(t + 1) * P]
                    units.append(dict(nk=768, ready=[t_in, t_b], bias=bias, done=done,
                                      scores=[(q_, nak[rows, hh // 2, 0:512], 0, 512, True, True),
                                              (q_, nak[rows, hh // 2, 512:768], 512, 256, True, True)],
                                      values=[nav[:, s, hh * 64:(hh + 1) * 64] for s in range(NTOK)]))
            attention(units, att, att_out)
            t_in = [g.last("act"), g.last("dve"), g.last("pe")]
        return lambda t, k: (ON if k < 4 else OD)[t][:, k % 4, :]

    def mod_first(i):
        return modulation("w_mod", i, "b_mod", i * 24, cond1, 1, 3072)

    def mod_second(i):
        return modulation("w_mod_2", i, "b_mod_2", i * 48, cond2, 2, 6144)

    t_mod = mod_first(0)
    for i in range(4):
        if stop <= i:
            break
        ready = prenorm(LAT, 0, "norm_pre_g", i * KT, (0, 1), 1, t_mod)
        if i % 3 == 0:
            Y, gb = gla(i, i // 3, ready)
        elif i == 1:
            Y, gb = sgu(i, ready)
        else:
            Y, gb = fox(i, ready)
        post(LAT, Y, [gb, gb])
        t_mod = mod_first(i + 1) if i < 3 else mod_second(0)
    for i in range(2):
        if stop <= 4 + i:
            break
        both = list(range(NTOK)) if i == 0 else LAT
        if i == 0:
            ctx_in.append(g.dma("act", "ctx_in", HC, io["ctx_2"].rearrange("a (t p) d -> p (a t) d", p=P),
                                after=[g.last("dve"), g.last("pe")]))
        ready = prenorm(list(range(NTOK)), 0, "g_pre_mix_2", i * KT, (0, 1), 2, t_mod)
        if i == 0:
            O = even(ready)
            y = lambda t, k: O[:, t, k * P:(k + 1) * P]
        else:
            y = odd(ready)
        tf = to_feat(y, both, [g.last("act"), g.last("dve"), g.last("pe")])
        gb = [6144, 7168]
        done_all = [g.last("dve"), g.last("pe"), g.last("act")]
        for v in range(2 - i):
            post_begin(v, "g_post_mix_2", i * KT, 2, 2, gb[v], done_all)
        Yv = grid(ar(0, NTOK * D), NTOK)
        linear_tok(feat_tile, KT, "w_out_even_2" if i == 0 else "w_out_odd_2", 0, D, both, keep_y(Yv), [tf])
        post(both, Yv, gb)
        ready = prenorm(both, 0, "g_pre_ffn_2", i * KT, (3, 4), 2, [])
        Yf = ffn(both, ready)
        for v in range(2 - i):
            post_begin(v, "g_post_ffn_2", i * KT, 5, 2, gb[v], [g.last("dve"), g.last("pe")])
        post(both, Yf, gb)
        if i == 0:
            t_mod = mod_second(1)

    t_out = g.dma("sp", "x_out", out.rearrange("a (t p) d -> p (a t) d", p=P), X, after=[g.last("dve"), t_x])
    g.put("sp", lambda e: e.wait_ge(g.names["x_out"], 16), [], count=False)

    block = stack.enter_context(nc.Block())
    for name, deco in (("sp", block.sync), ("pe", block.tensor), ("act", block.scalar), ("dve", block.vector),
                       ("pool", block.gpsimd)):
        def run(eng, name=name):
            for f in g.queue[name]:
                f(eng)
        deco(run)


def weight_plan(io):
    plan = []

    def add(name, index, c0, cols, kt=KT, split=True, k0=0):
        for n0 in range(0, cols, NMAX):
            plan.append((name, index, k0, kt, c0 + n0, min(NMAX, cols - n0), split))

    add("w_mod", 0, 0, 3 * D, split=False)
    for i in range(4):
        if i % 3 == 0:
            j = i // 3
            add("gla_w_in", j, 3072, 16)
            add("gla_w_in", j, 0, 1024)
            add("gla_w_in", j, 1024, 2048)
            add("gla_w_out", j, 0, D)
        elif i == 1:
            for c0 in (D, 0, 2 * D):
                add("sgu_w_in", 0, c0, D)
            add("sgu_w_out", 0, 0, D)
        else:
            add("fox_w_in", 0, 4096, 16)
            add("fox_w_in", 0, 0, 3072)
            add("fox_w_in", 0, 3072, 1024)
            add("fox_w_out", 0, 0, D)
        if i < 3:
            add("w_mod", i + 1, 0, 3 * D, split=False)
    add("w_mod_2", 0, 0, 6 * D, split=False)
    for i in range(2):
        if i == 0:
            for c0, cols in ((2048, 32), (1536, 512), (2080, 416), (0, 1536)):
                add("w_in_even_2", 0, c0, cols)
            for grp in range(2):
                add("mla_w_q_up_2", 0, grp * 384, 384, kt=2, split=False)
                add("mla_w_kv_up_2", 0, grp * 512, 512, kt=1, split=False)
            add("w_out_even_2", 0, 0, D)
        else:
            for c0, cols in ((0, 512), (512, 512), (1024, 512), (1536, 512), (2048, 256)):
                add("w_in_odd_2", 0, c0, cols)
            add("w_out_odd_2", 0, 0, D)
        for f0 in range(0, DFF, NMAX):
            nf = min(NMAX, DFF - f0)
            add("w_ffn_gate_2", i, f0, nf)
            add("w_ffn_up_2", i, f0, nf)
            add("w_ffn_down_2", i, 0, D, kt=nf // P, k0=f0 // P)
        if i == 0:
            add("w_mod_2", 1, 0, 6 * D, split=False)
    return plan


def constants():
    i = np.arange(P)
    r, c = i[:, None], i[None, :]
    up = []
    for lv in range(LEVELS):
        s = 1 << lv
        up.append(((r // (2 * s) == c // (2 * s)) & ((r // s) % 2 == 0) & ((c // s) % 2 == 1)))
    small_up = [m[:64, :64] for m in up[:LEVELS - 1]]
    compact = [np.concatenate([m, m], 0) for m in [m.T for m in small_up] + small_up + [np.eye(64)]]
    mats = [r == c, r <= c, r >= c] + up + compact
    fold = (i % 32)[:, None] == np.arange(2)[None, :]
    const = np.concatenate([m.astype(np.float32) for m in mats + [fold]], 1)
    reset = np.broadcast_to((np.arange(512) % P != 0).astype(np.float32), (P, 512))
    neg = np.where(c > r, np.float32(-1e30), np.float32(0))
    col, kc = (i % 64)[:, None], np.arange(64)[None, :]
    st = np.clip(col - 8, 0, 48)
    window = np.where((kc >= st) & (kc < st + 16), np.float32(0), np.float32(-1e30))

    def rope_tables(dim):
        t = np.arange(512)
        nf = dim // 4
        inv = (np.float32(10000.0) ** (-np.arange(nf, dtype=np.float32) / np.float32(nf))).astype(np.float32)
        ang = np.concatenate([(t // 64).astype(np.float32)[:, None] * inv, (t % 64).astype(np.float32)[:, None] * inv], 1)
        f = lambda a: np.ascontiguousarray(a.astype(np.float32).reshape(4, P, dim // 2).transpose(1, 0, 2))
        return f(np.cos(ang)), f(np.sin(ang))

    cm, sm = rope_tables(32)
    cg, sg = rope_tables(64)
    out = {"k_const": const, "k_reset": reset, "k_neg": neg, "k_window": window, "k_cos_mla": cm, "k_sin_mla": sm,
           "k_cos_gqa": cg, "k_sin_gqa": sg}
    return {k: np.ascontiguousarray(v, dtype=np.float32) for k, v in out.items()}


STOP = 99


def kernel(**inputs):
    import numpy as _np
    import concourse.bacc as _bacc
    from concourse import mybir as _mybir
    from concourse.bass_utils import run_bass_kernel_spmd as _run

    nc = _bacc.Bacc("TRN2", target_bir_lowering=False, num_devices=1)
    arrays, io = {}, {}
    for name, a in list(inputs.items()) + list(constants().items()):
        a = _np.ascontiguousarray(a)
        arrays[f"in_{name}"] = a
        io[name] = nc.dram_tensor(f"in_{name}", a.shape, _mybir.dt.from_np(a.dtype), kind="ExternalInput").ap()
    out = nc.dram_tensor("out_x", (1, 512, D), F32, kind="ExternalOutput").ap()
    build(nc, io, out, STOP)
    r = _run(nc, [arrays], core_ids=[0])
    return r.results[0]["out_x"]
```
